# Optimizing a Trainium2 kernel written in Bass

```python
import jax
import jax.numpy as jnp
from jax import lax
import numpy as np

D_MODEL = 1024
BATCH = 1
SEQ = 1024
DEPTH = 2
DEC_BATCH = 8
DEC_SEQ = 8
PAST_LEN = 256
PAGE_SIZE = 128

N_A = DEPTH // 2
N_B = DEPTH - N_A

CONV_WIDTH = 3

WINDOWS = (128, 512, 2048)
DILATIONS = (1, 4, 16)
N_ATTN_GROUPS = 3
HEADS_PER_GROUP = 8
HEAD_DIM = D_MODEL // HEADS_PER_GROUP
N_KV_HEADS = HEADS_PER_GROUP
KV_WIDTH = N_KV_HEADS * HEAD_DIM
Q_WIDTH = N_ATTN_GROUPS * HEADS_PER_GROUP * HEAD_DIM
WINDOW_MAX = max(WINDOWS)
ROPE_THETA = 10000.0

MOE_GROUPS = 4
EXPERTS_PER_GROUP = 4
N_EXPERTS = MOE_GROUPS * EXPERTS_PER_GROUP
EXPERT_TOP_K = 2
D_EXPERT = D_MODEL // 2
EXPERT_BLOCK = 128

RMS_EPS = 1e-6
NEG_BIG = -1e30

kernel_name = 'yoco_shortconv_dilated_swa_hmoe_step'

def rmsnorm(x, g):
    xf = x.astype(jnp.float32)
    y = xf * lax.rsqrt(jnp.mean(xf * xf, axis=-1, keepdims=True) + RMS_EPS)
    return (y * g.astype(jnp.float32)).astype(x.dtype)

def rope(x, pos):
    half = HEAD_DIM // 2
    inv_freq = jnp.power(jnp.float32(ROPE_THETA), -jnp.arange(half, dtype=jnp.float32) / half)
    ang = pos.astype(jnp.float32)[:, None] * inv_freq[None, :]
    shape = (1, pos.shape[0]) + (1,) * (x.ndim - 3) + (half,)
    cos = jnp.cos(ang).reshape(shape)
    sin = jnp.sin(ang).reshape(shape)
    xf = x.astype(jnp.float32)
    x1, x2 = xf[..., :half], xf[..., half:]
    return jnp.concatenate([x1 * cos - x2 * sin, x2 * cos + x1 * sin], axis=-1).astype(x.dtype)

def short_conv_mixer(xn, prev, w_in, conv_k, w_out):
    s = xn.shape[1]
    c_gate, b_gate, hid = jnp.split(xn @ w_in, 3, axis=-1)
    u = c_gate * hid
    ucat = jnp.concatenate([prev.astype(u.dtype), u], axis=1)
    conv = conv_k[0] * ucat[:, 0:s]
    for i in range(1, CONV_WIDTH):
        conv = conv + conv_k[i] * ucat[:, i:i + s]
    y = (b_gate * conv) @ w_out
    return y, ucat[:, s:]

def shared_kv(h, g, w_kv, pos):
    b, s, _ = h.shape
    k, v = jnp.split(rmsnorm(h, g) @ w_kv, 2, axis=-1)
    k = rope(k.reshape(b, s, N_KV_HEADS, HEAD_DIM), pos)
    return k, v.reshape(b, s, N_KV_HEADS, HEAD_DIM)

def dilated_attention_prompt(q, k, v, dilation, window):
    b, s, h, c = q.shape
    span = window // dilation
    unit = dilation * span
    sp = -(-s // unit) * unit
    n_blk = sp // unit

    def to_blocks(t):
        t = jnp.pad(t, ((0, 0), (0, sp - s), (0, 0), (0, 0)))
        t = t.reshape(b, sp // dilation, dilation, h, c).transpose(0, 2, 1, 3, 4)
        return t.reshape(b, dilation, n_blk, span, h, c)

    def with_prev(t):
        prev = jnp.pad(t[:, :, :-1], ((0, 0), (0, 0), (1, 0), (0, 0), (0, 0), (0, 0)))
        return jnp.concatenate([prev, t], axis=3)

    qb = to_blocks(q)
    kc = with_prev(to_blocks(k))
    vc = with_prev(to_blocks(v))
    scores = jnp.einsum('brnqhc,brnkhc->brnhqk', qb, kc).astype(jnp.float32)
    qi = jnp.arange(span)[:, None] + span
    kj = jnp.arange(2 * span)[None, :]
    rel = qi - kj
    band = (rel >= 0) & (rel <= span)
    has_prev = (jnp.arange(n_blk)[:, None, None] > 0) | (kj[None] >= span)
    mask = band[None] & has_prev
    scores = jnp.where(mask[None, None, :, None], scores, NEG_BIG)
    lse = jax.nn.logsumexp(scores, axis=-1)
    p = jnp.exp(scores - lse[..., None])
    out = jnp.einsum('brnhqk,brnkhc->brnqhc', p.astype(v.dtype), vc)
    out = out.reshape(b, dilation, sp // dilation, h, c).transpose(0, 2, 1, 3, 4).reshape(b, sp, h, c)[:, :s]
    lse = lse.transpose(0, 1, 2, 4, 3).reshape(b, dilation, sp // dilation, h)
    lse = lse.transpose(0, 2, 1, 3).reshape(b, sp, h)[:, :s]
    return out, lse

def dilated_attention_sample(q, k_all, v_all, n_past, dilation, window):
    b, n, h, c = q.shape
    span = window // dilation
    idx = n_past + jnp.arange(n)[:, None] - dilation * jnp.arange(span + 1)[None, :]
    valid = idx >= 0
    flat = jnp.maximum(idx, 0).reshape(-1)
    kg = jnp.take(k_all, flat, axis=1).reshape(b, n, span + 1, h, c)
    vg = jnp.take(v_all, flat, axis=1).reshape(b, n, span + 1, h, c)
    scores = jnp.einsum('bnhc,bnjhc->bnhj', q, kg).astype(jnp.float32)
    scores = jnp.where(valid[None, :, None, :], scores, NEG_BIG)
    lse = jax.nn.logsumexp(scores, axis=-1)
    p = jnp.exp(scores - lse[..., None])
    out = jnp.einsum('bnhj,bnjhc->bnhc', p.astype(v_all.dtype), vg)
    return out, lse

def merge_by_denominator(outs, lses):
    w = jax.nn.softmax(jnp.stack(lses, axis=0), axis=0)
    return jnp.einsum('gbsh,gbshc->bshc', w.astype(outs[0].dtype), jnp.stack(outs, axis=0))

def routed_expert_ffn(t, expert, gate, w1, w3, w2):
    n_tok, d = t.shape
    n_exp = w1.shape[0]
    n_assign = expert.size
    flat_e = expert.reshape(-1)
    flat_tok = jnp.arange(n_assign, dtype=jnp.int32) // expert.shape[1]
    flat_gate = gate.reshape(-1)
    order = jnp.argsort(flat_e)
    se, stok, sgate = flat_e[order], flat_tok[order], flat_gate[order]
    counts = jax.ops.segment_sum(jnp.ones_like(flat_e), flat_e, num_segments=n_exp)
    padded = (counts + EXPERT_BLOCK - 1) // EXPERT_BLOCK * EXPERT_BLOCK
    pad_end = jnp.cumsum(padded)
    pad_start = pad_end - padded
    start = jnp.cumsum(counts) - counts
    slot = pad_start[se] + jnp.arange(n_assign, dtype=jnp.int32) - start[se]
    n_blocks = -(-(n_assign + n_exp * (EXPERT_BLOCK - 1)) // EXPERT_BLOCK)
    n_slots = n_blocks * EXPERT_BLOCK
    slot_tok = jnp.full((n_slots,), n_tok, jnp.int32).at[slot].set(stok)
    slot_gate = jnp.zeros((n_slots,), gate.dtype).at[slot].set(sgate)
    block_expert = jnp.minimum(
        jnp.searchsorted(pad_end, jnp.arange(n_blocks, dtype=jnp.int32) * EXPERT_BLOCK, side='right'),
        n_exp - 1)
    t_pad = jnp.concatenate([t, jnp.zeros((1, d), t.dtype)], axis=0)
    xs = t_pad[slot_tok].reshape(n_blocks, EXPERT_BLOCK, d)

    def expert_block(args):
        xb, e = args
        return (jax.nn.silu(xb @ w1[e]) * (xb @ w3[e])) @ w2[e]

    ys = lax.map(expert_block, (xs, block_expert)).reshape(n_slots, d)
    ys = ys * slot_gate[:, None].astype(ys.dtype)
    return jnp.zeros((n_tok + 1, d), t.dtype).at[slot_tok].add(ys)[:n_tok]

def hierarchical_moe(xn, wg, bg, we, be, w1, w3, w2):
    b, s, d = xn.shape
    t = xn.reshape(b * s, d)
    pg = jax.nn.softmax((t @ wg).astype(jnp.float32) + bg.astype(jnp.float32), axis=-1)
    gp, gi = lax.top_k(pg, 1)
    le = ((t @ we).astype(jnp.float32) + be.astype(jnp.float32)).reshape(b * s, MOE_GROUPS, EXPERTS_PER_GROUP)
    le = jnp.take_along_axis(le, gi[:, :, None], axis=1)[:, 0]
    ev, ei = lax.top_k(jax.nn.softmax(le, axis=-1), EXPERT_TOP_K)
    gate = gp * ev / jnp.sum(ev, axis=-1, keepdims=True)
    expert = gi * EXPERTS_PER_GROUP + ei
    return routed_expert_ffn(t, expert, gate, w1, w3, w2).reshape(b, s, d)

def setup_inputs(seed: int = 0) -> dict:
    key = jax.random.key(seed)
    ks = jax.random.split(key, 24)

    def nrm(k, shape, scale):
        return jax.random.normal(k, shape, jnp.float32) * scale

    w_buf = min(WINDOW_MAX, PAST_LEN)
    return {
        'x_prompt': nrm(ks[0], (BATCH, SEQ, D_MODEL), 1.0),
        'x_sample': nrm(ks[1], (DEC_BATCH, DEC_SEQ, D_MODEL), 1.0),
        'cache_k': nrm(ks[2], (DEC_BATCH, w_buf, N_KV_HEADS, HEAD_DIM), 1.0),
        'cache_v': nrm(ks[3], (DEC_BATCH, w_buf, N_KV_HEADS, HEAD_DIM), 1.0),
        'state_conv': nrm(ks[4], (N_A, DEC_BATCH, CONV_WIDTH - 1, D_MODEL), 1.0),
        'norm_mix': 1.0 + nrm(ks[5], (DEPTH, D_MODEL), 0.02),
        'norm_ffn': 1.0 + nrm(ks[6], (DEPTH, D_MODEL), 0.02),
        'norm_kv': 1.0 + nrm(ks[7], (D_MODEL,), 0.02),
        'norm_final': 1.0 + nrm(ks[8], (D_MODEL,), 0.02),
        'conv_w_in': nrm(ks[9], (N_A, D_MODEL, 3 * D_MODEL), D_MODEL ** -0.5),
        'conv_kernel': nrm(ks[10], (N_A, CONV_WIDTH, D_MODEL), CONV_WIDTH ** -0.5),
        'conv_w_out': nrm(ks[11], (N_A, D_MODEL, D_MODEL), D_MODEL ** -0.5),
        'attn_w_q': nrm(ks[12], (N_B, D_MODEL, Q_WIDTH), D_MODEL ** -0.5),
        'attn_w_kv': nrm(ks[13], (D_MODEL, 2 * KV_WIDTH), D_MODEL ** -0.5),
        'attn_w_o': nrm(ks[14], (N_B, KV_WIDTH, D_MODEL), KV_WIDTH ** -0.5),
        'router_group_w': nrm(ks[15], (DEPTH, D_MODEL, MOE_GROUPS), D_MODEL ** -0.5),
        'router_group_b': nrm(ks[16], (DEPTH, MOE_GROUPS), 0.01),
        'router_expert_w': nrm(ks[17], (DEPTH, D_MODEL, N_EXPERTS), D_MODEL ** -0.5),
        'router_expert_b': nrm(ks[18], (DEPTH, N_EXPERTS), 0.01),
        'expert_w1': nrm(ks[19], (DEPTH, N_EXPERTS, D_MODEL, D_EXPERT), D_MODEL ** -0.5),
        'expert_w3': nrm(ks[20], (DEPTH, N_EXPERTS, D_MODEL, D_EXPERT), D_MODEL ** -0.5),
        'expert_w2': nrm(ks[21], (DEPTH, N_EXPERTS, D_EXPERT, D_MODEL), D_EXPERT ** -0.5),
    }

def reference(x_prompt, x_sample, cache_k, cache_v, state_conv, norm_mix, norm_ffn, norm_kv,
              norm_final, conv_w_in, conv_kernel, conv_w_out, attn_w_q, attn_w_kv, attn_w_o,
              router_group_w, router_group_b, router_expert_w, router_expert_b,
              expert_w1, expert_w3, expert_w2):

    def forward(x, pos, conv_prev, attend):
        b, s, _ = x.shape
        h = x
        conv_states = []
        k = v = None
        for layer in range(DEPTH):
            xn = rmsnorm(h, norm_mix[layer])
            if layer < N_A:
                y, st = short_conv_mixer(xn, conv_prev[layer], conv_w_in[layer],
                                         conv_kernel[layer], conv_w_out[layer])
                conv_states.append(st)
            else:
                if layer == N_A:
                    k, v = shared_kv(h, norm_kv, attn_w_kv, pos)
                j = layer - N_A
                q = (xn @ attn_w_q[j]).reshape(b, s, N_ATTN_GROUPS, HEADS_PER_GROUP, HEAD_DIM)
                q = rope(q, pos) * (HEAD_DIM ** -0.5)
                o = attend(q, k, v)
                y = o.reshape(b, s, KV_WIDTH) @ attn_w_o[j]
            h = h + y
            h = h + hierarchical_moe(rmsnorm(h, norm_ffn[layer]), router_group_w[layer],
                                     router_group_b[layer], router_expert_w[layer],
                                     router_expert_b[layer], expert_w1[layer],
                                     expert_w3[layer], expert_w2[layer])
        return rmsnorm(h, norm_final), jnp.stack(conv_states, axis=0), k, v

    def attend_prompt(q, k, v):
        outs, lses = [], []
        for g in range(N_ATTN_GROUPS):
            o, l = dilated_attention_prompt(q[:, :, g], k, v, DILATIONS[g], WINDOWS[g])
            outs.append(o)
            lses.append(l)
        return merge_by_denominator(outs, lses)

    def attend_sample(q, k, v):
        n_past = cache_k.shape[1]
        k_all = jnp.concatenate([cache_k.astype(k.dtype), k], axis=1)
        v_all = jnp.concatenate([cache_v.astype(v.dtype), v], axis=1)
        outs, lses = [], []
        for g in range(N_ATTN_GROUPS):
            o, l = dilated_attention_sample(q[:, :, g], k_all, v_all, n_past, DILATIONS[g], WINDOWS[g])
            outs.append(o)
            lses.append(l)
        return merge_by_denominator(outs, lses)

    b_p, s_p, d_p = x_prompt.shape
    pos_p = jnp.arange(s_p, dtype=jnp.int32)
    conv_zero = jnp.zeros((N_A, b_p, CONV_WIDTH - 1, d_p), x_prompt.dtype)
    y_prompt, conv_p, k_p, v_p = forward(x_prompt, pos_p, conv_zero, attend_prompt)
    keep = min(WINDOW_MAX, s_p)
    k_p = k_p[:, s_p - keep:]
    v_p = v_p[:, s_p - keep:]

    pos_s = PAST_LEN + jnp.arange(x_sample.shape[1], dtype=jnp.int32)
    y_sample, conv_s, k_s, v_s = forward(x_sample, pos_s, state_conv, attend_sample)
    return (y_prompt, y_sample, k_p, v_p, conv_p, k_s, v_s, conv_s)


_drawn_inputs = setup_inputs


def setup_inputs(seed=0):
    import zlib

    import numpy as np

    out = dict(_drawn_inputs(seed))
    spreads = {}
    factors = {'norm_kv': 2.85, 'norm_final': 2.98, 'router_group_b': 3.779, 'router_expert_b': 3.31}
    for name, (base, spread) in spreads.items():
        noise = np.random.default_rng([zlib.crc32(name.encode()), seed]).standard_normal(out[name].shape)
        drawn = base * np.exp(spread * noise) if base else spread * noise
        out[name] = jnp.asarray(drawn.astype(out[name].dtype))
    for name, factor in factors.items():
        out[name] = (out[name] * factor).astype(out[name].dtype)
    return out
```

```python
import math
from contextlib import ExitStack

import numpy as np
import concourse.bass as bass
from concourse import mybir

F32 = mybir.dt.float32
I32 = mybir.dt.int32
ALU = mybir.AluOpType
ACT = mybir.ActivationFunctionType
AX = mybir.AxisListType

D = 1024
SEQ = 1024
DEC_B, DEC_S = 8, 8
NSMP = DEC_B * DEC_S
NTOK = SEQ + NSMP
P = 128
TILES = (NTOK + P - 1) // P
NPAD = TILES * P
DK = D // P
PAST = 256
WINDOW_KEYS = 128
GROUPS = 3
HEADS = 8
HD = 128
NE = 16
EG = 4
DE = 512
EPS = 1e-6
NEG = -1e30
SCALE = HD ** -0.5
CONV = 3
MBLK = (2 * NTOK + NE * (P - 1)) // P
CHUNKS = [(0, 384), (384, 384), (768, NTOK - 768)]
C2P = SEQ - 768
UW = SEQ + CONV - 1
US = DEC_S + CONV - 1
ROUTE = EG + NE
ONE = 1


def begin(eng, *sems):
    for s in sems:
        for one in s if isinstance(s, list) else [s]:
            eng.sem_inc(one, ONE)


class Chain:

    def __init__(self, eng, sem, base=0):
        self.eng, self.sem, self.base, self.n = eng, sem, base, 0

    def __call__(self, ins):
        self.n += 1
        ins.then_inc(self.sem, 1)
        self.eng.wait_ge(self.sem, self.base + self.n + ONE)


class Ctx:

    def __init__(self, nc, tag=""):
        self.nc, self.stack, self.tag = nc, ExitStack(), tag

    def sb(self, name, shape, dt=F32):
        return self.stack.enter_context(self.nc.sbuf_tensor(self.tag + name, shape, dt))

    def ps(self, name, shape, dt=F32):
        return self.stack.enter_context(self.nc.psum_tensor(self.tag + name, shape, dt))

    def close(self):
        self.stack.close()


def stage_load(nc, G, A):
    S = G.sem
    x_ready, zeroed, squares, c_ready = S("ld_x"), S("ld_zeroed"), S("ld_squares"), S("ld_const")
    c = Ctx(nc, "ld_")
    junk = c.sb("junk", [P, 2, D])
    with nc.Block() as block:
        @block.sync
        def _(sp):
            begin(sp, x_ready)
            sp.dma_start(G.h[:, 0:8, :], A["x_prompt"].rearrange("b (t p) d -> p (b t) d", p=P)).then_inc(x_ready, 16)
            sp.dma_start(G.h[0:NSMP, 8, :], A["x_sample"].rearrange("b s d -> (b s) d")).then_inc(x_ready, 16)
            sp.wait_ge(c_ready, 16 * 4 + ONE)

        @block.gpsimd
        def _(pool):
            begin(pool, zeroed)
            pool.memset(G.h[NSMP:P, 8, :], 0.0).then_inc(zeroed, 1)

        @block.vector
        def _(dve):
            dve.memset(G.ones[:, :], 1.0)

        @block.scalar
        def _(act):
            begin(act, c_ready, squares)
            act.dma_start(G.ident[:, :], A["c_ident"]).then_inc(c_ready, 16)
            act.dma_start(G.upper[:, :], A["c_upper"]).then_inc(c_ready, 16)
            act.dma_start(G.iota[:, :], A["c_iota"]).then_inc(c_ready, 16)
            act.dma_start(G.gcol[:, :, :], A["gains_col"]).then_inc(c_ready, 16)
            act.wait_ge(x_ready, 32 + ONE)
            act.wait_ge(zeroed, 1 + ONE)
            with act.Fori(0, TILES) as t:
                act.wait_ge(squares, t + ONE)
                act.activation(junk[:, 0, :], G.h[:, bass.ds(t, 1), :], ACT.Square,
                               accum_out=G.ssq[:, bass.ds(t, 1)]).then_inc(squares, 1)
    c.close()


def stage_norm(nc, G, tag, gain, xT):
    S = G.sem
    var_ok, root_ok, rstd_ok, rows_ok, tr_ok, out_ok, pad_ok = (
        S(f"{tag}_{n}") for n in ("var", "root", "rstd", "rows", "transposed", "out", "pad"))
    c = Ctx(nc, tag + "_")
    st = c.sb("stats", [P, 3, TILES])
    rows = c.sb("rows", [P, 3, D])
    tp = [c.ps(f"tp{u}", [P, DK, P]) for u in range(3)]
    with nc.Block() as block:
        @block.scalar
        def _(act):
            begin(act, root_ok)
            act.wait_ge(var_ok, 1 + ONE)
            act.activation(st[:, 1, :], st[:, 0, :], ACT.Sqrt).then_inc(root_ok, 1)

        @block.vector
        def _(dve):
            begin(dve, var_ok, rstd_ok, rows_ok, out_ok)
            dve.tensor_scalar(st[:, 0, :], G.ssq[:, :], 1.0 / D, EPS, ALU.mult, ALU.add).then_inc(var_ok, 1)
            dve.wait_ge(root_ok, 1 + ONE)
            dve.reciprocal(st[:, 2, :], st[:, 1, :]).then_inc(rstd_ok, 1)
            dve.wait_ge(rstd_ok, 1 + ONE)
            with dve.Fori(0, TILES // 3) as i:
                for u in range(3):
                    t = i * 3 + u
                    dve.wait_ge(tr_ok, i * 3 + ONE)
                    dve.tensor_scalar(rows[:, u, :], G.h[:, bass.ds(t, 1), :], st[:, 2, bass.ds(t, 1)], None,
                                      ALU.mult).then_inc(rows_ok, 1)
                for u in range(3):
                    t = i * 3 + u
                    dve.wait_ge(tr_ok, t + 1 + ONE)
                    dst = xT[:, :, bass.ds(t * P, P)]
                    if gain is None:
                        dve.tensor_copy(dst, tp[u][:, :, :]).then_inc(out_ok, 1)
                    else:
                        g = G.gcol[:, gain, :].unsqueeze(2).to_broadcast([P, DK, P])
                        dve.tensor_tensor(dst, tp[u][:, :, :], g, ALU.mult).then_inc(out_ok, 1)

        @block.tensor
        def _(pe):
            begin(pe, tr_ok)
            with pe.Fori(0, TILES // 3) as i:
                for u in range(3):
                    pe.wait_ge(rows_ok, i * 3 + u + 1 + ONE)
                    pe.wait_ge(out_ok, i * 3 + ONE)
                    for k in range(DK):
                        mm = pe.transpose(tp[u][:, k, :], rows[:, u, k * P:(k + 1) * P], G.ident[:, :])
                    mm.then_inc(tr_ok, 1)
    c.close()


def stage_conv(nc, G, A, xT, zT, w_out):
    S = G.sem
    w_ready, bsb_used = ([S(f"cv_{n}{u}") for u in range(2)] for n in ("w_ready", "b_used"))
    cb_ok, u_ok = ([S(f"cv_{n}{v}") for v in range(2)] for n in ("copied", "gated"))
    small_ready, prod_ok, chain, last_ok, stored, zero_ok, wo_ready = (S("cv_" + n) for n in (
        "small_ready", "product", "chain", "last", "stored", "zeroed", "w_out_ready"))
    c = Ctx(nc, "cv_")
    win = c.sb("win", [P, 2, DK, 3, P])
    kc = c.sb("kc", [P, DK, CONV])
    hist = c.sb("hist", [P, DK, DEC_B, CONV - 1])
    csb = c.sb("csb", [P, 2, 384])
    bsb = c.sb("bsb", [P, 2, NTOK])
    ub = c.sb("ub", [P, 2, UW + DEC_B * US])
    acc = c.sb("acc", [P, 2, NTOK])
    last = c.sb("last", [P, DK, (CONV - 1) * (1 + DEC_B)])
    pp = [[c.ps(f"pp{part}{v}", [P, 512]) for v in range(2)] for part in range(3)]
    NC = len(CHUNKS)

    def hist_view(u):
        return ub[:, u, UW:].rearrange("p (b s) -> p b s", s=US)

    with nc.Block() as block:
        @block.sync
        def _(sp):
            begin(sp, small_ready, w_ready, wo_ready, stored)
            sp.dma_start(kc[:, :, :], A["conv_kernel_col"]).then_inc(small_ready, 16)
            sp.dma_start(hist[:, :, :, :], A["state_col"]).then_inc(small_ready, 16)
            for u in range(2):
                sp.dma_start(win[:, u], A["conv_w_in_t"][u]).then_inc(w_ready[u], 16)
            sp.dma_start(w_out[:, :, :], A["conv_w_out"].rearrange("a (k p) n -> p (a k) n", p=P)).then_inc(wo_ready, 16)
            with sp.Fori(0, DK // 2 - 1) as i:
                for u in range(2):
                    sp.wait_ge(prod_ok, (i * 2 + u + 1) * NC + ONE)
                    sp.dma_start(win[:, u], A["conv_w_in_t"][bass.ds(i * 2 + 2 + u, 1)]
                                 .rearrange("a p k c n -> p (a k) c n")).then_inc(w_ready[u], 16)
            sp.wait_ge(last_ok, DK + ONE)
            sp.dma_start(A["o_conv"], last[:, :, :]).then_inc(stored, 16)
            sp.wait_ge(stored, 16 + ONE)
            sp.wait_ge(wo_ready, 16 + ONE)

        @block.gpsimd
        def _(pool):
            begin(pool, zero_ok)
            pool.memset(ub[:, :, 0:CONV - 1], 0.0).then_inc(zero_ok, 1)
            pool.wait_ge(zero_ok, 1 + ONE)
            pool.memset(zT[:, :, NTOK:], 0.0).then_inc(zero_ok, 1)

        @block.tensor
        def _(pe):
            begin(pe, prod_ok)
            with pe.Fori(0, DK // 2) as i:
                for u in range(2):
                    pe.wait_ge(w_ready[u], i * 16 + 16 + ONE)
                    for n, (c0, cn) in enumerate(CHUNKS):
                        m = u * NC + n
                        pe.wait_ge(cb_ok[m % 2], i * NC + m // 2 + ONE)
                        pe.wait_ge(u_ok[m % 2], i * NC + m // 2 + ONE)
                        for part in range(3):
                            for k in range(DK):
                                mm = pe.matmul(pp[part][m % 2][:, 0:cn], win[:, u, k, part, :], xT[:, k, c0:c0 + cn],
                                               start=(k == 0), stop=(k == DK - 1))
                        mm.then_inc(prod_ok, 1)

        @block.scalar
        def _(act):
            begin(act, cb_ok)
            with act.Fori(0, DK // 2) as i:
                for u in range(2):
                    act.wait_ge(bsb_used[u], i + ONE)
                    for n, (c0, cn) in enumerate(CHUNKS):
                        m = u * NC + n
                        act.wait_ge(prod_ok, i * (2 * NC) + m + 1 + ONE)
                        act.wait_ge(u_ok[m % 2], i * NC + m // 2 + ONE)
                        act.activation(bsb[:, u, c0:c0 + cn], pp[1][m % 2][:, 0:cn], ACT.Copy)
                        act.activation(csb[:, m % 2, 0:cn], pp[0][m % 2][:, 0:cn], ACT.Copy).then_inc(cb_ok[m % 2], 1)

        @block.vector
        def _(dve):
            begin(dve, u_ok, last_ok, bsb_used, chain)
            dve.wait_ge(small_ready, 32 + ONE)
            dve.wait_ge(zero_ok, 2 + ONE)
            LINKS = 2 * CONV
            with dve.Fori(0, DK // 2) as i:
                for u in range(2):
                    f = i * 2 + u
                    link = Chain(dve, chain, f * LINKS)
                    dve.tensor_copy(hist_view(u)[:, :, 0:CONV - 1],
                                    hist[:, bass.ds(f, 1), :, :].rearrange("p a b s -> p (a b) s"))
                    for n, (c0, cn) in enumerate(CHUNKS):
                        m = u * NC + n
                        dve.wait_ge(cb_ok[m % 2], i * NC + m // 2 + 1 + ONE)
                        q, cs = pp[2][m % 2], csb[:, m % 2, :]
                        w = cn if n < NC - 1 else C2P
                        up = dve.tensor_tensor(ub[:, u, CONV - 1 + c0:CONV - 1 + c0 + w], q[:, 0:w], cs[:, 0:w], ALU.mult)
                        if n == NC - 1:
                            up = dve.tensor_tensor(hist_view(u)[:, :, CONV - 1:],
                                                   q[:, w:cn].rearrange("p (b s) -> p b s", s=DEC_S),
                                                   cs[:, w:cn].rearrange("p (b s) -> p b s", s=DEC_S), ALU.mult)
                        up.then_inc(u_ok[m % 2], 1)
                    dve.wait_ge(u_ok[m % 2], i * NC + m // 2 + 1 + ONE)
                    dve.tensor_copy(last[:, bass.ds(f, 1), 0:CONV - 1], ub[:, u, SEQ:UW])
                    dve.tensor_copy(last[:, bass.ds(f, 1), CONV - 1:].rearrange("p a (b s) -> p (a b) s", s=CONV - 1),
                                    hist_view(u)[:, :, DEC_S:]).then_inc(last_ok, 1)
                    for j in range(CONV):
                        k = kc[:, bass.ds(f, 1), j]
                        for src, dst in (
                            (ub[:, u, j:j + SEQ], acc[:, u, 0:SEQ]),
                            (hist_view(u)[:, :, j:j + DEC_S], acc[:, u, SEQ:].rearrange("p (b s) -> p b s", s=DEC_S)),
                        ):
                            if j == 0:
                                op = dve.tensor_scalar(dst, src, k, None, ALU.mult)
                            else:
                                op = dve.scalar_tensor_tensor(out=dst, in0=src, scalar=k, in1=dst,
                                                              op0=ALU.mult, op1=ALU.add)
                            link(op)
                    assert link.n == LINKS
                    dve.tensor_tensor(zT[:, bass.ds(f, 1), 0:NTOK], acc[:, u, :], bsb[:, u, :],
                                      ALU.mult).then_inc(bsb_used[u], 1)
    c.close()
def stage_project(nc, G, tag, zT, w):
    S = G.sem
    staged, used, prod, added, sq = (S(f"{tag}_{n}") for n in ("staged", "used", "product", "added", "squares"))
    c = Ctx(nc, tag + "_")
    st = c.sb("stage", [P, 3, DK, P])
    junk = c.sb("junk", [P, D])
    py = [c.ps(f"py{u}", [P, 2, 512]) for u in range(3)]
    with nc.Block() as block:
        @block.gpsimd
        def _(pool):
            begin(pool, staged)
            with pool.Fori(0, TILES // 3) as i:
                for u in range(3):
                    pool.wait_ge(prod, i * 3 + ONE)
                    pool.tensor_copy(st[:, u], zT[:, :, bass.ds((i * 3 + u) * P, P)]).then_inc(staged, 1)

        @block.tensor
        def _(pe):
            begin(pe, prod)
            with pe.Fori(0, TILES // 3) as i:
                for u in range(3):
                    pe.wait_ge(staged, i * 3 + u + 1 + ONE)
                    pe.wait_ge(added, i * 3 + ONE)
                    for half in range(2):
                        for k in range(DK):
                            mm = pe.matmul(py[u][:, half, :], st[:, u, k, :], w[:, k, half * 512:(half + 1) * 512],
                                           start=(k == 0), stop=(k == DK - 1))
                    mm.then_inc(prod, 1)

        @block.vector
        def _(dve):
            begin(dve, added)
            with dve.Fori(0, TILES // 3) as i:
                for u in range(3):
                    t = i * 3 + u
                    dve.wait_ge(prod, t + 1 + ONE)
                    row = G.h[:, bass.ds(t, 1), :].rearrange("p a d -> p (a d)")
                    dve.tensor_tensor(row, py[u][:, :, :].rearrange("p a n -> p (a n)"), row, ALU.add).then_inc(added, 1)

        @block.scalar
        def _(act):
            begin(act, sq)
            with act.Fori(0, TILES) as t:
                act.wait_ge(added, t + 1 + ONE)
                act.wait_ge(sq, t + ONE)
                act.activation(junk[:, :], G.h[:, bass.ds(t, 1), :], ACT.Square,
                               accum_out=G.ssq[:, bass.ds(t, 1)]).then_inc(sq, 1)
    c.close()
def stage_route(nc, G, A, tag, layer, gain, R):
    S = G.sem
    (var_ok, root_ok, rstd_ok, rows_ok, tr_ok, xt_ok, small_ready, logit_ok, bias_ok, chain, exp_in, exp_ok, both_ok,
     count_ok, hot_ok, tok_ok) = (S(f"{tag}_{n}") for n in (
         "var", "root", "rstd", "rows", "transposed", "xt", "small_ready", "logits", "biased", "chain", "exp_in",
         "exp", "both", "counted", "one_hot", "slot_tok"))
    stored = [S(f"{tag}_stored{u}") for u in range(3)]
    c = Ctx(nc, tag + "_")
    st = c.sb("stats", [P, 3, TILES])
    rows = c.sb("rows", [P, 3, D])
    xt = c.sb("xt", [P, 3, DK, P])
    wr = c.sb("wr", [P, DK, ROUTE])
    bias = c.sb("bias", [P, ROUTE])
    lg = c.sb("logits", [P, TILES, ROUTE])
    tp = [c.ps(f"tp{u}", [P, DK, P]) for u in range(3)]
    pl = [c.ps(f"pl{u}", [P, 512]) for u in range(2)]

    T = TILES
    e4 = c.sb("e4", [P, 6, T, EG])
    group, pick1, pick2, l4, l4b, tmp4 = (e4[:, n] for n in range(6))
    col = c.sb("col", [P, 8, T])
    m, s, m1, m2, ge, gp, r, e2 = (col[:, n] for n in range(8))
    big = c.sb("big", [P, 5, T, NE])
    sel, hot1, hot2, both, slots = (big[:, n] for n in range(5))
    pre = c.sb("pre", [P, T + 1, NE])
    tot = c.sb("tot", [P, T, NE])
    exp_t = c.sb("exp_t", [P, 2, T, EG])
    ex = c.sb("ex", [P, 5, NE])
    nb, ends, base, one16, _spare = (ex[:, n] for n in range(5))
    cmp9 = c.sb("cmp9", [P, NE, T])
    cmpb = c.sb("cmpb", [P, MBLK, NE])
    bef = c.sb("bef", [P, MBLK])
    slotf = c.sb("slotf", [P, 2, T])
    part_i = c.sb("part_i", [P, 2, 2, T], I32)
    part_f = c.sb("part_f", [P, 2, 2, T])
    hr = c.sb("hr", [P, 2, P])
    hb = c.sb("hb", [P, 2, MBLK])
    iota = G.iota
    desc = iota[:, P + T:P + T + EG].unsqueeze(1).to_broadcast([P, T, EG])
    steps = iota[:, P + T + EG:P + 2 * T + EG].unsqueeze(1).to_broadcast([P, NE, T])

    def b4(x):
        return x.unsqueeze(2).to_broadcast([P, T, EG])

    with nc.Block() as block:
        @block.sync
        def _(sp):
            begin(sp, small_ready, stored)
            sp.dma_start(wr[:, :, :], A["router_w"][:, layer]).then_inc(small_ready, 16)
            sp.dma_start(bias[:, 0:EG], A["router_group_b"][layer, :].partition_broadcast(P)).then_inc(small_ready, 16)
            sp.dma_start(bias[:, EG:], A["router_expert_b"][layer, :].partition_broadcast(P)).then_inc(small_ready, 16)
            with sp.Fori(0, T // 3) as i:
                for u in range(3):
                    sp.wait_ge(rows_ok, i * 3 + u + 1 + ONE)
                    sp.dma_start(A["s_rows"][bass.ds((i * 3 + u) * P, P), :], rows[:, u, :]).then_inc(stored[u], 16)
            for u in range(3):
                sp.wait_ge(stored[u], 16 * (T // 3) + ONE)

        @block.scalar
        def _(act):
            begin(act, root_ok, exp_ok)
            act.wait_ge(var_ok, 1 + ONE)
            act.activation(st[:, 1, :], st[:, 0, :], ACT.Sqrt).then_inc(root_ok, 1)
            act.wait_ge(exp_in, 1 + ONE)
            act.activation(exp_t[:, 1], exp_t[:, 0], ACT.Exp).then_inc(exp_ok, 1)
            act.wait_ge(exp_in, 2 + ONE)
            act.activation(e2, ge, ACT.Exp).then_inc(exp_ok, 1)

        @block.tensor
        def _(pe):
            begin(pe, tr_ok, logit_ok, count_ok, tok_ok)
            pe.wait_ge(small_ready, 48 + ONE)
            with pe.Fori(0, T // 3) as i:
                for u in range(3):
                    pe.wait_ge(rows_ok, i * 3 + u + 1 + ONE)
                    pe.wait_ge(xt_ok, i * 3 + ONE)
                    for k in range(DK):
                        mm = pe.transpose(tp[u][:, k, :], rows[:, u, k * P:(k + 1) * P], G.ident[:, :])
                    mm.then_inc(tr_ok, 1)
                for u in range(3):
                    pe.wait_ge(xt_ok, i * 3 + u + 1 + ONE)
                    pe.wait_ge(bias_ok, i * 3 + u + ONE)
                    for k in range(DK):
                        mm = pe.matmul(pl[0][:, 0:ROUTE], xt[:, u, k, :], wr[:, k, :], start=(k == 0), stop=(k == DK - 1))
                    mm.then_inc(logit_ok, 1)
            pe.wait_ge(both_ok, 1 + ONE)
            pe.matmul(pl[0][:, 0:T * NE], G.upper[:, :], both.rearrange("p t e -> p (t e)"), start=True, stop=True)
            pe.matmul(pl[1][:, 0:T * NE], G.ones[:, :], both.rearrange("p t e -> p (t e)"), start=True, stop=True)\
                .then_inc(count_ok, 1)
            n = 0
            for t in range(T):
                rows_in = P if t < T - 1 else NTOK - P * (T - 1)
                for k in range(2):
                    pe.wait_ge(hot_ok, n + 1 + ONE)
                    mm = pe.matmul(pl[1][:, 256:256 + MBLK], hr[0:rows_in, n % 2, :], hb[0:rows_in, n % 2, :],
                                   start=(n == 0), stop=(n == 2 * T - 1))
                    mm.then_inc(tok_ok, 1)
                    n += 1

        @block.vector
        def _(dve):
            begin(dve, var_ok, rstd_ok, rows_ok, xt_ok, bias_ok, exp_in, both_ok, hot_ok, chain)
            dve.tensor_scalar(st[:, 0, :], G.ssq[:, :], 1.0 / D, EPS, ALU.mult, ALU.add).then_inc(var_ok, 1)
            dve.wait_ge(root_ok, 1 + ONE)
            dve.reciprocal(st[:, 2, :], st[:, 1, :]).then_inc(rstd_ok, 1)
            dve.wait_ge(rstd_ok, 1 + ONE)
            dve.wait_ge(small_ready, 48 + ONE)
            with dve.Fori(0, T // 3) as i:
                for u in range(3):
                    t = i * 3 + u
                    dve.wait_ge(tr_ok, i * 3 + ONE)
                    dve.wait_ge(stored[u], i * 16 + ONE)
                    dve.tensor_scalar(rows[:, u, :], G.h[:, bass.ds(t, 1), :], st[:, 2, bass.ds(t, 1)], None,
                                      ALU.mult).then_inc(rows_ok, 1)
                for u in range(3):
                    t = i * 3 + u
                    dve.wait_ge(tr_ok, t + 1 + ONE)
                    dve.wait_ge(logit_ok, i * 3 + ONE)
                    g = G.gcol[:, gain, :].unsqueeze(2).to_broadcast([P, DK, P])
                    dve.tensor_tensor(xt[:, u], tp[u][:, :, :], g, ALU.mult).then_inc(xt_ok, 1)
                for u in range(3):
                    t = i * 3 + u
                    dve.wait_ge(logit_ok, t + 1 + ONE)
                    dve.tensor_tensor(lg[:, bass.ds(t, 1), :].rearrange("p a n -> p (a n)"), pl[0][:, 0:ROUTE],
                                      bias[:, :], ALU.add).then_inc(bias_ok, 1)
            dve.wait_ge(bias_ok, T + ONE)
            link = Chain(dve, chain)

            def tt(out, a, b, op):
                link(dve.tensor_tensor(out, a, b, op))

            def first_max(logits, top, hot):
                link(dve.tensor_reduce(top, logits, AX.X, ALU.max))
                tt(hot, logits, b4(top), ALU.is_equal)
                tt(hot, hot, desc, ALU.mult)
                link(dve.tensor_reduce(s, hot, AX.X, ALU.max))
                tt(hot, hot, b4(s), ALU.is_equal)

            grp = lg[:, :, 0:EG]
            first_max(grp, m, group)
            dve.tensor_tensor(exp_t[:, 0], grp, b4(m), ALU.subtract).then_inc(exp_in, 1)
            lexp = lg[:, :, EG:].rearrange("p t (g j) -> p t g j", j=EG)
            hot_g = group.unsqueeze(3).to_broadcast([P, T, EG, EG])
            sel4 = sel.rearrange("p t (g j) -> p t g j", j=EG)
            tt(sel4, lexp, hot_g, ALU.mult)
            link(dve.tensor_reduce(l4, sel4.rearrange("p t g j -> p t j g"), AX.X, ALU.add))
            first_max(l4, m1, pick1)
            link(dve.scalar_tensor_tensor(out=l4b, in0=pick1, scalar=NEG, in1=l4, op0=ALU.mult, op1=ALU.add))
            first_max(l4b, m2, pick2)
            dve.tensor_tensor(ge, m2, m1, ALU.subtract).then_inc(exp_in, 1)
            for hot, pick in ((hot1, pick1), (hot2, pick2)):
                tt(hot.rearrange("p t (g j) -> p t g j", j=EG), hot_g,
                   pick.unsqueeze(2).to_broadcast([P, T, EG, EG]), ALU.mult)
            tt(both, hot1, hot2, ALU.add)
            dve.memset(both[NTOK - P * (T - 1):, T - 1:T, :], 0.0).then_inc(both_ok, 1)
            dve.wait_ge(exp_ok, 2 + ONE)
            link(dve.tensor_reduce(s, exp_t[:, 1], AX.X, ALU.add))
            link(dve.reciprocal(gp, s))
            link(dve.tensor_scalar(r, e2, 1.0, None, ALU.add))
            link(dve.reciprocal(r, r))
            tt(R.gates[:, 0], gp, r, ALU.mult)
            tt(R.gates[:, 1], R.gates[:, 0], e2, ALU.mult)
            dve.wait_ge(count_ok, 1 + ONE)
            link(dve.tensor_copy(tot.rearrange("p t e -> p (t e)"), pl[1][:, 0:T * NE]))
            link(dve.memset(pre[:, 0], 0.0))
            for t in range(T):
                tt(pre[:, t + 1], pre[:, t], tot[:, t], ALU.add)
            tt(cmp9[:, :, :], pre[:, T].unsqueeze(2).to_broadcast([P, NE, T]), steps, ALU.is_gt)
            link(dve.tensor_reduce(nb, cmp9[:, :, :], AX.X, ALU.add))
            link(dve.memset(one16, 1.0))
            link(dve.tensor_tensor_scan(ends, one16, nb, 0.0, ALU.mult, ALU.add))
            tt(base, ends, nb, ALU.subtract)
            link(dve.tensor_scalar(base, base, float(P), None, ALU.mult))
            tt(slots, pl[0][:, 0:T * NE].rearrange("p (t e) -> p t e", e=NE), pre[:, 0:T], ALU.add)
            tt(slots, slots, base.unsqueeze(1).to_broadcast([P, T, NE]), ALU.add)
            for k, hot in enumerate((hot1, hot2)):
                tt(sel, slots, hot, ALU.mult)
                link(dve.tensor_reduce(slotf[:, k], sel, AX.X, ALU.add))
            link(dve.tensor_copy(R.slot[:, :, :], slotf[:, :, :]))
            link(dve.tensor_scalar(part_i[:, 0], R.slot[:, :, :], 7, None, ALU.logical_shift_right))
            link(dve.tensor_scalar(part_i[:, 1], R.slot[:, :, :], P - 1, None, ALU.bitwise_and))
            link(dve.tensor_copy(part_f.rearrange("p a k t -> p (a k t)"), part_i.rearrange("p a k t -> p (a k t)")))
            tt(cmpb[:, :, :], ends.unsqueeze(1).to_broadcast([P, MBLK, NE]),
               iota[:, 0:MBLK].unsqueeze(2).to_broadcast([P, MBLK, NE]), ALU.is_le)
            link(dve.tensor_reduce(bef[:, :], cmpb[:, :, :], AX.X, ALU.add))
            link(dve.tensor_scalar(R.block_expert[:, :], bef[:, :], float(NE - 1), None, ALU.min))
            n = 0
            for t in range(T):
                for k in range(2):
                    if n >= 2:
                        dve.wait_ge(tok_ok, n - 1 + ONE)
                    dve.tensor_scalar(hr[:, n % 2, :], iota[:, 0:P], part_f[:, 1, k, t:t + 1], None, ALU.is_equal)
                    dve.tensor_scalar(hb[:, n % 2, :], iota[:, 0:MBLK], part_f[:, 0, k, t:t + 1],
                                      iota[:, P + t:P + t + 1], ALU.is_equal, ALU.mult).then_inc(hot_ok, 1)
                    n += 1
            dve.wait_ge(tok_ok, 2 * T + ONE)
            link(dve.tensor_copy(R.slot_tok[:, :], pl[1][:, 256:256 + MBLK]))
    c.close()


def stage_experts(nc, G, A, tag, layer, gain, R):
    S = G.sem

    def two(name):
        return [S(f"{tag}_{name}{u}") for u in range(2)]

    index_ok, gathered, w13_ready, w2_ready, stored, xt_ps, y_ok = (two(n) for n in (
        "index", "gathered", "w13", "w2", "stored", "x_transposed", "w2_product"))
    passed, xt_ok, a_ok, b_ok, silu_ok, hid_ok, hid_ps, ht_ok, ys_ok = (S(f"{tag}_{n}") for n in (
        "passed", "xt", "w1_product", "w3_product", "silu", "hidden", "hidden_transposed", "ht", "rows"))
    c = Ctx(nc, tag + "_")
    w13 = [c.sb(f"w13{u}", [P, 2, DK, DE]) for u in range(2)]
    w2 = [c.sb(f"w2{u}", [P, DE // P, D]) for u in range(2)]
    idx = [c.sb(f"idx{u}", [P, 1], I32) for u in range(2)]
    xg = [c.sb(f"xg{u}", [P, D]) for u in range(2)]
    xt = [c.sb(f"xt{u}", [P, DK, P]) for u in range(2)]
    sa = c.sb("sa", [P, 2, DE])
    hid = c.sb("hid", [P, 2, DE])
    ht = [c.sb(f"ht{u}", [P, DE // P, P]) for u in range(2)]
    ys = c.sb("ys", [P, 2, D])
    tp = c.ps("tp", [P, DK, P])
    pa = c.ps("pa", [P, DE])
    pb = c.ps("pb", [P, DE])
    ph = c.ps("ph", [P, DE // P, P])
    py = c.ps("py", [P, 2, 512])
    HK = DE // P
    w1_d = A["expert_w1"][layer].rearrange("e (k p) f -> e p k f", p=P)
    w3_d = A["expert_w3"][layer].rearrange("e (k p) f -> e p k f", p=P)
    w2_d = A["expert_w2"][layer].rearrange("e (k p) d -> e p k d", p=P)
    assert MBLK % 2 == 0

    with nc.Block() as block:
        @block.sync
        def _(sp):
            begin(sp, w13_ready, w2_ready)
            def load(b, u, n):
                first = isinstance(n, int)
                e = sp.value_load(R.block_expert[0:1, bass.ds(b, 1)], min_val=0, max_val=NE - 1)
                if not first:
                    sp.wait_ge(b_ok, b - 1 + ONE)
                sp.dma_start(w13[u][:, 0], w1_d[bass.ds(e, 1)].rearrange("a p k f -> p (a k) f")).then_inc(w13_ready[u], 16)
                sp.dma_start(w13[u][:, 1], w3_d[bass.ds(e, 1)].rearrange("a p k f -> p (a k) f")).then_inc(w13_ready[u], 16)
                if not first:
                    sp.wait_ge(y_ok[u], n + ONE)
                sp.dma_start(w2[u][:, :, :], w2_d[bass.ds(e, 1)].rearrange("a p k d -> p (a k) d")).then_inc(w2_ready[u], 16)

            load(0, 0, 0)
            load(1, 1, 0)
            with sp.Fori(0, MBLK // 2 - 1) as i:
                for u in range(2):
                    load(i * 2 + 2 + u, u, i + 1)

        @block.gpsimd
        def _(pool):
            begin(pool, index_ok)
            bound = pool.to_reg(NPAD - 1)
            with pool.Fori(0, MBLK // 2) as i:
                for u in range(2):
                    b = i * 2 + u
                    pool.wait_ge(xt_ps[u], i + ONE)
                    pool.tensor_copy(idx[u][:, :], R.slot_tok[:, bass.ds(b, 1)]).then_inc(index_ok[u], 1)
                    pool.wait_ge(index_ok[u], i + 1 + ONE)
                    pool.sem_inc(passed, 1)
                    pool.indirect_dma_start(out=xg[u][:, :], out_offset=None, in_=A["s_rows"][:, :],
                                            in_offset=bass.IndirectOffsetOnAxis(ap=idx[u][:, 0:1], axis=0),
                                            bounds_check=bound).then_inc(gathered[u], 16)

        @block.tensor
        def _(pe):
            begin(pe, xt_ps, a_ok, b_ok, hid_ps, y_ok)
            def x_transposes(b, u, n):
                pe.wait_ge(gathered[u], n * 16 + 16)
                pe.wait_ge(xt_ok, b + ONE)
                for k in range(DK):
                    mm = pe.transpose(tp[:, k, :], xg[u][:, k * P:(k + 1) * P], G.ident[:, :])
                mm.then_inc(xt_ps[u], 1)

            def up(b, u, n):
                pe.wait_ge(w13_ready[u], n * 32 + 32 + ONE)
                pe.wait_ge(xt_ok, b + 1 + ONE)
                pe.wait_ge(silu_ok, b + ONE)
                for k in range(DK):
                    mm = pe.matmul(pa[:, :], xt[u][:, k, :], w13[u][:, 0, k, :], start=(k == 0), stop=(k == DK - 1))
                mm.then_inc(a_ok, 1)

            def gate(b, u):
                pe.wait_ge(hid_ok, b + ONE)
                for k in range(DK):
                    mm = pe.matmul(pb[:, :], xt[u][:, k, :], w13[u][:, 1, k, :], start=(k == 0), stop=(k == DK - 1))
                mm.then_inc(b_ok, 1)

            def hidden_transposes(b, u):
                pe.wait_ge(hid_ok, b + 1 + ONE)
                pe.wait_ge(ht_ok, b + ONE)
                for k in range(HK):
                    mm = pe.transpose(ph[:, k, :], hid[:, u, k * P:(k + 1) * P], G.ident[:, :])
                mm.then_inc(hid_ps, 1)

            def down(b, u, n):
                pe.wait_ge(w2_ready[u], n * 16 + 16 + ONE)
                pe.wait_ge(ht_ok, b + 1 + ONE)
                pe.wait_ge(ys_ok, b + ONE)
                for half in range(2):
                    for k in range(HK):
                        mm = pe.matmul(py[:, half, :], ht[u][:, k, :], w2[u][:, k, half * 512:(half + 1) * 512],
                                       start=(k == 0), stop=(k == HK - 1))
                mm.then_inc(y_ok[u], 1)

            def step(b, u, n, more):
                before = (b - 1, 1 - u, n - 1 + u)
                up(b, u, n)
                hidden_transposes(*before[:2])
                gate(b, u)
                if more:
                    x_transposes(b + 1, 1 - u, n + u)
                down(*before)

            x_transposes(0, 0, 0)
            up(0, 0, 0)
            gate(0, 0)
            x_transposes(1, 1, 0)
            with pe.Fori(0, MBLK // 2 - 1) as i:
                step(i * 2 + 1, 1, i, True)
                step(i * 2 + 2, 0, i + 1, True)
            step(MBLK - 1, 1, MBLK // 2 - 1, False)
            hidden_transposes(MBLK - 1, 1)
            down(MBLK - 1, 1, MBLK // 2 - 1)

        @block.scalar
        def _(act):
            begin(act, silu_ok, ys_ok, stored)
            def silu(b, u):
                act.wait_ge(a_ok, b + 1 + ONE)
                if not isinstance(b, int) or b > 0:
                    act.wait_ge(hid_ok, b - 1 + ONE)
                act.activation(sa[:, u, :], pa[:, :], ACT.Silu).then_inc(silu_ok, 1)

            def rows(b, u, n):
                act.wait_ge(y_ok[u], n + 1 + ONE)
                act.wait_ge(stored[u], n * 16 + ONE)
                act.activation(ys[:, u, :], py[:, :, :].rearrange("p a n -> p (a n)"), ACT.Copy).then_inc(ys_ok, 1)
                act.wait_ge(ys_ok, b + 1 + ONE)
                act.dma_start(A["s_ys"][bass.ds(b * P, P), :], ys[:, u, :]).then_inc(stored[u], 16)

            silu(0, 0)
            with act.Fori(0, MBLK // 2 - 1) as i:
                silu(i * 2 + 1, 1)
                rows(i * 2, 0, i)
                silu(i * 2 + 2, 0)
                rows(i * 2 + 1, 1, i)
            silu(MBLK - 1, 1)
            rows(MBLK - 2, 0, MBLK // 2 - 1)
            rows(MBLK - 1, 1, MBLK // 2 - 1)
            for u in range(2):
                act.wait_ge(stored[u], 16 * (MBLK // 2) + ONE)

        @block.vector
        def _(dve):
            begin(dve, xt_ok, hid_ok, ht_ok)
            g = G.gcol[:, gain, :].unsqueeze(2).to_broadcast([P, DK, P])

            def x_scaled(u, n, used):
                dve.wait_ge(xt_ps[u], n + 1 + ONE)
                dve.wait_ge(b_ok, used + ONE)
                dve.tensor_tensor(xt[u][:, :, :], tp[:, :, :], g, ALU.mult).then_inc(xt_ok, 1)

            def hidden(b, u):
                dve.wait_ge(b_ok, b + 1 + ONE)
                dve.wait_ge(silu_ok, b + 1 + ONE)
                if not isinstance(b, int) or b > 0:
                    dve.wait_ge(hid_ps, b - 1 + ONE)
                dve.tensor_tensor(hid[:, u, :], pb[:, :], sa[:, u, :], ALU.mult).then_inc(hid_ok, 1)

            def ht_out(b, u, n):
                dve.wait_ge(hid_ps, b + 1 + ONE)
                dve.wait_ge(y_ok[u], n + ONE)
                dve.tensor_copy(ht[u][:, :, :], ph[:, :, :]).then_inc(ht_ok, 1)

            x_scaled(0, 0, 0)
            hidden(0, 0)
            x_scaled(1, 0, 0)
            with dve.Fori(0, MBLK // 2 - 1) as i:
                ht_out(i * 2, 0, i)
                hidden(i * 2 + 1, 1)
                x_scaled(0, i + 1, i * 2 + 1)
                ht_out(i * 2 + 1, 1, i)
                hidden(i * 2 + 2, 0)
                x_scaled(1, i + 1, i * 2 + 2)
            ht_out(MBLK - 2, 0, MBLK // 2 - 1)
            hidden(MBLK - 1, 1)
            ht_out(MBLK - 1, 1, MBLK // 2 - 1)
    c.close()


def stage_combine(nc, G, A, tag, R):
    S = G.sem
    got = [S(f"{tag}_gathered{u}") for u in range(3)]
    first, done, sq = (S(f"{tag}_{n}") for n in ("first", "added", "squares"))
    c = Ctx(nc, tag + "_")
    y = [[c.sb(f"y{u}{k}", [P, D]) for k in range(2)] for u in range(3)]
    junk = c.sb("junk", [P, D])

    def rows_of(t):
        return P if t < TILES - 1 else NTOK - P * (TILES - 1)

    with nc.Block() as block:
        @block.gpsimd
        def _(pool):
            for t in range(TILES):
                if t >= 3:
                    pool.wait_ge(done, t - 2 + ONE)
                for k in range(2):
                    pool.indirect_dma_start(out=y[t % 3][k][0:rows_of(t), :], out_offset=None, in_=A["s_ys"][:, :],
                                            in_offset=bass.IndirectOffsetOnAxis(ap=R.slot[0:rows_of(t), k, t:t + 1], axis=0),
                                            bounds_check=MBLK * P - 1).then_inc(got[t % 3], 16)

        @block.vector
        def _(dve):
            begin(dve, first, done)
            for t in range(TILES):
                n = rows_of(t)
                dve.wait_ge(got[t % 3], 32 * (t // 3 + 1))
                for k, s in ((0, first), (1, done)):
                    dve.scalar_tensor_tensor(out=G.h[0:n, t, :], in0=y[t % 3][k][0:n, :], scalar=R.gates[0:n, k, t:t + 1],
                                             in1=G.h[0:n, t, :], op0=ALU.mult, op1=ALU.add).then_inc(s, 1)
                    dve.wait_ge(s, t + 1 + ONE)

        @block.scalar
        def _(act):
            begin(act, sq)
            with act.Fori(0, TILES) as t:
                act.wait_ge(done, t + 1 + ONE)
                act.wait_ge(sq, t + ONE)
                act.activation(junk[:, :], G.h[:, bass.ds(t, 1), :], ACT.Square,
                               accum_out=G.ssq[:, bass.ds(t, 1)]).then_inc(sq, 1)
    c.close()


def layer_moe(nc, G, A, layer, gain):
    R = Ctx(nc, f"moe{layer}_")
    R.gates = R.sb("gates", [P, 2, TILES])
    R.slot = R.sb("slot", [P, 2, TILES], I32)
    R.slot_tok = R.sb("slot_tok", [P, MBLK], I32)
    R.block_expert = R.sb("block_expert", [P, MBLK], I32)
    stage_route(nc, G, A, f"r{layer}", layer, gain, R)
    stage_experts(nc, G, A, f"e{layer}", layer, gain, R)
    stage_combine(nc, G, A, f"c{layer}", R)
    R.close()
SLOTS = 2 + GROUPS
K_SLOT, V_SLOT = 0, 1
Q_SLOT = 2
QT = SEQ // P
PAIRS = 4


def group_tiles():
    def plain(t):
        return lambda x: x[:, t * P:(t + 1) * P]

    def by4(nb, r):
        return lambda x: x[:, 4 * P * nb + r:4 * P * (nb + 1) - 3 + r:4]

    def by8(j):
        return lambda x: x[:, j:SEQ - 7 + j:8]

    out = []
    for t in range(QT):
        out.append((0, t, plain(t), [t] if t == 0 else [t - 1, t]))
    for nb in range(2):
        for r in range(4):
            out.append((1, 4 * nb + r, by4(nb, r), [4 * k + r for k in range(nb + 1)]))
    for j in range(8):
        out.append((2, j, by8(j), [j]))
    return out


def stage_heads(nc, G, A, xT, H):
    S = G.sem
    w_ready = [S(f"hd_w_ready{s}") for s in range(SLOTS)]
    scaled, proj_ok, pj_ok, pj_out, t1_ok, rope_ok, table_ready, k_stored, v_stored, o_stored = (
        S("hd_" + n) for n in ("w_scaled", "product", "bank_full", "bank_read", "rope_part", "rope",
                               "tables", "k_stored", "v_stored", "o_stored"))
    passed, sc_ok, masked, exp_ok, pt_ps, pt_ok = (S("hd_" + n) for n in (
        "passed", "scores", "masked", "exp", "p_transposed", "pt"))
    c = Ctx(nc, "hd_")
    wt = c.sb("wt", [P, SLOTS, DK, P])
    cos = c.sb("cos", [P, NTOK])
    sin = c.sb("sin", [P, NTOK])
    band = c.sb("band", [P, 2 * P])
    pair = c.sb("pair", [P, P])
    raw = c.sb("raw", [P, 2, NTOK])
    half = c.sb("half", [P, NTOK])
    hT = c.sb("hT", [P, SLOTS, NTOK])
    vb = c.sb("vb", [P, GROUPS, QT, HD])
    vs = c.sb("vs", [P, HD])
    sc = c.sb("sc", [P, 3, 2 * P])
    pr = c.sb("pr", [P, 3, 2 * P])
    pt = c.sb("pt", [P, 3, 2, P])
    ob = c.sb("ob", [P, GROUPS, QT, HD + 2])
    pj = [c.ps(f"pj{u}", [P, 512]) for u in range(3)]
    psc = [c.ps(f"psc{u}", [P, 512]) for u in range(2)]
    ppt = [c.ps(f"ppt{u}", [P, 2, P]) for u in range(2)]
    NC = len(CHUNKS)
    TL = group_tiles()
    NT = len(TL)

    uses = [("proj", s, n) for s in range(SLOTS) for n in range(NC)]
    v_batches = [TL[n:n + PAIRS] for n in range(0, NT, PAIRS)] + [None]
    uses += [("v", b) for b in range(len(v_batches))] + [("o", b) for b in range(NT // PAIRS)]
    NU = len(uses)
    O0 = SLOTS * NC + len(v_batches)

    def bank(n):
        return pj[n % 3]

    with nc.Block() as block:
        @block.sync
        def _(sp):
            begin(sp, table_ready, k_stored, v_stored, o_stored, w_ready)
            sp.dma_start(cos[:, :], A["c_cos"]).then_inc(table_ready, 16)
            sp.dma_start(sin[:, :], A["c_sin"]).then_inc(table_ready, 16)
            sp.dma_start(band[:, :], A["c_band"]).then_inc(table_ready, 16)
            sp.dma_start(pair[:, :], A["c_pair"]).then_inc(table_ready, 16)

            def stores(h):
                sp.wait_ge(rope_ok, h * (1 + GROUPS) + 1 + ONE)
                sp.dma_start(A["o_kT"][bass.ds(h, 1)].rearrange("a c t -> c (a t)"), hT[:, K_SLOT, :]).then_inc(k_stored, 16)
                sp.wait_ge(pj_out, h * NU + O0 + ONE)
                v_out = A["o_v"][:, bass.ds(h, 1), :].rearrange("t a c -> t (a c)")
                sp.dma_start(v_out[0:SEQ, :].rearrange("(t p) c -> p t c", p=P), vb[:, 0]).then_inc(v_stored, 16)
                sp.dma_start(v_out[SEQ:, :], vs[P - NSMP:, :]).then_inc(v_stored, 16)
                sp.wait_ge(pj_out, h * NU + NU + ONE)
                og = A["s_og"][:, :, bass.ds(h, 1), :].rearrange("g t a c -> g t (a c)")
                sp.dma_start(og[0].rearrange("(t p) c -> p t c", p=P), ob[:, 0]).then_inc(o_stored, 16)
                by4 = og[1].rearrange("(n p r) c -> n p r c", n=2, r=4)
                for n in range(2):
                    sp.dma_start(by4[n], ob[:, 1, 4 * n:4 * n + 4]).then_inc(o_stored, 16)
                sp.dma_start(og[2].rearrange("(n j) c -> n j c", j=8), ob[:, 2]).then_inc(o_stored, 16)

            for s in range(SLOTS):
                sp.dma_start(wt[:, s], A["w_heads"][0, s]).then_inc(w_ready[s], 16)
            with sp.Fori(0, HEADS - 1) as h:
                for s in range(SLOTS):
                    sp.wait_ge(proj_ok, (h * SLOTS + s + 1) * NC + ONE)
                    sp.dma_start(wt[:, s], A["w_heads"][bass.ds(h + 1, 1), s].rearrange("a p k n -> p (a k) n"))\
                        .then_inc(w_ready[s], 16)
                stores(h)
            stores(HEADS - 1)
            sp.wait_ge(k_stored, 16 * HEADS + ONE)
            sp.wait_ge(v_stored, 32 * HEADS + ONE)
            sp.wait_ge(o_stored, 64 * HEADS + ONE)

        @block.gpsimd
        def _(pool):
            begin(pool, scaled)
            with pool.Fori(0, HEADS) as h:
                for s in range(SLOTS):
                    g = G.gcol[:, GAIN_KV if s < Q_SLOT else GAIN_MIX1, :].unsqueeze(2).to_broadcast([P, DK, P])
                    pool.wait_ge(w_ready[s], h * 16 + 16 + ONE)
                    pool.wait_ge(scaled, h * SLOTS + s + ONE)
                    pool.tensor_tensor(wt[:, s], wt[:, s], g, ALU.mult).then_inc(scaled, 1)

        @block.tensor
        def _(pe):
            begin(pe, proj_ok, pj_ok, sc_ok, pt_ps)
            with pe.Fori(0, HEADS) as h:
                def claim(n):
                    pe.wait_ge(pj_out, (h * NU + n - 2 if n >= 2 else h * NU) + ONE)

                n = 0
                for s in range(SLOTS):
                    pe.wait_ge(scaled, h * SLOTS + s + 1 + ONE)
                    for c0, cn in CHUNKS:
                        claim(n)
                        for k in range(DK):
                            mm = pe.matmul(bank(n)[:, 0:cn], wt[:, s, k, :], xT[:, k, c0:c0 + cn],
                                           start=(k == 0), stop=(k == DK - 1))
                        mm.then_inc(proj_ok, 1)
                        n += 1
                pe.wait_ge(pj_out, h * NU + (V_SLOT + 1) * NC + ONE)
                for batch in v_batches:
                    claim(n)
                    if batch is None:
                        pe.transpose(bank(n)[:, 0:HD], hT[:, V_SLOT, NTOK - P:], G.ident[:, :]).then_inc(pj_ok, 1)
                    else:
                        for q, (g, t, view, keys) in enumerate(batch):
                            mm = pe.transpose(bank(n)[:, q * P:(q + 1) * P], view(hT[:, V_SLOT, :]), G.ident[:, :])
                        mm.then_inc(pj_ok, 1)
                    n += 1

                def scores(j):
                    g, t, view, keys = TL[j]
                    pe.wait_ge(rope_ok, h * (1 + GROUPS) + 2 + g + ONE)
                    pe.wait_ge(masked, (h * NT + j - 1 if j >= 2 else h * NT) + ONE)
                    kT = hT[:, K_SLOT, :]
                    for b, key in enumerate(keys):
                        kv = [x for x in TL if x[0] == g and x[1] == key][0][2]
                        mm = pe.matmul(psc[j % 2][:, b * P:(b + 1) * P], view(hT[:, Q_SLOT + g, :]), kv(kT),
                                       start=True, stop=True)
                    mm.then_inc(sc_ok, 1)

                def p_transposes(j):
                    pe.wait_ge(exp_ok, h * NT + j + 1 + ONE)
                    pe.wait_ge(pt_ok, (h * NT + j - 1 if j >= 2 else h * NT) + ONE)
                    for b in range(len(TL[j][3])):
                        mm = pe.transpose(ppt[j % 2][:, b, :], pr[:, j % 3, b * P:(b + 1) * P], G.ident[:, :])
                    mm.then_inc(pt_ps, 1)

                def weighted(j):
                    g, t, view, keys = TL[j]
                    if j % PAIRS == 0:
                        claim(O0 + j // PAIRS)
                    pe.wait_ge(pt_ok, h * NT + j + 1 + ONE)
                    for b, key in enumerate(keys):
                        mm = pe.matmul(bank(O0 + j // PAIRS)[:, (j % PAIRS) * P:(j % PAIRS + 1) * P], pt[:, j % 3, b, :],
                                       vb[:, g, key, :], start=(b == 0), stop=(b == len(keys) - 1))
                    if j % PAIRS == PAIRS - 1:
                        mm.then_inc(pj_ok, 1)

                pe.wait_ge(pj_out, h * NU + O0 + ONE)
                for j in range(NT + 3):
                    if j < NT:
                        scores(j)
                    if 0 <= j - 2 < NT:
                        p_transposes(j - 2)
                    if j >= 3:
                        weighted(j - 3)

        @block.scalar
        def _(act):
            begin(act, pj_out, exp_ok)
            with act.Fori(0, HEADS) as h:
                n = 0
                for s in range(SLOTS):
                    if s == V_SLOT:
                        dst = hT[:, V_SLOT, :]
                    else:
                        r = s if s == 0 else s - 1
                        dst = raw[:, r % 2, :]
                        act.wait_ge(rope_ok, (h * (1 + GROUPS) + r - 1 if r >= 2 else h * (1 + GROUPS)) + ONE)
                    for c0, cn in CHUNKS:
                        act.wait_ge(proj_ok, h * SLOTS * NC + n + 1 + ONE)
                        act.activation(dst[:, c0:c0 + cn], bank(n)[:, 0:cn], ACT.Copy).then_inc(pj_out, 1)
                        n += 1
                act.wait_ge(v_stored, h * 32 + ONE)
                for b, batch in enumerate(v_batches):
                    act.wait_ge(pj_ok, h * (NU - O0 + len(v_batches)) + b + 1 + ONE)
                    if batch is None:
                        act.activation(vs[:, :], bank(n)[:, 0:HD], ACT.Copy).then_inc(pj_out, 1)
                    else:
                        g, t = batch[0][:2]
                        act.activation(vb[:, g, t:t + PAIRS, :], bank(n)[:, :].rearrange("p (t c) -> p t c", c=HD),
                                       ACT.Copy).then_inc(pj_out, 1)
                    n += 1
                act.wait_ge(o_stored, h * 64 + ONE)
                for j in range(NT + 4):
                    if j < NT:
                        g, t, view, keys = TL[j]
                        w = len(keys) * P
                        act.wait_ge(masked, h * NT + j + 1 + ONE)
                        act.wait_ge(pt_ps, (h * NT + j - 2 if j >= 3 else h * NT) + ONE)
                        act.activation(pr[:, j % 3, 0:w], sc[:, j % 3, 0:w], ACT.Exp, bias=ob[:, g, t, HD:HD + 1],
                                       scale=-1.0, accum_out=ob[:, g, t, HD + 1:HD + 2]).then_inc(exp_ok, 1)
                    if j >= 4 and (j - 4) % PAIRS == PAIRS - 1:
                        b = (j - 4) // PAIRS
                        g, t = TL[b * PAIRS][:2]
                        act.wait_ge(pj_ok, h * (NU - O0 + len(v_batches)) + len(v_batches) + b + 1 + ONE)
                        act.activation(ob[:, g, t:t + PAIRS, 0:HD], bank(O0 + b)[:, :].rearrange("p (t c) -> p t c", c=HD),
                                       ACT.Copy).then_inc(pj_out, 1)

        @block.vector
        def _(dve):
            begin(dve, t1_ok, rope_ok, masked, pt_ok)
            dve.wait_ge(table_ready, 64 + ONE)
            HALF = HD // 2
            with dve.Fori(0, HEADS) as h:
                def rope(s, r):
                    dve.wait_ge(pj_out, h * NU + (s + 1) * NC + ONE)
                    if s == K_SLOT:
                        dve.wait_ge(k_stored, h * 16 + ONE)
                    src, dst = raw[:, r % 2, :], hT[:, s, :]
                    dve.tensor_tensor(dst, src, cos[:, :], ALU.mult)
                    dve.tensor_tensor(half[0:HALF, :], src[HALF:, :], sin[HALF:, :], ALU.mult)
                    dve.tensor_tensor(half[HALF:, :], src[0:HALF, :], sin[0:HALF, :], ALU.mult).then_inc(t1_ok, 1)
                    dve.wait_ge(t1_ok, h * (1 + GROUPS) + r + 1 + ONE)
                    dve.tensor_tensor(dst, dst, half[:, :], ALU.add).then_inc(rope_ok, 1)
                    dve.wait_ge(rope_ok, h * (1 + GROUPS) + r + 1 + ONE)
                    if s == K_SLOT:
                        dve.tensor_copy(H.ks[:, bass.ds(h, 1), :].rearrange("p a n -> p (a n)"), dst[:, SEQ:])
                    else:
                        dve.tensor_copy(H.qs[:, bass.ds(h, 1), s - Q_SLOT, :].rearrange("p a n -> p (a n)"), dst[:, SEQ:])

                for r, s in enumerate((K_SLOT, Q_SLOT, Q_SLOT + 1, Q_SLOT + 2)):
                    rope(s, r)
                for j in range(NT + 2):
                    if j < NT:
                        g, t, view, keys = TL[j]
                        w = len(keys) * P
                        mask = pair[:, :] if g == 2 else band[:, 2 * P - w:]
                        dve.wait_ge(sc_ok, h * NT + j + 1 + ONE)
                        dve.wait_ge(exp_ok, (h * NT + j - 2 if j >= 3 else h * NT) + ONE)
                        if j == 0:
                            dve.wait_ge(o_stored, h * 64 + ONE)
                        dve.sem_inc(passed, 1)
                        dve.tensor_tensor_reduce(out=sc[:, j % 3, 0:w], in0=psc[j % 2][:, 0:w], in1=mask, scale=-SCALE,
                                                 scalar=3.0e38, op0=ALU.add, op1=ALU.min,
                                                 accum_out=ob[:, g, t, HD:HD + 1]).then_inc(masked, 1)
                    if j >= 2:
                        b = j - 2
                        w = len(TL[b][3])
                        dve.wait_ge(pt_ps, h * NT + b + 1 + ONE)
                        dve.tensor_copy(pt[:, b % 3, 0:w, :], ppt[b % 2][:, 0:w, :]).then_inc(pt_ok, 1)
    c.close()


def stage_sample(nc, G, A, H):
    S = G.sem
    passed = S("sm_passed")
    (k_ready, v_ready, mask_ready, q_ok, kt_ps, kt_out, new_ok, st_ps, st_out, s_ps, masked, exp_ok, chain, norm_ok, pt_ps, pt_out,
     o_ps, o_out) = (S("sm_" + n) for n in (
         "k_ready", "v_ready", "mask_ready", "q", "kt_bank", "kt", "new_k", "st_bank", "st", "scores", "masked", "exp",
         "chain", "normed", "pt_bank", "pt", "o_bank", "o"))
    c = Ctx(nc, "sm_")
    NB = 2
    KC = PAST // P
    NK = PAST + DEC_S
    QN = GROUPS * DEC_S
    R = NB * HEADS * DEC_S
    assert R == P
    kc = c.sb("kc", [P, NB, KC, HEADS, HD])
    vc = c.sb("vc", [P, NB, KC, HEADS, HD])
    vn = c.sb("vn", [DEC_S, NB, HEADS, HD])
    mask = c.sb("mask", [P, GROUPS, NK])
    qb = c.sb("qb", [P, NB, HEADS, GROUPS, DEC_S])
    kT = c.sb("kT", [P, NB, HEADS, NK])
    sT = c.sb("sT", [P, KC + 1, GROUPS, NB, HEADS, DEC_S])
    sc = c.sb("sc", [P, GROUPS, NK])
    pr = c.sb("pr", [P, GROUPS, NK])
    stat = c.sb("stat", [P, 8])
    pT = c.sb("pT", [P, KC + 1, P])
    bk = [c.ps(f"bk{u}", [P, 4, P]) for u in range(2)]
    pst = [c.ps(f"pst{u}", [P, HEADS, GROUPS, DEC_S]) for u in range(2)]
    psc = c.ps("psc", [P, GROUPS, 512])
    px = c.ps("px", [P, 512])
    KB = NB * KC * HEADS // 4
    STEPS = DEC_B // NB
    LINKS = 5

    with nc.Block() as block:
        @block.sync
        def _(sp):
            begin(sp, mask_ready, k_ready, v_ready)
            sp.dma_start(mask[:, :, :], A["c_smp"]).then_inc(mask_ready, 16)
            with sp.Fori(0, STEPS) as i:
                sp.wait_ge(kt_ps, i * KB + ONE)
                for b in range(NB):
                    sp.dma_start(kc[:, b], A["cache_k"][bass.ds(i * NB + b, 1)].rearrange("a (k p) h c -> p (a k) h c", p=P))\
                        .then_inc(k_ready, 16)
                sp.wait_ge(o_ps, i + ONE)
                for b in range(NB):
                    sp.dma_start(vc[:, b], A["cache_v"][bass.ds(i * NB + b, 1)].rearrange("a (k p) h c -> p (a k) h c", p=P))\
                        .then_inc(v_ready, 16)
                    sp.dma_start(vn[:, b], A["o_v"][bass.ds(i * (NB * DEC_S) + SEQ + b * DEC_S, DEC_S)]).then_inc(v_ready, 16)

        @block.gpsimd
        def _(pool):
            begin(pool, q_ok)
            with pool.Fori(0, STEPS) as i:
                pool.wait_ge(st_ps, i * (NB * (KC + 1)) + ONE)
                for b in range(NB):
                    pool.wait_ge(q_ok, i * (2 * NB) + 2 * b + ONE)
                    t0 = i * (NB * DEC_S) + b * DEC_S
                    pool.tensor_copy(qb[:, b], H.qs[:, :, :, bass.ds(t0, DEC_S)]).then_inc(q_ok, 1)
                    pool.wait_ge(q_ok, i * (2 * NB) + 2 * b + 1 + ONE)
                    pool.tensor_copy(kT[:, b, :, PAST:], H.ks[:, :, bass.ds(t0, DEC_S)]).then_inc(q_ok, 1)

        @block.tensor
        def _(pe):
            begin(pe, kt_ps, st_ps, s_ps, pt_ps, o_ps)
            with pe.Fori(0, STEPS) as i:
                pe.wait_ge(k_ready, i * (16 * NB) + 16 * NB + ONE)
                n = 0
                for b in range(NB):
                    for h in range(0, HEADS, 2):
                        pe.wait_ge(kt_out, (i * KB + n - 1 if n >= 2 else i * KB) + ONE)
                        for q in range(4):
                            mm = pe.transpose(bk[n % 2][:, q, :], kc[:, b, q % 2, h + q // 2, :], G.ident[:, :])
                        mm.then_inc(kt_ps, 1)
                        n += 1
                pe.wait_ge(kt_out, i * KB + KB + ONE)
                pe.wait_ge(q_ok, i * (2 * NB) + 2 * NB + ONE)
                n = 0
                for k in range(KC + 1):
                    kw = P if k < KC else DEC_S
                    for b in range(NB):
                        pe.wait_ge(st_out, (i * (NB * (KC + 1)) + n - 1 if n >= 2 else i * (NB * (KC + 1))) + ONE)
                        for h in range(HEADS):
                            mm = pe.matmul(pst[n % 2][0:kw, h], kT[:, b, h, k * P:k * P + kw],
                                           qb[:, b, h], start=True, stop=True)
                        mm.then_inc(st_ps, 1)
                        n += 1
                pe.wait_ge(st_out, i * (NB * (KC + 1)) + n + ONE)
                pe.wait_ge(masked, i * GROUPS + ONE)
                for g in range(GROUPS):
                    for k in range(KC + 1):
                        kw = P if k < KC else DEC_S
                        mm = pe.transpose(psc[:, g, k * P:k * P + kw],
                                          sT[0:kw, k, g].rearrange("p b h n -> p (b h n)"), G.ident[0:kw, 0:kw])
                    mm.then_inc(s_ps, 1)
                pe.wait_ge(norm_ok, i + 1 + ONE)
                pe.wait_ge(o_out, i + ONE)
                for k in range(KC + 1):
                    kw = P if k < KC else DEC_S
                    mm = pe.transpose(px[0:kw, k * P:(k + 1) * P], pr[:, 0, k * P:k * P + kw], G.ident[:, :])
                mm.then_inc(pt_ps, 1)
                pe.wait_ge(pt_out, i + 1 + ONE)
                pe.wait_ge(v_ready, i * (32 * NB) + 32 * NB + ONE)
                for b in range(NB):
                    for h in range(HEADS):
                        q0 = (b * HEADS + h) * DEC_S
                        for k in range(KC + 1):
                            kw = P if k < KC else DEC_S
                            v = vc[:, b, k, h, :] if k < KC else vn[:, b, h, :]
                            mm = pe.matmul(px[:, q0:q0 + DEC_S], v, pT[0:kw, k, q0:q0 + DEC_S],
                                           start=(k == 0), stop=(k == KC))
                mm.then_inc(o_ps, 1)

        @block.scalar
        def _(act):
            begin(act, kt_out, exp_ok)
            with act.Fori(0, STEPS) as i:
                for n in range(KB):
                    b, h = n // (HEADS // 2), n % (HEADS // 2) * 2
                    act.wait_ge(kt_ps, i * KB + n + 1 + ONE)
                    if n == 0:
                        act.wait_ge(st_ps, i * (NB * (KC + 1)) + ONE)
                    act.activation(kT[:, b, h:h + 2, 0:PAST].rearrange("p h (k c) -> p h k c", c=P),
                                   bk[n % 2][:, :, :].rearrange("p (h k) c -> p h k c", k=KC), ACT.Copy).then_inc(kt_out, 1)
                act.wait_ge(masked, i * GROUPS + GROUPS + 0 + ONE)
                act.wait_ge(chain, i * LINKS + 1 + ONE)
                act.wait_ge(norm_ok, i + ONE)
                act.activation(pr[:, :, :].rearrange("p g k -> p (g k)"), sc[:, :, :].rearrange("p g k -> p (g k)"),
                               ACT.Exp, bias=stat[:, 3:4], scale=-1.0, accum_out=stat[:, 4:5]).then_inc(exp_ok, 1)

        @block.vector
        def _(dve):
            begin(dve, st_out, masked, norm_ok, pt_out, o_out, chain)
            dve.wait_ge(mask_ready, 16 + ONE)
            with dve.Fori(0, STEPS) as i:
                link = Chain(dve, chain, i * LINKS)
                n = 0
                for k in range(KC + 1):
                    kw = P if k < KC else DEC_S
                    for b in range(NB):
                        dve.wait_ge(st_ps, i * (NB * (KC + 1)) + n + 1 + ONE)
                        dve.tensor_copy(sT[0:kw, k, :, b], pst[n % 2][0:kw].rearrange("p h g n -> p g h n"))\
                            .then_inc(st_out, 1)
                        n += 1
                for g in range(GROUPS):
                    dve.wait_ge(s_ps, i * GROUPS + g + 1 + ONE)
                    if g == 0:
                        dve.wait_ge(exp_ok, i + ONE)
                    dve.sem_inc(passed, 1)
                    dve.tensor_tensor_reduce(out=sc[:, g, :], in0=psc[:, g, 0:NK], in1=mask[:, g, :], scale=-SCALE,
                                             scalar=3.0e38, op0=ALU.add, op1=ALU.min,
                                             accum_out=stat[:, g:g + 1]).then_inc(masked, 1)
                dve.wait_ge(masked, i * GROUPS + GROUPS + ONE)
                link(dve.tensor_reduce(stat[:, 3:4], stat[:, 0:3], AX.X, ALU.min))
                dve.wait_ge(exp_ok, i + 1 + ONE)
                link(dve.reciprocal(stat[:, 5:6], stat[:, 4:5]))
                link(dve.tensor_tensor(pr[:, 0, :], pr[:, 0, :], pr[:, 1, :], ALU.add))
                link(dve.tensor_tensor(pr[:, 0, :], pr[:, 0, :], pr[:, 2, :], ALU.add))
                dve.tensor_scalar(pr[:, 0, :], pr[:, 0, :], stat[:, 5:6], None, ALU.mult).then_inc(norm_ok, 1)
                dve.wait_ge(pt_ps, i + 1 + ONE)
                dve.wait_ge(o_ps, i + ONE)
                dve.tensor_copy(pT[:, 0:KC, :], px[:, 0:KC * P].rearrange("p (k c) -> p k c", c=P))
                dve.tensor_copy(pT[0:DEC_S, KC, :], px[0:DEC_S, KC * P:(KC + 1) * P]).then_inc(pt_out, 1)
                dve.wait_ge(o_ps, i + 1 + ONE)
                for b in range(NB):
                    last = dve.tensor_copy(H.oT[:, :, bass.ds(i * (NB * DEC_S) + b * DEC_S, DEC_S)],
                                           px[:, b * HEADS * DEC_S:(b + 1) * HEADS * DEC_S].rearrange("p (h n) -> p h n", n=DEC_S))
                last.then_inc(o_out, 1)
                link(dve.memset(stat[:, 6:7], 0.0))
                assert link.n == LINKS
    c.close()


def stage_merge(nc, G, A, H):
    S = G.sem
    og_ready = [S(f"mg_og_ready{u}") for u in range(2)]
    w_ready, diff_ok, exp_ok, chain, rows_ok, tr_ok, ot_ok, prod, added, sq = (S("mg_" + n) for n in (
        "w_ready", "diff", "exp", "chain", "rows", "transposed", "ot", "product", "added", "squares"))
    c = Ctx(nc, "mg_")
    wo = c.sb("wo", [P, HEADS, D])
    og = c.sb("og", [P, 2, GROUPS, HEADS, HD + 2])
    df = c.sb("df", [P, 2, GROUPS, HEADS])
    ex = c.sb("ex", [P, 2, GROUPS, HEADS])
    den = c.sb("den", [P, 2, 3, HEADS])
    orow = c.sb("orow", [P, 2, HEADS, HD])
    term = c.sb("term", [P, HEADS, HD])
    oT = c.sb("oT", [P, 2, HEADS, P])
    junk = c.sb("junk", [P, D])
    tp = c.ps("tp", [P, HEADS, P])
    py = [c.ps(f"py{u}", [P, 2, 512]) for u in range(2)]
    LINKS = 11

    with nc.Block() as block:
        @block.sync
        def _(sp):
            begin(sp, og_ready, w_ready)
            def load(t, u):
                for g in range(GROUPS):
                    sp.dma_start(og[:, u, g], A["s_og"][g, bass.ds(t * P, P)]).then_inc(og_ready[u], 16)

            for u in range(2):
                load(u, u)
            sp.dma_start(wo[:, :, :], A["attn_w_o"].rearrange("a (h p) n -> p (a h) n", p=P)).then_inc(w_ready, 16)
            with sp.Fori(0, QT // 2 - 1) as i:
                for u in range(2):
                    sp.wait_ge(rows_ok, i * 2 + u + 1 + ONE)
                    load(i * 2 + u + 2, u)

        @block.vector
        def _(dve):
            begin(dve, added, diff_ok, rows_ok, ot_ok, chain)
            def finish(t, u, n):
                dve.wait_ge(prod, t + 1 + ONE)
                row = G.h[0:n, bass.ds(t, 1), :].rearrange("p a d -> p (a d)")
                dve.tensor_tensor(row, py[u][0:n].rearrange("p a n -> p (a n)"), row, ALU.add).then_inc(added, 1)

            with dve.Fori(0, QT // 2) as i:
                for u in range(2):
                    t = i * 2 + u
                    link = Chain(dve, chain, t * LINKS)
                    nmax = og[:, u, :, :, HD]
                    low, dn, rc = (den[:, u, n] for n in range(3))
                    dve.wait_ge(og_ready[u], i * 48 + 48 + ONE)
                    link(dve.tensor_tensor(low, nmax[:, 0], nmax[:, 1], ALU.min))
                    link(dve.tensor_tensor(low, low, nmax[:, 2], ALU.min))
                    dve.tensor_tensor(df[:, u], low.unsqueeze(1).to_broadcast([P, GROUPS, HEADS]), nmax,
                                      ALU.subtract).then_inc(diff_ok, 1)
                    dve.wait_ge(exp_ok, t + 1 + ONE)
                    link(dve.tensor_tensor(df[:, u], ex[:, u], og[:, u, :, :, HD + 1], ALU.mult))
                    link(dve.tensor_tensor(dn, df[:, u, 0], df[:, u, 1], ALU.add))
                    link(dve.tensor_tensor(dn, dn, df[:, u, 2], ALU.add))
                    link(dve.reciprocal(rc, dn))
                    link(dve.tensor_tensor(ex[:, u], ex[:, u], rc.unsqueeze(1).to_broadcast([P, GROUPS, HEADS]), ALU.mult))
                    dve.wait_ge(tr_ok, i * 2 + ONE)
                    for g in range(GROUPS):
                        w = ex[:, u, g].unsqueeze(2).to_broadcast([P, HEADS, HD])
                        if g == 0:
                            link(dve.tensor_tensor(orow[:, u], og[:, u, g, :, 0:HD], w, ALU.mult))
                        else:
                            link(dve.tensor_tensor(term[:, :, :], og[:, u, g, :, 0:HD], w, ALU.mult))
                            if g == 1:
                                link(dve.tensor_tensor(orow[:, u], orow[:, u], term[:, :, :], ALU.add))
                            else:
                                dve.tensor_tensor(orow[:, u], orow[:, u], term[:, :, :], ALU.add).then_inc(rows_ok, 1)
                    assert link.n == LINKS
                    dve.wait_ge(tr_ok, t + 1 + ONE)
                    dve.wait_ge(prod, i * 2 + ONE)
                    dve.tensor_copy(oT[:, u], tp[:, :, :]).then_inc(ot_ok, 1)
                for u in range(2):
                    finish(i * 2 + u, u, P)
            finish(QT, 0, NSMP)

        @block.tensor
        def _(pe):
            begin(pe, prod, tr_ok)
            def project(u, lhs, n):
                for half in range(2):
                    for k in range(HEADS):
                        mm = pe.matmul(py[u][0:n, half, :], lhs(k), wo[:, k, half * 512:(half + 1) * 512],
                                       start=(k == 0), stop=(k == HEADS - 1))
                mm.then_inc(prod, 1)

            with pe.Fori(0, QT // 2) as i:
                for u in range(2):
                    pe.wait_ge(rows_ok, i * 2 + u + 1 + ONE)
                    pe.wait_ge(ot_ok, i * 2 + u + ONE)
                    for k in range(HEADS):
                        mm = pe.transpose(tp[:, k, :], orow[:, u, k, :], G.ident[:, :])
                    mm.then_inc(tr_ok, 1)
                for u in range(2):
                    if u == 0:
                        pe.wait_ge(w_ready, 16 + ONE)
                    pe.wait_ge(ot_ok, i * 2 + u + 1 + ONE)
                    pe.wait_ge(added, i * 2 + ONE)
                    project(u, lambda k: oT[:, u, k, :], P)
            pe.wait_ge(added, QT + ONE)
            project(0, lambda k: H.oT[:, k, :], NSMP)

        @block.scalar
        def _(act):
            begin(act, sq, exp_ok)
            def square(t):
                act.wait_ge(added, t + 1 + ONE)
                act.wait_ge(sq, t + ONE)
                act.activation(junk[:, :], G.h[:, bass.ds(t, 1), :], ACT.Square,
                               accum_out=G.ssq[:, bass.ds(t, 1)]).then_inc(sq, 1)

            with act.Fori(0, QT // 2) as i:
                for u in range(2):
                    act.wait_ge(diff_ok, i * 2 + u + 1 + ONE)
                    act.activation(ex[:, u], df[:, u], ACT.Exp).then_inc(exp_ok, 1)
                for u in range(2):
                    square(i * 2 + u)
            square(QT)
    c.close()


def stage_out(nc, G, A):
    S = G.sem
    var_ok, root_ok, rstd_ok, rows_ok, out_ok, g_ready = (S("fn_" + n) for n in ("var", "root", "rstd", "rows", "out", "gain"))
    stored = [S(f"fn_stored{u}") for u in range(3)]
    c = Ctx(nc, "fn_")
    st = c.sb("stats", [P, 3, TILES])
    g = c.sb("gain", [P, D])
    rows = c.sb("rows", [P, 3, D])
    with nc.Block() as block:
        @block.sync
        def _(sp):
            begin(sp, g_ready, stored)
            sp.dma_start(g[:, :], A["norm_final"].partition_broadcast(P)).then_inc(g_ready, 16)
            with sp.Fori(0, QT // 2) as i:
                for u in range(2):
                    sp.wait_ge(out_ok, i * 2 + u + 1 + ONE)
                    sp.dma_start(A["o_y"][bass.ds((i * 2 + u) * P, P), :], rows[:, u, :]).then_inc(stored[u], 16)
            sp.wait_ge(out_ok, TILES + ONE)
            sp.dma_start(A["o_y"][SEQ:, :], rows[0:NSMP, 2, :]).then_inc(stored[2], 16)
            sp.wait_ge(stored[0], 16 * (QT // 2) + ONE)
            sp.wait_ge(stored[1], 16 * (QT // 2) + ONE)
            sp.wait_ge(stored[2], 16 + ONE)

        @block.scalar
        def _(act):
            begin(act, root_ok)
            act.wait_ge(var_ok, 1 + ONE)
            act.activation(st[:, 1, :], st[:, 0, :], ACT.Sqrt).then_inc(root_ok, 1)

        @block.vector
        def _(dve):
            begin(dve, var_ok, rstd_ok, rows_ok, out_ok)
            dve.tensor_scalar(st[:, 0, :], G.ssq[:, :], 1.0 / D, EPS, ALU.mult, ALU.add).then_inc(var_ok, 1)
            dve.wait_ge(root_ok, 1 + ONE)
            dve.reciprocal(st[:, 2, :], st[:, 1, :]).then_inc(rstd_ok, 1)
            dve.wait_ge(rstd_ok, 1 + ONE)
            dve.wait_ge(g_ready, 16 + ONE)

            def row(t, u):
                dve.tensor_scalar(rows[:, u, :], G.h[:, bass.ds(t, 1), :].rearrange("p a d -> p (a d)"),
                                  st[:, 2, bass.ds(t, 1)], None, ALU.mult).then_inc(rows_ok, 1)
                dve.wait_ge(rows_ok, t + 1 + ONE)
                dve.tensor_tensor(rows[:, u, :], rows[:, u, :], g[:, :], ALU.mult).then_inc(out_ok, 1)

            with dve.Fori(0, QT // 2) as i:
                for u in range(2):
                    dve.wait_ge(stored[u], i * 16 + ONE)
                    row(i * 2 + u, u)
            row(QT, 2)
    c.close()


def layer_attention(nc, G, A):
    H = Ctx(nc, "la_")
    H.qs = H.sb("qs", [P, HEADS, GROUPS, NSMP])
    H.ks = H.sb("ks", [P, HEADS, NSMP])
    H.oT = H.sb("oT", [P, HEADS, NSMP])
    cx = Ctx(nc, "lb_")
    xT = cx.sb("xT", [P, DK, NPAD])
    stage_norm(nc, G, "n1", None, xT)
    stage_heads(nc, G, A, xT, H)
    cx.close()
    stage_sample(nc, G, A, H)
    stage_merge(nc, G, A, H)
    H.close()
def build(nc, A):
    G = Ctx(nc)
    sems = []

    def new_sem(name):
        sems.append(nc.alloc_semaphore(name))
        return sems[-1]

    def clear_sems():
        nc.clear_and_free_semaphores(sems)
        nc.all_engine_barrier()
        sems.clear()

    G.sem = new_sem
    G.h = G.sb("h", [P, TILES, D])
    G.ssq = G.sb("ssq", [P, TILES])
    G.ident = G.sb("ident", [P, P])
    G.upper = G.sb("upper", [P, P])
    G.ones = G.sb("ones", [P, P])
    G.iota = G.sb("iota", [P, IOTA_COLS])
    G.gcol = G.sb("gcol", [P, N_GAINS, DK])
    stage_load(nc, G, A)
    layer_conv(nc, G, A)
    layer_moe(nc, G, A, 0, GAIN_FFN0)
    clear_sems()
    layer_attention(nc, G, A)
    layer_moe(nc, G, A, 1, GAIN_FFN1)
    stage_out(nc, G, A)
    clear_sems()
    G.close()


def layer_conv(nc, G, A):
    c = Ctx(nc, "lc_")
    w_out = c.sb("w_out", [P, DK, D])
    zT = c.sb("zT", [P, DK, NPAD])
    cx = Ctx(nc, "lx_")
    xT = cx.sb("xT", [P, DK, NPAD])
    stage_norm(nc, G, "n0", GAIN_MIX0, xT)
    stage_conv(nc, G, A, xT, zT, w_out)
    cx.close()
    stage_project(nc, G, "po", zT, w_out)
    c.close()



IOTA_COLS = P + 2 * TILES + EG
N_GAINS = 5
GAIN_MIX0, GAIN_FFN0, GAIN_MIX1, GAIN_FFN1, GAIN_KV = range(5)


def _col(a, np):
    b = a.reshape(a.shape[:-1] + (DK, P))
    return np.ascontiguousarray(np.moveaxis(b, -1, 0))


def _constants(np):
    f = np.float32
    half = HD // 2
    inv = np.power(f(10000.0), -np.arange(half, dtype=f) / f(half)).astype(f)
    pos = np.concatenate([np.arange(SEQ), PAST + np.tile(np.arange(DEC_S), DEC_B)]).astype(f)
    ang = (inv[:, None] * pos[None, :]).astype(f)
    q, k = np.arange(P)[:, None], np.arange(2 * P)[None, :]
    rel = q + P - k
    band = np.where((rel >= 0) & (rel <= WINDOW_KEYS), 0.0, NEG)
    n = np.arange(P)
    back = n[:, None] - n[None, :]
    pair = np.where((back >= 0) & (back % 2 == 0), 0.0, NEG)
    qn = np.arange(P) % DEC_S
    j = np.arange(PAST + DEC_S)
    smp = []
    for dil in (1, 4, 16):
        dist = PAST + qn[:, None] - j[None, :]
        smp.append(np.where((dist >= 0) & (dist % dil == 0) & (dist // dil <= WINDOW_KEYS), 0.0, NEG))
    tok = np.arange(TILES)[None, :] * P + np.arange(P)[:, None]
    return {
        "c_ident": np.eye(P, dtype=f),
        "c_upper": (np.arange(P)[:, None] < np.arange(P)[None, :]).astype(f),
        "c_iota": np.concatenate([np.tile(np.arange(P), (P, 1)), tok, np.tile(np.arange(EG, 0, -1), (P, 1)),
                                  np.tile(np.arange(TILES) * P, (P, 1))], axis=1).astype(f),
        "c_cos": np.concatenate([np.cos(ang)] * 2).astype(f),
        "c_sin": np.concatenate([np.sin(ang), -np.sin(ang)]).astype(f),
        "c_band": band.astype(f),
        "c_pair": pair.astype(f),
        "c_smp": np.stack(smp, axis=1).astype(f),
    }


_OUTS = {
    "o_y": (NTOK, D), "o_kT": (HEADS, HD, NTOK), "o_v": (NTOK, HEADS, HD), "o_conv": (P, DK, (CONV - 1) * (1 + DEC_B)),
}
_PLAIN = ["x_prompt", "x_sample", "conv_w_out", "attn_w_o", "expert_w1", "expert_w3", "expert_w2", "cache_k", "cache_v",
          "norm_final", "router_group_b", "router_expert_b"]


def kernel(**inputs):
    import numpy as _np
    import concourse.bacc as _bacc
    from concourse import mybir as _mybir
    from concourse.bass_utils import run_bass_kernel_spmd as _run

    x = {k: _np.asarray(v) for k, v in inputs.items()}
    arrays = {k: _np.ascontiguousarray(x[k]) for k in _PLAIN}
    arrays.update(_constants(_np))
    gains = _np.stack([x["norm_mix"][0], x["norm_ffn"][0], x["norm_mix"][1], x["norm_ffn"][1], x["norm_kv"]])
    arrays["gains_col"] = _col(gains, _np)
    arrays["conv_kernel_col"] = _np.ascontiguousarray(_col(x["conv_kernel"][0], _np).transpose(0, 2, 1))
    arrays["state_col"] = _np.ascontiguousarray(_col(x["state_conv"][0], _np).transpose(0, 3, 1, 2))
    w = x["conv_w_in"][0].reshape(DK, P, 3, DK, P)
    arrays["conv_w_in_t"] = _np.ascontiguousarray(w.transpose(3, 1, 0, 2, 4))
    kv = x["attn_w_kv"].reshape(DK, P, 2, HEADS, HD)
    q = x["attn_w_q"][0].reshape(DK, P, GROUPS, HEADS, HD)
    arrays["w_heads"] = _np.ascontiguousarray(_np.concatenate([kv, q], axis=2).transpose(3, 2, 1, 0, 4))
    wr = _np.concatenate([x["router_group_w"], x["router_expert_w"]], axis=2).reshape(2, DK, P, ROUTE)
    arrays["router_w"] = _np.ascontiguousarray(wr.transpose(2, 0, 1, 3))

    nc = _bacc.Bacc("TRN2", target_bir_lowering=False, num_devices=1)
    A = {}
    for name, a in arrays.items():
        A[name] = nc.dram_tensor("in_" + name, a.shape, _mybir.dt.from_np(a.dtype), kind="ExternalInput").ap()
    for name, shape in _OUTS.items():
        A[name] = nc.dram_tensor("out_" + name, shape, _mybir.dt.float32, kind="ExternalOutput").ap()
    A["s_rows"] = nc.dram_tensor("s_rows", (NPAD, D), _mybir.dt.float32).ap()
    A["s_ys"] = nc.dram_tensor("s_ys", (MBLK * P, D), _mybir.dt.float32).ap()
    A["s_og"] = nc.dram_tensor("s_og", (GROUPS, SEQ, HEADS, HD + 2), _mybir.dt.float32).ap()
    build(nc, A)
    r = _run(nc, [{"in_" + k: v for k, v in arrays.items()}], core_ids=[0]).results[0]
    y, kT, v, cv = (r["out_" + n] for n in ("o_y", "o_kT", "o_v", "o_conv"))
    k = kT.transpose(2, 0, 1)
    cv = _np.ascontiguousarray(cv.transpose(2, 1, 0)).reshape(1, 1 + DEC_B, CONV - 1, D)
    return (
        y[:SEQ].reshape(1, SEQ, D), y[SEQ:].reshape(DEC_B, DEC_S, D),
        _np.ascontiguousarray(k[:SEQ]).reshape(1, SEQ, HEADS, HD), v[:SEQ].reshape(1, SEQ, HEADS, HD),
        cv[:, :1], _np.ascontiguousarray(k[SEQ:]).reshape(DEC_B, DEC_S, HEADS, HD),
        v[SEQ:].reshape(DEC_B, DEC_S, HEADS, HD), cv[:, 1:],
    )
```

```python
import math
from contextlib import ExitStack

import numpy as np
import concourse.bass as bass
from concourse import mybir

F32 = mybir.dt.float32
F32R = mybir.dt.float32r
I32 = mybir.dt.int32
ALU = mybir.AluOpType
ACT = mybir.ActivationFunctionType
AX = mybir.AxisListType

D = 1024
SEQ = 1024
DEC_B, DEC_S = 8, 8
NSMP = DEC_B * DEC_S
NTOK = SEQ + NSMP
P = 128
TILES = (NTOK + P - 1) // P
NPAD = TILES * P
DK = D // P
PAST = 256
WINDOW_KEYS = 128
GROUPS = 3
HEADS = 8
HD = 128
NE = 16
EG = 4
DE = 512
EPS = 1e-6
NEG = -1e30
SCALE = HD ** -0.5
CONV = 3
MBLK = (2 * NTOK + NE * (P - 1)) // P
CHUNKS = [(0, 384), (384, 384), (768, NTOK - 768)]
C2P = SEQ - 768
UW = SEQ + CONV - 1
US = DEC_S + CONV - 1
ROUTE = EG + NE
ONE = 1


def begin(eng, *sems):
    for s in sems:
        for one in s if isinstance(s, list) else [s]:
            eng.sem_inc(one, ONE)


class Chain:

    def __init__(self, eng, sem, base=0):
        self.eng, self.sem, self.base, self.n = eng, sem, base, 0

    def __call__(self, ins):
        self.n += 1
        ins.then_inc(self.sem, 1)
        self.eng.wait_ge(self.sem, self.base + self.n + ONE)


class Ctx:

    def __init__(self, nc, tag=""):
        self.nc, self.stack, self.tag = nc, ExitStack(), tag

    def sb(self, name, shape, dt=F32):
        return self.stack.enter_context(self.nc.sbuf_tensor(self.tag + name, shape, dt))

    def ps(self, name, shape, dt=F32):
        return self.stack.enter_context(self.nc.psum_tensor(self.tag + name, shape, dt))

    def close(self):
        self.stack.close()


def stage_load(nc, G, A, W):
    S = G.sem
    zeroed, squares, c_ready, w_ready = (S("ld_" + n) for n in ("zeroed", "squares", "const", "w_ready"))
    x_ready = [S(f"ld_x{u}") for u in range(TILES // 3)]
    c = Ctx(nc, "ld_")
    junk = c.sb("junk", [P, 2, D])
    raw = W.first
    with nc.Block() as block:
        @block.sync
        def _(sp):
            begin(sp, x_ready, w_ready)
            x = A["x_prompt"].rearrange("b (t p) d -> p (b t) d", p=P)
            for u in range(TILES // 3):
                full = min(u * 3 + 3, QT)
                sp.dma_start(G.h[:, u * 3:full, :], x[:, u * 3:full, :]).then_inc(x_ready[u], 16)
            sp.dma_start(G.h[0:NSMP, QT, :], A["x_sample"].rearrange("b s d -> (b s) d")).then_inc(x_ready[-1], 16)
            sp.dma_start(raw, A["conv_w_in_t"][0]).then_inc(w_ready, 16)
            sp.wait_ge(c_ready, 16 * 2 + ONE)

        @block.gpsimd
        def _(pool):
            begin(pool, zeroed)
            pool.memset(G.h[NSMP:P, QT, :], 0.0).then_inc(zeroed, 1)
            pool.wait_ge(c_ready, 16 * 2 + ONE)
            pool.wait_ge(w_ready, 16 + ONE)
            pool.wait_ge(zeroed, 1 + ONE)
            g = G.gcol[:, GAIN_MIX0, :].unsqueeze(2).to_broadcast([P, DK, 3 * P])
            flat = raw.rearrange("p k c n -> p k (c n)")
            pool.tensor_tensor(flat, flat, g, ALU.mult)

        @block.scalar
        def _(act):
            begin(act, c_ready, squares)
            act.dma_start(G.ident[:, :], A["c_ident"]).then_inc(c_ready, 16)
            act.dma_start(G.gcol[:, :, :], A["gains_col"]).then_inc(c_ready, 16)
            for t in range(TILES):
                if t % 3 == 0:
                    act.wait_ge(x_ready[t // 3], (16 if t < TILES - 3 else 32) + ONE)
                if t == QT:
                    act.wait_ge(zeroed, 1 + ONE)
                if t >= 2:
                    act.wait_ge(squares, t - 1 + ONE)
                act.activation(junk[:, t % 2, :], G.h[:, t, :], ACT.Square,
                               accum_out=G.ssq[:, t:t + 1]).then_inc(squares, 1)
    c.close()


def stage_norm(nc, G, tag, xh, xl, keep=None, W=None):
    S = G.sem
    var_ok, root_ok, rstd_ok, rows_ok, tr_ok, high_ok, low_ok, kept = (
        S(f"{tag}_{n}") for n in ("var", "root", "rstd", "rows", "transposed", "high", "low", "kept"))
    w_high = S(f"{tag}_w_high")
    c = Ctx(nc, tag + "_")
    st = c.sb("stats", [P, 3, TILES])
    rows = c.sb("rows", [P, 3, D])
    tp = [c.ps(f"tp{u}", [P, DK, P]) for u in range(3)]
    with nc.Block() as block:
        if keep is not None:
            @block.sync
            def _(sp):
                begin(sp, kept)
                sp.dma_start(keep.rearrange("(t p) d -> p t d", p=P), G.h[:, :, :]).then_inc(kept, 16)
                sp.wait_ge(kept, 16 + ONE)

        if W is not None:
            @block.gpsimd
            def _(pool):
                pool.wait_ge(w_high, 1 + ONE)
                pool.tensor_tensor(W.wl[:, 0], W.first, W.wh[:, 0].bitcast(F32), ALU.subtract)

        @block.scalar
        def _(act):
            begin(act, root_ok, high_ok, w_high)
            act.wait_ge(var_ok, 1 + ONE)
            act.activation(st[:, 1, :], st[:, 0, :], ACT.Sqrt).then_inc(root_ok, 1)

            def high_part(t, u):
                act.wait_ge(tr_ok, t + 1 + ONE)
                act.activation(xh[:, :, bass.ds(t * P, P)], tp[u][:, :, :], ACT.Copy).then_inc(high_ok, 1)

            for u in range(3):
                high_part(u, u)
            if W is not None:
                act.activation(W.wh[:, 0], W.first, ACT.Copy).then_inc(w_high, 1)
            with act.Fori(0, TILES // 3 - 1) as i:
                for u in range(3):
                    high_part(i * 3 + u + 3, u)

        @block.vector
        def _(dve):
            begin(dve, var_ok, rstd_ok, rows_ok, low_ok)
            dve.tensor_scalar(st[:, 0, :], G.ssq[:, :], 1.0 / D, EPS, ALU.mult, ALU.add).then_inc(var_ok, 1)
            dve.wait_ge(root_ok, 1 + ONE)
            dve.reciprocal(st[:, 2, :], st[:, 1, :]).then_inc(rstd_ok, 1)
            dve.wait_ge(rstd_ok, 1 + ONE)

            def scale_rows(t, u):
                dve.tensor_scalar(rows[:, u, :], G.h[:, bass.ds(t, 1), :], st[:, 2, bass.ds(t, 1)], None,
                                  ALU.mult).then_inc(rows_ok, 1)

            def low_part(t, u):
                dve.wait_ge(high_ok, t + 1 + ONE)
                at = bass.ds(t * P, P)
                dve.tensor_tensor(xl[:, :, at], tp[u][:, :, :], xh[:, :, at].bitcast(F32), ALU.subtract).then_inc(low_ok, 1)

            for u in range(3):
                scale_rows(u, u)
            with dve.Fori(0, TILES // 3 - 1) as i:
                for u in range(3):
                    dve.wait_ge(tr_ok, i * 3 + u + 1 + ONE)
                    scale_rows(i * 3 + u + 3, u)
                    low_part(i * 3 + u, u)
            for t in range(TILES - 3, TILES):
                low_part(t, t % 3)

        @block.tensor
        def _(pe):
            begin(pe, tr_ok)

            def transposes(t, u):
                pe.wait_ge(rows_ok, t + 1 + ONE)
                for k in range(DK):
                    mm = pe.transpose(tp[u][:, k, :], rows[:, u, k * P:(k + 1) * P], G.ident[:, :])
                mm.then_inc(tr_ok, 1)

            for u in range(3):
                transposes(u, u)
            with pe.Fori(0, TILES // 3 - 1) as i:
                for u in range(3):
                    pe.wait_ge(low_ok, i * 3 + u + 1 + ONE)
                    transposes(i * 3 + u + 3, u)
    c.close()


def stage_conv(nc, G, A, xh, xl, W, zT, w_out):
    S = G.sem
    w_ready = [S(f"cv_w_ready{u}") for u in range(2)]
    cb_ok, u_ok = ([S(f"cv_{n}{v}") for v in range(2)] for n in ("copied", "gated"))
    small_ready, scaled, high_ok, low_ok, prod_ok, chain, last_ok, stored, zero_ok, z_ok = (S("cv_" + n) for n in (
        "small_ready", "w_scaled", "w_high", "w_low", "product", "chain", "last", "stored", "zeroed", "z"))
    c = Ctx(nc, "cv_")
    flat_h = G.h[:, :, :].rearrange("p t d -> p (t d)")
    SLICE = DK * 3 * P
    UB = UW + DEC_B * US
    assert 2 * (SLICE + UB) <= TILES * D
    raw = [flat_h[:, u * SLICE:(u + 1) * SLICE].rearrange("p (k c n) -> p k c n", k=DK, c=3) for u in range(2)]
    ub = flat_h[:, 2 * SLICE:2 * (SLICE + UB)].rearrange("p (u n) -> p u n", u=2)
    wh, wl = W.wh, W.wl
    kc = c.sb("kc", [P, DK, CONV])
    hist = c.sb("hist", [P, DK, DEC_B, CONV - 1])
    csb = c.sb("csb", [P, 2, 384])
    acc = c.sb("acc", [P, NTOK])
    last = c.sb("last", [P, DK, (CONV - 1) * (1 + DEC_B)])
    pp = [[c.ps(f"pp{part}{v}", [P, 512]) for v in range(2)] for part in range(3)]
    NC = len(CHUNKS)

    def hist_view(u):
        return ub[:, u, UW:].rearrange("p (b s) -> p b s", s=US)

    with nc.Block() as block:
        @block.sync
        def _(sp):
            begin(sp, small_ready, w_ready, stored, w_out.ready)

            def load(f, u):
                sp.dma_start(raw[u], A["conv_w_in_t"][bass.ds(f, 1)].rearrange("a p k c n -> p (a k) c n"))\
                    .then_inc(w_ready[u], 16)

            load(1, 1)
            sp.dma_start(kc[:, :, :], A["conv_kernel_col"]).then_inc(small_ready, 16)
            sp.dma_start(hist[:, :, :, :], A["state_col"]).then_inc(small_ready, 16)
            load(2, 0)
            with sp.Fori(0, DK // 2 - 2) as i:
                for u in (1, 0):
                    f = i * 2 + (1 if u else 2)
                    sp.wait_ge(low_ok, f + ONE)
                    load(f + 2, u)
            sp.wait_ge(low_ok, DK - 3 + ONE)
            load(DK - 1, 1)
            sp.wait_ge(low_ok, DK - 2 + ONE)
            n = w_out.early // 2
            for u in range(2):
                if u:
                    sp.wait_ge(low_ok, DK - 1 + ONE)
                sp.dma_start(w_out.raw[:, u * n:(u + 1) * n, :], w_out.dram[:, u * n:(u + 1) * n, :]).then_inc(w_out.ready, 16)
            sp.wait_ge(last_ok, DK + ONE)
            sp.dma_start(A["o_conv"], last[:, :, :]).then_inc(stored, 16)
            sp.wait_ge(stored, 16 + ONE)

        @block.gpsimd
        def _(pool):
            begin(pool, zero_ok, scaled, low_ok)
            pool.memset(ub[:, :, 0:CONV - 1], 0.0).then_inc(zero_ok, 1)
            pool.wait_ge(zero_ok, 1 + ONE)
            pool.memset(zT[:, :, NTOK:], 0.0).then_inc(zero_ok, 1)
            g = G.gcol[:, GAIN_MIX0, :].unsqueeze(2).to_broadcast([P, DK, 3 * P])

            def prepare(f, u, turn):
                flat = raw[u].rearrange("p k c n -> p k (c n)")
                pool.wait_ge(w_ready[u], turn * 16 + 16 + ONE)
                pool.wait_ge(low_ok, f - 1 + ONE)
                pool.tensor_tensor(flat, flat, g, ALU.mult).then_inc(scaled, 1)
                pool.wait_ge(high_ok, f + ONE)
                pool.tensor_tensor(wl[:, u], raw[u], wh[:, u].bitcast(F32), ALU.subtract).then_inc(low_ok, 1)

            pool.wait_ge(zero_ok, 2 + ONE)
            with pool.Fori(0, DK // 2 - 1) as i:
                prepare(i * 2 + 1, 1, i)
                prepare(i * 2 + 2, 0, i)
            prepare(DK - 1, 1, DK // 2 - 1)

        @block.tensor
        def _(pe):
            begin(pe, prod_ok)
            with pe.Fori(0, DK // 2) as i:
                for u in range(2):
                    pe.wait_ge(low_ok, i * 2 + u + ONE)
                    for n, (c0, cn) in enumerate(CHUNKS):
                        m = u * NC + n
                        pe.wait_ge(cb_ok[m % 2], i * NC + m // 2 + ONE)
                        pe.wait_ge(u_ok[m % 2], i * NC + m // 2 + ONE)
                        for part in range(3):
                            for k in range(DK):
                                for q, (w, x) in enumerate(((wh, xh), (wh, xl), (wl, xh))):
                                    mm = pe.matmul(pp[part][m % 2][:, 0:cn], w[:, u, k, part, :], x[:, k, c0:c0 + cn],
                                                   start=(k == 0 and q == 0), stop=(k == DK - 1 and q == 2))
                        mm.then_inc(prod_ok, 1)

        @block.scalar
        def _(act):
            begin(act, cb_ok, high_ok)

            def high_part(f, u):
                act.wait_ge(scaled, f + ONE)
                act.activation(wh[:, u], raw[u], ACT.Copy).then_inc(high_ok, 1)

            def copies(i, u, n, c0, cn):
                m = u * NC + n
                act.wait_ge(prod_ok, i * (2 * NC) + m + 1 + ONE)
                act.wait_ge(u_ok[m % 2], i * NC + m // 2 + ONE)
                act.activation(zT[:, bass.ds(i * 2 + u, 1), c0:c0 + cn].rearrange("p a n -> p (a n)"), pp[1][m % 2][:, 0:cn],
                               ACT.Copy)
                act.activation(csb[:, m % 2, 0:cn], pp[0][m % 2][:, 0:cn], ACT.Copy).then_inc(cb_ok[m % 2], 1)

            def tile(i, u):
                for n, (c0, cn) in enumerate(CHUNKS):
                    copies(i, u, n, c0, cn)

            high_part(1, 1)
            with act.Fori(0, DK // 2 - 1) as i:
                tile(i, 0)
                high_part(i * 2 + 2, 0)
                tile(i, 1)
                high_part(i * 2 + 3, 1)
            tile(DK // 2 - 1, 0)
            tile(DK // 2 - 1, 1)

        @block.vector
        def _(dve):
            begin(dve, u_ok, last_ok, z_ok, chain)
            dve.wait_ge(small_ready, 32 + ONE)
            dve.wait_ge(zero_ok, 2 + ONE)
            LINKS = 2 * CONV
            with dve.Fori(0, DK // 2) as i:
                for u in range(2):
                    f = i * 2 + u
                    link = Chain(dve, chain, f * LINKS)
                    dve.tensor_copy(hist_view(u)[:, :, 0:CONV - 1],
                                    hist[:, bass.ds(f, 1), :, :].rearrange("p a b s -> p (a b) s"))
                    for n, (c0, cn) in enumerate(CHUNKS):
                        m = u * NC + n
                        dve.wait_ge(cb_ok[m % 2], i * NC + m // 2 + 1 + ONE)
                        q, cs = pp[2][m % 2], csb[:, m % 2, :]
                        w = cn if n < NC - 1 else C2P
                        up = dve.tensor_tensor(ub[:, u, CONV - 1 + c0:CONV - 1 + c0 + w], q[:, 0:w], cs[:, 0:w], ALU.mult)
                        if n == NC - 1:
                            up = dve.tensor_tensor(hist_view(u)[:, :, CONV - 1:],
                                                   q[:, w:cn].rearrange("p (b s) -> p b s", s=DEC_S),
                                                   cs[:, w:cn].rearrange("p (b s) -> p b s", s=DEC_S), ALU.mult)
                        up.then_inc(u_ok[m % 2], 1)
                    dve.wait_ge(u_ok[m % 2], i * NC + m // 2 + 1 + ONE)
                    dve.tensor_copy(last[:, bass.ds(f, 1), 0:CONV - 1], ub[:, u, SEQ:UW])
                    dve.tensor_copy(last[:, bass.ds(f, 1), CONV - 1:].rearrange("p a (b s) -> p (a b) s", s=CONV - 1),
                                    hist_view(u)[:, :, DEC_S:]).then_inc(last_ok, 1)
                    for j in range(CONV):
                        k = kc[:, bass.ds(f, 1), j]
                        for src, dst in (
                            (ub[:, u, j:j + SEQ], acc[:, 0:SEQ]),
                            (hist_view(u)[:, :, j:j + DEC_S], acc[:, SEQ:].rearrange("p (b s) -> p b s", s=DEC_S)),
                        ):
                            if j == 0:
                                op = dve.tensor_scalar(dst, src, k, None, ALU.mult)
                            else:
                                op = dve.scalar_tensor_tensor(out=dst, in0=src, scalar=k, in1=dst,
                                                              op0=ALU.mult, op1=ALU.add)
                            link(op)
                    assert link.n == LINKS
                    z = zT[:, bass.ds(f, 1), 0:NTOK].rearrange("p a n -> p (a n)")
                    dve.tensor_tensor(z, acc[:, :], z, ALU.mult).then_inc(z_ok, 1)
    c.close()


def stage_project(nc, G, A, tag, zT, w):
    S = G.sem
    wl_ok = [S(f"{tag}_w_low_{who}") for who in ("vector", "pool")]
    rest, wh_ok, zh_ok, zl_ok, prod, added, sq, zeroed = (S(f"{tag}_{n}") for n in (
        "rest", "w_high", "z_high", "z_low", "product", "added", "squares", "zeroed"))
    x_ready = S(f"{tag}_x_ready")
    c = Ctx(nc, tag + "_")
    wh = c.sb("wh", [P, DK, D], F32R)
    wl = c.sb("wl", [P, DK, D], F32R)
    zh = c.sb("zh", [P, 3, DK, P], F32R)
    zl = c.sb("zl", [P, 3, DK, P], F32R)
    junk = c.sb("junk", [P, D])
    py = [c.ps(f"py{u}", [P, 2, 512]) for u in range(3)]
    with nc.Block() as block:
        @block.sync
        def _(sp):
            begin(sp, rest, x_ready)
            sp.dma_start(w.raw[:, w.early:, :], w.dram[:, w.early:, :]).then_inc(rest, 16)
            for who in range(2):
                sp.wait_ge(wl_ok[who], DK // 2 + ONE)
            sp.dma_start(G.h[:, 0:QT, :], A["x_prompt"].rearrange("b (t p) d -> p (b t) d", p=P)).then_inc(x_ready, 16)
            sp.dma_start(G.h[0:NSMP, QT, :], A["x_sample"].rearrange("b s d -> (b s) d")).then_inc(x_ready, 16)

        @block.gpsimd
        def _(pool):
            begin(pool, wl_ok[1], zeroed)
            for k in range(1, DK, 2):
                pool.wait_ge(wh_ok, k + 1 + ONE)
                pool.tensor_tensor(wl[:, k, :], w.raw[:, k, :], wh[:, k, :].bitcast(F32), ALU.subtract).then_inc(wl_ok[1], 1)
                pool.wait_ge(wl_ok[1], k // 2 + 1 + ONE)
            pool.memset(G.h[NSMP:P, QT, :], 0.0).then_inc(zeroed, 1)

        @block.tensor
        def _(pe):
            begin(pe, prod)

            def project(t, u):
                pe.wait_ge(zl_ok, t + 1 + ONE)
                for half in range(2):
                    cols = slice(half * 512, (half + 1) * 512)
                    for k in range(DK):
                        if half == 0:
                            pe.wait_ge(wl_ok[k % 2], k // 2 + 1 + ONE)
                        for q, (a, b) in enumerate(((zh, wh), (zl, wh), (zh, wl))):
                            mm = pe.matmul(py[u][:, half, :], a[:, u, k, :], b[:, k, cols],
                                           start=(k == 0 and q == 0), stop=(k == DK - 1 and q == 2))
                mm.then_inc(prod, 1)

            for u in range(3):
                project(u, u)
            with pe.Fori(0, TILES // 3 - 1) as i:
                for u in range(3):
                    pe.wait_ge(added, i * 3 + u + 1 + ONE)
                    project(i * 3 + u + 3, u)

        @block.vector
        def _(dve):
            begin(dve, added, zl_ok, wl_ok[0])

            def low_part(t, u):
                dve.wait_ge(zh_ok, t + 1 + ONE)
                dve.tensor_tensor(zl[:, u], zT[:, :, bass.ds(t * P, P)], zh[:, u].bitcast(F32), ALU.subtract).then_inc(zl_ok, 1)

            def finish(t, u):
                dve.wait_ge(prod, t + 1 + ONE)
                row = G.h[:, bass.ds(t, 1), :].rearrange("p a d -> p (a d)")
                dve.tensor_tensor(row, py[u][:, :, :].rearrange("p a n -> p (a n)"), row, ALU.add).then_inc(added, 1)

            low_part(0, 0)
            for k in range(0, DK, 2):
                dve.wait_ge(wh_ok, k + 1 + ONE)
                dve.tensor_tensor(wl[:, k, :], w.raw[:, k, :], wh[:, k, :].bitcast(F32), ALU.subtract).then_inc(wl_ok[0], 1)
            for u in range(1, 3):
                low_part(u, u)
            dve.wait_ge(x_ready, 32 + ONE)
            dve.wait_ge(zeroed, 1 + ONE)
            with dve.Fori(0, TILES // 3 - 1) as i:
                for u in range(3):
                    finish(i * 3 + u, u)
                    low_part(i * 3 + u + 3, u)
            for t in range(TILES - 3, TILES):
                finish(t, t % 3)

        @block.scalar
        def _(act):
            begin(act, wh_ok, zh_ok, sq)

            def high_part(t, u):
                act.activation(zh[:, u], zT[:, :, bass.ds(t * P, P)], ACT.Copy).then_inc(zh_ok, 1)

            def square(t):
                act.wait_ge(added, t + 1 + ONE)
                act.wait_ge(sq, t + ONE)
                act.activation(junk[:, :], G.h[:, bass.ds(t, 1), :], ACT.Square,
                               accum_out=G.ssq[:, bass.ds(t, 1)]).then_inc(sq, 1)

            high_part(0, 0)
            act.wait_ge(w.ready, 32 + ONE)
            for k in range(DK):
                if k == w.early:
                    act.wait_ge(rest, 16 + ONE)
                act.activation(wh[:, k, :], w.raw[:, k, :], ACT.Copy).then_inc(wh_ok, 1)
            for u in range(1, 3):
                high_part(u, u)
            with act.Fori(0, TILES // 3 - 1) as i:
                for u in range(3):
                    act.wait_ge(prod, i * 3 + u + 1 + ONE)
                    high_part(i * 3 + u + 3, u)
                    square(i * 3 + u)
            for t in range(TILES - 3, TILES):
                square(t)
    c.close()


def expert_weights(A, layer, m):
    return A[("expert_w1", "expert_w3", "expert_w2")[m]][layer].rearrange("e (k p) n -> e p k n", p=P)


def halves(m, half):
    n = (DK, DK, DE // P)[m] // 2
    return slice(half * n, (half + 1) * n)


def stage_route(nc, G, A, tag, layer, R):
    S = G.sem
    scaled, gain_ready = S(f"{tag}_scaled"), S(f"{tag}_gain_ready")
    (var_ok, root_ok, rstd_ok, rows_ok, tr_ok, xt_ok, small_ready, logit_ok, bias_ok, chain, exp_in, exp_ok, both_ok,
     count_ok, hot_ok, tok_ok) = (S(f"{tag}_{n}") for n in (
         "var", "root", "rstd", "rows", "transposed", "xt", "small_ready", "logits", "biased", "chain", "exp_in",
         "exp", "both", "counted", "one_hot", "slot_tok"))
    stored = [S(f"{tag}_stored{u}") for u in range(3)]
    piece = S(f"{tag}_w_low_half")
    c = Ctx(nc, tag + "_")
    st = c.sb("stats", [P, 3, TILES])
    rows = c.sb("rows", [P, 3, D])
    xt = c.sb("xt", [P, 3, DK, P])
    wr = c.sb("wr", [P, DK, ROUTE])
    bias = c.sb("bias", [P, ROUTE])
    gain = c.sb("gain", [P, D])
    lg = c.sb("logits", [P, TILES, ROUTE])
    tp = [c.ps(f"tp{u}", [P, DK, P]) for u in range(3)]
    pl = [c.ps(f"pl{u}", [P, 512]) for u in range(2)]

    T = TILES
    e4 = c.sb("e4", [P, 6, T, EG])
    group, pick1, pick2, l4, l4b, tmp4 = (e4[:, n] for n in range(6))
    col = c.sb("col", [P, 8, T])
    m, s, m1, m2, ge, gp, r, e2 = (col[:, n] for n in range(8))
    big = c.sb("big", [P, 5, T, NE])
    sel, hot1, hot2, both, slots = (big[:, n] for n in range(5))
    pre = c.sb("pre", [P, T + 1, NE])
    tot = c.sb("tot", [P, T, NE])
    exp_t = c.sb("exp_t", [P, 2, T, EG])
    ex = c.sb("ex", [P, 5, NE])
    nb, ends, base, one16, _spare = (ex[:, n] for n in range(5))
    cmp9 = c.sb("cmp9", [P, NE, T])
    cmpb = c.sb("cmpb", [P, MBLK + 1, NE])
    bef = c.sb("bef", [P, MBLK + 1])
    slotf = c.sb("slotf", [P, 2, T])
    part_i = c.sb("part_i", [P, 2, 2, T], I32)
    part_f = c.sb("part_f", [P, 2, 2, T])
    hr = c.sb("hr", [P, 2, P])
    hb = c.sb("hb", [P, 2, MBLK])
    upper = c.sb("upper", [P, P])
    ones = c.sb("ones", [P, P])
    iota = c.sb("iota", [P, IOTA_COLS])
    desc = iota[:, P + T:P + T + EG].unsqueeze(1).to_broadcast([P, T, EG])
    steps = iota[:, P + T + EG:P + 2 * T + EG].unsqueeze(1).to_broadcast([P, NE, T])

    def b4(x):
        return x.unsqueeze(2).to_broadcast([P, T, EG])

    with nc.Block() as block:
        @block.sync
        def _(sp):
            begin(sp, gain_ready, small_ready, stored, R.raw_ready)
            sp.dma_start(gain[:, :], A["norm_ffn"][layer, :].partition_broadcast(P)).then_inc(gain_ready, 16)
            sp.dma_start(wr[:, :, :], A["router_w"][:, layer]).then_inc(small_ready, 16)
            sp.dma_start(bias[:, 0:EG], A["router_group_b"][layer, :].partition_broadcast(P)).then_inc(small_ready, 16)
            sp.dma_start(bias[:, EG:], A["router_expert_b"][layer, :].partition_broadcast(P)).then_inc(small_ready, 16)
            sp.dma_start(upper[:, :], A["c_upper"]).then_inc(small_ready, 16)
            sp.dma_start(iota[:, :], A["c_iota"]).then_inc(small_ready, 16)
            with sp.Fori(0, T // 3) as i:
                for u in range(3):
                    sp.wait_ge(rows_ok, i * 3 + u + 1 + ONE)
                    sp.dma_start(A["s_rows"][bass.ds((i * 3 + u) * P, P), :], rows[:, u, :]).then_inc(stored[u], 16)
            for m in range(3):
                sp.dma_start(R.raw[m][:, :, :], expert_weights(A, layer, m)[0]).then_inc(R.raw_ready[m], 16)
            for u in range(3):
                sp.wait_ge(stored[u], 16 * (T // 3) + ONE)

        @block.scalar
        def _(act):
            begin(act, root_ok, exp_ok, xt_ok, R.hi_ok)
            act.wait_ge(var_ok, 1 + ONE)
            act.activation(st[:, 1, :], st[:, 0, :], ACT.Sqrt).then_inc(root_ok, 1)

            def copy_out(t, u):
                act.wait_ge(tr_ok, t + 1 + ONE)
                act.activation(xt[:, u], tp[u][:, :, :], ACT.Copy).then_inc(xt_ok, 1)

            for u in range(3):
                copy_out(u, u)
            with act.Fori(0, T // 3 - 1) as i:
                for u in range(3):
                    act.wait_ge(logit_ok, i * 3 + u + 1 + ONE)
                    copy_out(i * 3 + u + 3, u)
            def high(m):
                act.wait_ge(R.raw_ready[m], 16 + ONE)
                for half in range(2):
                    k = halves(m, half)
                    act.activation(R.wh[m][:, k, :], R.raw[m][:, k, :], ACT.Copy).then_inc(R.hi_ok[m], 1)

            high(0)
            act.wait_ge(exp_in, 1 + ONE)
            act.activation(exp_t[:, 1], exp_t[:, 0], ACT.Exp).then_inc(exp_ok, 1)
            act.wait_ge(exp_in, 2 + ONE)
            act.activation(e2, ge, ACT.Exp).then_inc(exp_ok, 1)
            high(1)

        @block.gpsimd
        def _(pool):
            begin(pool, R.lo_ok, piece)
            for m in range(2):
                for half in range(2):
                    k = halves(m, half)
                    pool.wait_ge(R.hi_ok[m], half + 1 + ONE)
                    op = pool.tensor_tensor(R.wl[m][:, k, :], R.raw[m][:, k, :], R.wh[m][:, k, :].bitcast(F32), ALU.subtract)
                    if half == 0:
                        op.then_inc(piece, 1)
                        pool.wait_ge(piece, m + 1 + ONE)
                    else:
                        op.then_inc(R.lo_ok[m], 1)
                        if m == 0:
                            pool.wait_ge(R.lo_ok[m], 1 + ONE)

        @block.tensor
        def _(pe):
            begin(pe, tr_ok, logit_ok, count_ok, tok_ok)
            pe.wait_ge(small_ready, 16 * 5 + ONE)

            def transposes(t, u):
                pe.wait_ge(rows_ok, t + 1 + ONE)
                for k in range(DK):
                    mm = pe.transpose(tp[u][:, k, :], rows[:, u, k * P:(k + 1) * P], G.ident[:, :])
                mm.then_inc(tr_ok, 1)

            def logits(t, u):
                pe.wait_ge(xt_ok, t + 1 + ONE)
                pe.wait_ge(bias_ok, t + ONE)
                for k in range(DK):
                    mm = pe.matmul(pl[0][:, 0:ROUTE], xt[:, u, k, :], wr[:, k, :], start=(k == 0), stop=(k == DK - 1))
                mm.then_inc(logit_ok, 1)

            transposes(0, 0)
            with pe.Fori(0, T // 3 - 1) as i:
                for u in range(3):
                    transposes(i * 3 + u + 1, (u + 1) % 3)
                    logits(i * 3 + u, u)
            for t in range(T - 3, T):
                if t + 1 < T:
                    transposes(t + 1, (t + 1) % 3)
                logits(t, t % 3)
            pe.wait_ge(both_ok, 1 + ONE)
            pe.matmul(pl[0][:, 0:T * NE], upper[:, :], both.rearrange("p t e -> p (t e)"), start=True, stop=True)
            pe.matmul(pl[1][:, 0:T * NE], ones[:, :], both.rearrange("p t e -> p (t e)"), start=True, stop=True)\
                .then_inc(count_ok, 1)
            n = 0
            for t in range(T):
                rows_in = P if t < T - 1 else NTOK - P * (T - 1)
                for k in range(2):
                    pe.wait_ge(hot_ok, n + 1 + ONE)
                    mm = pe.matmul(pl[1][:, 256:256 + MBLK], hr[0:rows_in, n % 2, :], hb[0:rows_in, n % 2, :],
                                   start=(n == 0), stop=(n == 2 * T - 1))
                    mm.then_inc(tok_ok, 1)
                    n += 1

        @block.vector
        def _(dve):
            dve.memset(ones[:, :], 1.0)
            begin(dve, var_ok, rstd_ok, rows_ok, scaled, bias_ok, exp_in, both_ok, hot_ok, chain)
            dve.tensor_scalar(st[:, 0, :], G.ssq[:, :], 1.0 / D, EPS, ALU.mult, ALU.add).then_inc(var_ok, 1)
            dve.wait_ge(root_ok, 1 + ONE)
            dve.reciprocal(st[:, 2, :], st[:, 1, :]).then_inc(rstd_ok, 1)
            dve.wait_ge(rstd_ok, 1 + ONE)
            def scale_rows(t, u):
                dve.tensor_scalar(rows[:, u, :], G.h[:, bass.ds(t, 1), :].rearrange("p a d -> p (a d)"),
                                  st[:, 2, bass.ds(t, 1)], None, ALU.mult).then_inc(scaled, 1)
                dve.wait_ge(scaled, t + 1 + ONE)
                dve.tensor_tensor(rows[:, u, :], rows[:, u, :], gain[:, :], ALU.mult).then_inc(rows_ok, 1)

            def add_bias(t):
                dve.wait_ge(logit_ok, t + 1 + ONE)
                dve.tensor_tensor(lg[:, bass.ds(t, 1), :].rearrange("p a n -> p (a n)"), pl[0][:, 0:ROUTE],
                                  bias[:, :], ALU.add).then_inc(bias_ok, 1)

            dve.wait_ge(gain_ready, 16 + ONE)
            for u in range(3):
                scale_rows(u, u)
            dve.wait_ge(small_ready, 16 * 5 + ONE)
            with dve.Fori(0, T // 3 - 1) as i:
                for u in range(3):
                    dve.wait_ge(tr_ok, i * 3 + u + 1 + ONE)
                    dve.wait_ge(stored[u], i * 16 + 16 + ONE)
                    scale_rows(i * 3 + u + 3, u)
                    add_bias(i * 3 + u)
            for t in range(T - 3, T):
                add_bias(t)
            dve.wait_ge(bias_ok, T + ONE)
            link = Chain(dve, chain)

            def tt(out, a, b, op):
                link(dve.tensor_tensor(out, a, b, op))

            def first_max(logits, top, hot):
                link(dve.tensor_reduce(top, logits, AX.X, ALU.max))
                tt(hot, logits, b4(top), ALU.is_equal)
                tt(hot, hot, desc, ALU.mult)
                link(dve.tensor_reduce(s, hot, AX.X, ALU.max))
                tt(hot, hot, b4(s), ALU.is_equal)

            grp = lg[:, :, 0:EG]
            first_max(grp, m, group)
            dve.tensor_tensor(exp_t[:, 0], grp, b4(m), ALU.subtract).then_inc(exp_in, 1)
            lexp = lg[:, :, EG:].rearrange("p t (g j) -> p t g j", j=EG)
            hot_g = group.unsqueeze(3).to_broadcast([P, T, EG, EG])
            sel4 = sel.rearrange("p t (g j) -> p t g j", j=EG)
            tt(sel4, lexp, hot_g, ALU.mult)
            link(dve.tensor_reduce(l4, sel4.rearrange("p t g j -> p t j g"), AX.X, ALU.add))
            first_max(l4, m1, pick1)
            link(dve.scalar_tensor_tensor(out=l4b, in0=pick1, scalar=NEG, in1=l4, op0=ALU.mult, op1=ALU.add))
            first_max(l4b, m2, pick2)
            dve.tensor_tensor(ge, m2, m1, ALU.subtract).then_inc(exp_in, 1)
            for hot, pick in ((hot1, pick1), (hot2, pick2)):
                tt(hot.rearrange("p t (g j) -> p t g j", j=EG), hot_g,
                   pick.unsqueeze(2).to_broadcast([P, T, EG, EG]), ALU.mult)
            tt(both, hot1, hot2, ALU.add)
            dve.memset(both[NTOK - P * (T - 1):, T - 1:T, :], 0.0).then_inc(both_ok, 1)
            dve.wait_ge(exp_ok, 2 + ONE)
            link(dve.tensor_reduce(s, exp_t[:, 1], AX.X, ALU.add))
            link(dve.reciprocal(gp, s))
            link(dve.tensor_scalar(r, e2, 1.0, None, ALU.add))
            link(dve.reciprocal(r, r))
            tt(R.gates[:, 0], gp, r, ALU.mult)
            tt(R.gates[:, 1], R.gates[:, 0], e2, ALU.mult)
            dve.wait_ge(count_ok, 1 + ONE)
            link(dve.tensor_copy(tot.rearrange("p t e -> p (t e)"), pl[1][:, 0:T * NE]))
            link(dve.memset(pre[:, 0], 0.0))
            for t in range(T):
                tt(pre[:, t + 1], pre[:, t], tot[:, t], ALU.add)
            tt(cmp9[:, :, :], pre[:, T].unsqueeze(2).to_broadcast([P, NE, T]), steps, ALU.is_gt)
            link(dve.tensor_reduce(nb, cmp9[:, :, :], AX.X, ALU.add))
            link(dve.tensor_scalar(nb, nb, 1.0, None, ALU.max))
            link(dve.memset(one16, 1.0))
            link(dve.tensor_tensor_scan(ends, one16, nb, 0.0, ALU.mult, ALU.add))
            tt(base, ends, nb, ALU.subtract)
            link(dve.tensor_scalar(base, base, float(P), None, ALU.mult))
            tt(slots, pl[0][:, 0:T * NE].rearrange("p (t e) -> p t e", e=NE), pre[:, 0:T], ALU.add)
            tt(slots, slots, base.unsqueeze(1).to_broadcast([P, T, NE]), ALU.add)
            for k, hot in enumerate((hot1, hot2)):
                tt(sel, slots, hot, ALU.mult)
                link(dve.tensor_reduce(slotf[:, k], sel, AX.X, ALU.add))
            link(dve.tensor_copy(R.slot[:, :, :], slotf[:, :, :]))
            link(dve.tensor_scalar(part_i[:, 0], R.slot[:, :, :], 7, None, ALU.logical_shift_right))
            link(dve.tensor_scalar(part_i[:, 1], R.slot[:, :, :], P - 1, None, ALU.bitwise_and))
            link(dve.tensor_copy(part_f.rearrange("p a k t -> p (a k t)"), part_i.rearrange("p a k t -> p (a k t)")))
            tt(cmpb[:, :, :], ends.unsqueeze(1).to_broadcast([P, MBLK + 1, NE]),
               iota[:, 0:MBLK + 1].unsqueeze(2).to_broadcast([P, MBLK + 1, NE]), ALU.is_le)
            link(dve.tensor_reduce(bef[:, :], cmpb[:, :, :], AX.X, ALU.add))
            link(dve.tensor_scalar(R.block_expert[:, :], bef[:, :], float(NE - 1), None, ALU.min))
            link(dve.tensor_scalar(R.last[:, :], ends[:, NE - 1:NE], -1.0, None, ALU.add))
            link(dve.memset(R.slot_tok[:, MBLK:], 0))
            n = 0
            for t in range(T):
                for k in range(2):
                    if n >= 2:
                        dve.wait_ge(tok_ok, n - 1 + ONE)
                    dve.tensor_scalar(hr[:, n % 2, :], iota[:, 0:P], part_f[:, 1, k, t:t + 1], None, ALU.is_equal)
                    dve.tensor_scalar(hb[:, n % 2, :], iota[:, 0:MBLK], part_f[:, 0, k, t:t + 1],
                                      iota[:, P + t:P + t + 1], ALU.is_equal, ALU.mult).then_inc(hot_ok, 1)
                    n += 1
            dve.wait_ge(tok_ok, 2 * T + ONE)
            link(dve.tensor_copy(R.slot_tok[:, 0:MBLK], pl[1][:, 256:256 + MBLK]))
    c.close()


def stage_experts(nc, G, A, tag, layer, R):
    S = G.sem
    hi_ok = R.hi_ok + [S(f"{tag}_w2_high")]
    lo_ok = R.lo_ok + [S(f"{tag}_w2_low")]
    xg_ok = S(f"{tag}_x_rows")
    (blank, zero_ok, passed, index_ok, gathered, xt_ps, xh_ok, xl_ok, a_ok, b_ok, silu_ok, hid_ok, hid_ps, hh_ok, hl_ok,
     y_ok, ys_ok, stored) = (S(f"{tag}_{n}") for n in (
         "blank", "zero", "passed", "index", "gathered", "x_transposed", "x_high", "x_low", "w1_product", "w3_product",
         "silu", "hidden", "hidden_transposed", "hidden_high", "hidden_low", "w2_product", "rows", "stored"))
    passed_end = S(f"{tag}_passed_end")
    c = Ctx(nc, tag + "_")
    HK = DE // P
    raw, raw_ready = R.raw, R.raw_ready
    wh = R.wh + [c.sb("wh_w2", [P, HK, D], F32R)]
    wl = R.wl + [c.sb("wl_w2", [P, HK, D], F32R)]
    zero = c.sb("zero", [P, 64])
    idx = c.sb("idx", [P, 1], I32)
    xn = c.sb("xn", [P, D])
    xg = c.sb("xg", [P, D])
    xh = c.sb("xh", [P, DK, P], F32R)
    xl = c.sb("xl", [P, DK, P], F32R)
    hid = c.sb("hid", [P, DE])
    hh = c.sb("hh", [P, HK, P], F32R)
    hl = c.sb("hl", [P, HK, P], F32R)
    ys = c.sb("ys", [P, D])
    tp = c.ps("tp", [P, DK, P])
    pa = c.ps("pa", [P, DE])
    pb = c.ps("pb", [P, DE])
    ph = c.ps("ph", [P, HK, P])
    py = c.ps("py", [P, 2, 512])

    def last_block(eng):
        return eng.value_load(R.last[0:1, 0:1], min_val=NE - 1, max_val=MBLK - 1)

    def expert_of(eng, b):
        return eng.value_load(R.block_expert[0:1, bass.ds(b, 1)], min_val=0, max_val=NE - 1)

    with nc.Block() as block:
        @block.sync
        def _(sp):
            begin(sp, blank)
            sp.wait_ge(zero_ok, 1 + ONE)
            last = last_block(sp)
            with sp.Fori(NE, MBLK) as b:
                sp.dma_start(A["s_ys"][bass.ds(b * P, P), :].rearrange("p (a d) -> p a d", d=64),
                             zero[:, :].unsqueeze(1).to_broadcast([P, D // 64, 64]), cond=(b > last)).then_inc(blank, 16)

            def load(m, e):
                sp.wait_ge(lo_ok[m], e + ONE)
                sp.dma_start(raw[m][:, :, :], expert_weights(A, layer, m)[bass.ds(e, 1)]
                             .rearrange("a p k n -> p (a k) n")).then_inc(raw_ready[m], 16)

            load(0, 1)
            load(1, 1)
            with sp.Fori(2, NE) as e:
                load(0, e)
                load(1, e)
                load(2, e - 1)
            load(2, NE - 1)
            sp.wait_ge(blank, 16 * (MBLK - NE) + ONE)

        @block.gpsimd
        def _(pool):
            begin(pool, index_ok, xg_ok)
            bound = pool.to_reg(NPAD - 1)

            def gather(b):
                pool.tensor_copy(idx[:, :], R.slot_tok[:, bass.ds(b, 1)]).then_inc(index_ok, 1)
                pool.wait_ge(index_ok, b + 1 + ONE)
                pool.sem_inc(passed, 1)
                pool.indirect_dma_start(out=xn[:, :], out_offset=None, in_=A["s_rows"][:, :],
                                        in_offset=bass.IndirectOffsetOnAxis(ap=idx[:, 0:1], axis=0),
                                        bounds_check=bound).then_inc(gathered, 16)

            gather(0)
            last = last_block(pool)
            with pool.Fori(0, MBLK + 1) as b:
                with pool.If(b <= last + 1):
                    pool.wait_ge(gathered, b * 16 + 16)
                    pool.wait_ge(xt_ps, b + ONE)
                    pool.sem_inc(passed, 1)
                    pool.tensor_copy(xg[:, :], xn[:, :]).then_inc(xg_ok, 1)
                    pool.wait_ge(xg_ok, b + 1 + ONE)
                    gather(b + 1)
            pool.wait_ge(gathered, last * 16 + 48)
            pool.sem_inc(passed, 1)

        @block.tensor
        def _(pe):
            begin(pe, xt_ps, a_ok, b_ok, hid_ps, y_ok)

            def product(out, lh, ll, m, k0, k1, cols):
                terms = [(k, a, b) for k in range(k0, k1) for a, b in ((lh, wh), (lh, wl), (ll, wh))]
                for n, (k, a, b) in enumerate(terms):
                    mm = pe.matmul(out, a[:, k, :], b[m][:, k, cols], start=(n == 0), stop=(n == len(terms) - 1))
                return mm

            def x_transposes(b):
                pe.wait_ge(xg_ok, b + 1 + ONE)
                pe.wait_ge(xl_ok, b + ONE)
                for k in range(DK):
                    mm = pe.transpose(tp[:, k, :], xg[:, k * P:(k + 1) * P], G.ident[:, :])
                mm.then_inc(xt_ps, 1)

            def up(b, e):
                pe.wait_ge(lo_ok[0], e + 1 + ONE)
                pe.wait_ge(xl_ok, b + 1 + ONE)
                pe.wait_ge(silu_ok, b + ONE)
                product(pa[:, :], xh, xl, 0, 0, DK, slice(0, DE)).then_inc(a_ok, 1)

            def gate(b, e):
                pe.wait_ge(lo_ok[1], e + 1 + ONE)
                pe.wait_ge(hid_ok, b + ONE)
                product(pb[:, :], xh, xl, 1, 0, DK, slice(0, DE)).then_inc(b_ok, 1)

            def hidden_transposes(b):
                pe.wait_ge(hid_ok, b + 1 + ONE)
                pe.wait_ge(hl_ok, b + ONE)
                for k in range(HK):
                    mm = pe.transpose(ph[:, k, :], hid[:, k * P:(k + 1) * P], G.ident[:, :])
                mm.then_inc(hid_ps, 1)

            def down(b, e):
                pe.wait_ge(lo_ok[2], e + 1 + ONE)
                pe.wait_ge(hl_ok, b + 1 + ONE)
                pe.wait_ge(ys_ok, b + ONE)
                for half in range(2):
                    mm = product(py[:, half, :], hh, hl, 2, 0, HK, slice(half * 512, (half + 1) * 512))
                mm.then_inc(y_ok, 1)

            x_transposes(0)
            up(0, 0)
            gate(0, 0)
            x_transposes(1)
            last = last_block(pe)
            with pe.Fori(1, MBLK) as b:
                with pe.If(b <= last):
                    e = expert_of(pe, b)
                    up(b, e)
                    hidden_transposes(b - 1)
                    gate(b, e)
                    x_transposes(b + 1)
                    down(b - 1, expert_of(pe, b - 1))
            hidden_transposes(last)
            down(last, NE - 1)

        @block.scalar
        def _(act):
            begin(act, hi_ok[2], silu_ok, hh_ok, xh_ok, ys_ok, stored)

            def high(m, e, used, count):
                act.wait_ge(raw_ready[m], e * 16 + 16 + ONE)
                act.wait_ge(used, count + ONE)
                for half in range(2):
                    k = halves(m, half)
                    act.activation(wh[m][:, k, :], raw[m][:, k, :], ACT.Copy).then_inc(hi_ok[m], 1)

            def silu(b):
                act.wait_ge(a_ok, b + 1 + ONE)
                act.wait_ge(hid_ps, b + ONE)
                act.activation(hid[:, :], pa[:, :], ACT.Silu).then_inc(silu_ok, 1)

            def x_high(b):
                act.wait_ge(xt_ps, b + 1 + ONE)
                act.wait_ge(b_ok, b + ONE)
                act.activation(xh[:, :, :], tp[:, :, :], ACT.Copy).then_inc(xh_ok, 1)

            def hidden_high(b):
                act.wait_ge(hid_ps, b + 1 + ONE)
                act.wait_ge(y_ok, b + ONE)
                act.activation(hh[:, :, :], ph[:, :, :], ACT.Copy).then_inc(hh_ok, 1)

            def rows(b):
                act.wait_ge(y_ok, b + 1 + ONE)
                act.wait_ge(stored, b * 16 + ONE)
                act.activation(ys[:, :], py[:, :, :].rearrange("p a n -> p (a n)"), ACT.Copy).then_inc(ys_ok, 1)
                act.wait_ge(ys_ok, b + 1 + ONE)
                act.dma_start(A["s_ys"][bass.ds(b * P, P), :], ys[:, :]).then_inc(stored, 16)

            x_high(0)
            high(2, 0, raw_ready[2], 16)
            last = last_block(act)
            silu(0)
            x_high(1)
            e_next = expert_of(act, 1)
            with act.If(e_next > 0):
                high(0, e_next, a_ok, 1)
                high(1, e_next, b_ok, 1)
            with act.Fori(1, MBLK) as b:
                with act.If(b <= last):
                    before, e, after = (expert_of(act, b + n) for n in (-1, 0, 1))
                    silu(b)
                    hidden_high(b - 1)
                    with act.If(after > e):
                        high(0, after, a_ok, b + 1)
                    x_high(b + 1)
                    with act.If(after > e):
                        high(1, after, b_ok, b + 1)
                    rows(b - 1)
                    with act.If(e > before):
                        high(2, e, y_ok, b)
            hidden_high(last)
            rows(last)
            act.wait_ge(stored, last * 16 + 16 + ONE)
            act.sem_inc(passed_end, 1)

        @block.vector
        def _(dve):
            begin(dve, lo_ok[2], xl_ok, hid_ok, hl_ok, zero_ok)
            dve.memset(zero[:, :], 0.0).then_inc(zero_ok, 1)

            def low(m, e):
                for half in range(2):
                    k = halves(m, half)
                    dve.wait_ge(hi_ok[m], e * 2 + half + 1 + ONE)
                    op = dve.tensor_tensor(wl[m][:, k, :], raw[m][:, k, :], wh[m][:, k, :].bitcast(F32), ALU.subtract)
                op.then_inc(lo_ok[m], 1)

            def hidden(b):
                dve.wait_ge(b_ok, b + 1 + ONE)
                dve.wait_ge(silu_ok, b + 1 + ONE)
                dve.tensor_tensor(hid[:, :], pb[:, :], hid[:, :], ALU.mult).then_inc(hid_ok, 1)

            def x_low(b):
                dve.wait_ge(xh_ok, b + 1 + ONE)
                dve.tensor_tensor(xl[:, :, :], tp[:, :, :], xh[:, :, :].bitcast(F32), ALU.subtract).then_inc(xl_ok, 1)

            def hidden_low(b):
                dve.wait_ge(hh_ok, b + 1 + ONE)
                dve.tensor_tensor(hl[:, :, :], ph[:, :, :], hh[:, :, :].bitcast(F32), ALU.subtract).then_inc(hl_ok, 1)

            x_low(0)
            low(2, 0)
            last = last_block(dve)
            hidden(0)
            x_low(1)
            e_next = expert_of(dve, 1)
            with dve.If(e_next > 0):
                low(0, e_next)
                low(1, e_next)
            with dve.Fori(1, MBLK) as b:
                with dve.If(b <= last):
                    before, e, after = (expert_of(dve, b + n) for n in (-1, 0, 1))
                    hidden_low(b - 1)
                    with dve.If(after > e):
                        low(0, after)
                    hidden(b)
                    x_low(b + 1)
                    with dve.If(after > e):
                        low(1, after)
                    with dve.If(e > before):
                        low(2, e)
            hidden_low(last)
    c.close()


def stage_combine(nc, G, A, tag, R):
    S = G.sem
    got = [S(f"{tag}_gathered{u}") for u in range(3)]
    first, done, sq = (S(f"{tag}_{n}") for n in ("first", "added", "squares"))
    c = Ctx(nc, tag + "_")
    y = [[c.sb(f"y{u}{k}", [P, D]) for k in range(2)] for u in range(3)]
    junk = c.sb("junk", [P, D])

    def rows_of(t):
        return P if t < TILES - 1 else NTOK - P * (TILES - 1)

    with nc.Block() as block:
        @block.gpsimd
        def _(pool):
            for t in range(TILES):
                if t >= 3:
                    pool.wait_ge(done, t - 2 + ONE)
                for k in range(2):
                    pool.indirect_dma_start(out=y[t % 3][k][0:rows_of(t), :], out_offset=None, in_=A["s_ys"][:, :],
                                            in_offset=bass.IndirectOffsetOnAxis(ap=R.slot[0:rows_of(t), k, t:t + 1], axis=0),
                                            bounds_check=MBLK * P - 1).then_inc(got[t % 3], 16)

        @block.vector
        def _(dve):
            begin(dve, first, done)
            for t in range(TILES):
                n = rows_of(t)
                dve.wait_ge(got[t % 3], 32 * (t // 3 + 1))
                for k, s in ((0, first), (1, done)):
                    dve.scalar_tensor_tensor(out=G.h[0:n, t, :], in0=y[t % 3][k][0:n, :], scalar=R.gates[0:n, k, t:t + 1],
                                             in1=G.h[0:n, t, :], op0=ALU.mult, op1=ALU.add).then_inc(s, 1)
                    dve.wait_ge(s, t + 1 + ONE)

        @block.scalar
        def _(act):
            begin(act, sq)
            with act.Fori(0, TILES) as t:
                act.wait_ge(done, t + 1 + ONE)
                act.wait_ge(sq, t + ONE)
                act.activation(junk[:, :], G.h[:, bass.ds(t, 1), :], ACT.Square,
                               accum_out=G.ssq[:, bass.ds(t, 1)]).then_inc(sq, 1)
    c.close()


def layer_moe(nc, G, A, layer):
    R = Ctx(nc, f"moe{layer}_")
    R.gates = R.sb("gates", [P, 2, TILES])
    R.slot = R.sb("slot", [P, 2, TILES], I32)
    R.slot_tok = R.sb("slot_tok", [P, MBLK + 2], I32)
    R.block_expert = R.sb("block_expert", [P, MBLK + 1], I32)
    R.last = R.sb("last", [P, 1], I32)
    X = Ctx(nc, f"raw{layer}_")
    R.raw = [X.sb("w1", [P, DK, DE]), X.sb("w3", [P, DK, DE]), X.sb("w2", [P, DE // P, D])]
    R.wh, R.wl = ([X.sb(f"{part}_{m}", [P, DK, DE], F32R) for m in ("w1", "w3")] for part in ("high", "low"))
    R.hi_ok, R.lo_ok = ([G.sem(f"moe{layer}_{m}_{part}") for m in ("w1", "w3")] for part in ("high", "low"))
    R.raw_ready = [G.sem(f"raw{layer}_ready{m}") for m in range(3)]
    stage_route(nc, G, A, f"r{layer}", layer, R)
    stage_experts(nc, G, A, f"e{layer}", layer, R)
    X.close()
    stage_combine(nc, G, A, f"c{layer}", R)
    R.close()
SLOTS = 2 + GROUPS
K_SLOT, V_SLOT = 0, 1
Q_SLOT = 2
QT = SEQ // P
PAIRS = 4


def group_tiles():
    def plain(t):
        return lambda x: x[:, t * P:(t + 1) * P]

    def by4(nb, r):
        return lambda x: x[:, 4 * P * nb + r:4 * P * (nb + 1) - 3 + r:4]

    def by8(j):
        return lambda x: x[:, j:SEQ - 7 + j:8]

    out = []
    for t in range(QT):
        out.append((0, t, plain(t), [t] if t == 0 else [t - 1, t]))
    for nb in range(2):
        for r in range(4):
            out.append((1, 4 * nb + r, by4(nb, r), [4 * k + r for k in range(nb + 1)]))
    for j in range(8):
        out.append((2, j, by8(j), [j]))
    return out


def stage_heads(nc, G, A, xh, xl, H):
    S = G.sem
    RING = (0, 1, 2, 0, 1)
    BEFORE = (2, 2, 5, 3, 3)
    w_ready = [S(f"hd_w_ready{s}") for s in range(3)]
    wh_ok, wl_ok = S("hd_w_high"), S("hd_w_low")
    scaled, proj_ok, pj_ok, pj_out, t1_ok, rope_ok, table_ready, k_stored, v_stored, o_stored = (
        S("hd_" + n) for n in ("w_scaled", "product", "bank_full", "bank_read", "rope_part", "rope",
                               "tables", "k_stored", "v_stored", "o_stored"))
    passed, sc_ok, masked, exp_ok, pt_ps, pt_ok = (S("hd_" + n) for n in (
        "passed", "scores", "masked", "exp", "p_transposed", "pt"))
    c = Ctx(nc, "hd_")
    wr = c.sb("wr", [P, 3, DK, P])
    wh = c.sb("wh", [P, 3, DK, P], F32R)
    wl = c.sb("wl", [P, 3, DK, P], F32R)
    cos = c.sb("cos", [P, NTOK])
    sin = c.sb("sin", [P, NTOK])
    band = c.sb("band", [P, 2 * P])
    pair = c.sb("pair", [P, P])
    raw = c.sb("raw", [P, 2, NTOK])
    half = c.sb("half", [P, NTOK])
    flat_h = G.h[:, :, :].rearrange("p t d -> p (t d)")
    OB = GROUPS * QT * (HD + 2)
    assert SLOTS * NTOK + OB <= TILES * D
    hT = flat_h[:, 0:SLOTS * NTOK].rearrange("p (s n) -> p s n", s=SLOTS)
    ob = flat_h[:, SLOTS * NTOK:SLOTS * NTOK + OB].rearrange("p (g t c) -> p g t c", g=GROUPS, t=QT)
    vb = c.sb("vb", [P, GROUPS, QT, HD])
    vs = c.sb("vs", [P, HD])
    sc = c.sb("sc", [P, 3, 2 * P])
    pr = c.sb("pr", [P, 3, 2 * P])
    pt = c.sb("pt", [P, 3, 2, P])
    pj = [c.ps(f"pj{u}", [P, 512]) for u in range(3)]
    psc = [c.ps(f"psc{u}", [P, 512]) for u in range(2)]
    ppt = [c.ps(f"ppt{u}", [P, 2, P]) for u in range(2)]
    NC = len(CHUNKS)
    TL = group_tiles()
    NT = len(TL)

    uses = [("proj", s, n) for s in range(SLOTS) for n in range(NC)]
    v_batches = [TL[n:n + PAIRS] for n in range(0, NT, PAIRS)] + [None]
    uses += [("v", b) for b in range(len(v_batches))] + [("o", b) for b in range(NT // PAIRS)]
    NU = len(uses)
    O0 = SLOTS * NC + len(v_batches)

    def bank(n):
        return pj[n % 3]

    with nc.Block() as block:
        @block.sync
        def _(sp):
            begin(sp, table_ready, k_stored, v_stored, o_stored, w_ready)
            sp.dma_start(cos[:, :], A["c_cos"]).then_inc(table_ready, 16)
            sp.dma_start(sin[:, :], A["c_sin"]).then_inc(table_ready, 16)
            sp.dma_start(band[:, :], A["c_band"]).then_inc(table_ready, 16)
            sp.dma_start(pair[:, :], A["c_pair"]).then_inc(table_ready, 16)

            def stores(h):
                sp.wait_ge(rope_ok, h * (1 + GROUPS) + 1 + ONE)
                sp.dma_start(A["o_kT"][bass.ds(h, 1)].rearrange("a c t -> c (a t)"), hT[:, K_SLOT, :]).then_inc(k_stored, 16)
                sp.wait_ge(pj_out, h * NU + O0 + ONE)
                v_out = A["o_v"][:, bass.ds(h, 1), :].rearrange("t a c -> t (a c)")
                sp.dma_start(v_out[0:SEQ, :].rearrange("(t p) c -> p t c", p=P), vb[:, 0]).then_inc(v_stored, 16)
                sp.dma_start(v_out[SEQ:, :], vs[P - NSMP:, :]).then_inc(v_stored, 16)
                sp.wait_ge(pj_out, h * NU + NU + ONE)
                og = A["s_og"][:, :, bass.ds(h, 1), :].rearrange("g t a c -> g t (a c)")
                sp.dma_start(og[0].rearrange("(t p) c -> p t c", p=P), ob[:, 0]).then_inc(o_stored, 16)
                by4 = og[1].rearrange("(n p r) c -> n p r c", n=2, r=4)
                for n in range(2):
                    sp.dma_start(by4[n], ob[:, 1, 4 * n:4 * n + 4]).then_inc(o_stored, 16)
                sp.dma_start(og[2].rearrange("(n j) c -> n j c", j=8), ob[:, 2]).then_inc(o_stored, 16)

            def load(h, s):
                sp.dma_start(wr[:, RING[s]], A["w_heads"][bass.ds(h, 1), s].rearrange("a p k n -> p (a k) n"))\
                    .then_inc(w_ready[RING[s]], 16)

            def late_loads(h):
                for s in (3, 4):
                    sp.wait_ge(wl_ok, h * SLOTS + s - BEFORE[s] + 1 + ONE)
                    load(h, s)

            for s in range(3):
                load(0, s)
            with sp.Fori(0, HEADS - 1) as h:
                late_loads(h)
                for s in range(3):
                    sp.wait_ge(wl_ok, (h + 1) * SLOTS + s - BEFORE[s] + 1 + ONE)
                    load(h + 1, s)
                stores(h)
            late_loads(HEADS - 1)
            stores(HEADS - 1)
            sp.wait_ge(k_stored, 16 * HEADS + ONE)
            sp.wait_ge(v_stored, 32 * HEADS + ONE)
            sp.wait_ge(o_stored, 64 * HEADS + ONE)

        @block.gpsimd
        def _(pool):
            begin(pool, scaled, wl_ok)

            def scale(h, s):
                g = G.gcol[:, GAIN_KV if s < Q_SLOT else GAIN_MIX1, :].unsqueeze(2).to_broadcast([P, DK, P])
                per_head, turn = (RING.count(RING[s]), RING[:s].count(RING[s]))
                pool.wait_ge(w_ready[RING[s]], h * (16 * per_head) + (16 * turn + 16) + ONE)
                pool.tensor_tensor(wr[:, RING[s]], wr[:, RING[s]], g, ALU.mult).then_inc(scaled, 1)

            def low_part(h, s):
                pool.wait_ge(wh_ok, h * SLOTS + s + 1 + ONE)
                pool.tensor_tensor(wl[:, RING[s]], wr[:, RING[s]], wh[:, RING[s]].bitcast(F32), ALU.subtract)\
                    .then_inc(wl_ok, 1)

            scale(0, 0)
            with pool.Fori(0, HEADS) as h:
                for s in range(SLOTS - 1):
                    pool.wait_ge(scaled, h * SLOTS + s + 1 + ONE)
                    pool.wait_ge(wl_ok, h * SLOTS + s + ONE)
                    scale(h, s + 1)
                    pool.wait_ge(scaled, h * SLOTS + s + 2 + ONE)
                    low_part(h, s)
                pool.wait_ge(wl_ok, h * SLOTS + SLOTS - 1 + ONE)
                low_part(h, SLOTS - 1)
                with pool.If(h < HEADS - 1):
                    pool.wait_ge(wl_ok, h * SLOTS + SLOTS + ONE)
                    scale(h + 1, 0)

        @block.tensor
        def _(pe):
            begin(pe, proj_ok, pj_ok, sc_ok, pt_ps)
            with pe.Fori(0, HEADS) as h:
                def claim(n):
                    pe.wait_ge(pj_out, (h * NU + n - 2 if n >= 2 else h * NU) + ONE)

                n = 0
                for s in range(SLOTS):
                    pe.wait_ge(wl_ok, h * SLOTS + s + 1 + ONE)
                    for c0, cn in CHUNKS:
                        claim(n)
                        for k in range(DK):
                            for q, (w, x) in enumerate(((wh, xh), (wh, xl), (wl, xh))):
                                mm = pe.matmul(bank(n)[:, 0:cn], w[:, RING[s], k, :], x[:, k, c0:c0 + cn],
                                               start=(k == 0 and q == 0), stop=(k == DK - 1 and q == 2))
                        mm.then_inc(proj_ok, 1)
                        n += 1
                pe.wait_ge(pj_out, h * NU + (V_SLOT + 1) * NC + ONE)
                for batch in v_batches:
                    claim(n)
                    if batch is None:
                        pe.transpose(bank(n)[:, 0:HD], hT[:, V_SLOT, NTOK - P:], G.ident[:, :]).then_inc(pj_ok, 1)
                    else:
                        for q, (g, t, view, keys) in enumerate(batch):
                            mm = pe.transpose(bank(n)[:, q * P:(q + 1) * P], view(hT[:, V_SLOT, :]), G.ident[:, :])
                        mm.then_inc(pj_ok, 1)
                    n += 1

                def scores(j):
                    g, t, view, keys = TL[j]
                    pe.wait_ge(rope_ok, h * (1 + GROUPS) + 2 + g + ONE)
                    pe.wait_ge(masked, (h * NT + j - 1 if j >= 2 else h * NT) + ONE)
                    kT = hT[:, K_SLOT, :]
                    for b, key in enumerate(keys):
                        kv = [x for x in TL if x[0] == g and x[1] == key][0][2]
                        mm = pe.matmul(psc[j % 2][:, b * P:(b + 1) * P], view(hT[:, Q_SLOT + g, :]), kv(kT),
                                       start=True, stop=True)
                    mm.then_inc(sc_ok, 1)

                def p_transposes(j):
                    pe.wait_ge(exp_ok, h * NT + j + 1 + ONE)
                    pe.wait_ge(pt_ok, (h * NT + j - 1 if j >= 2 else h * NT) + ONE)
                    for b in range(len(TL[j][3])):
                        mm = pe.transpose(ppt[j % 2][:, b, :], pr[:, j % 3, b * P:(b + 1) * P], G.ident[:, :])
                    mm.then_inc(pt_ps, 1)

                def weighted(j):
                    g, t, view, keys = TL[j]
                    if j % PAIRS == 0:
                        claim(O0 + j // PAIRS)
                    pe.wait_ge(pt_ok, h * NT + j + 1 + ONE)
                    for b, key in enumerate(keys):
                        mm = pe.matmul(bank(O0 + j // PAIRS)[:, (j % PAIRS) * P:(j % PAIRS + 1) * P], pt[:, j % 3, b, :],
                                       vb[:, g, key, :], start=(b == 0), stop=(b == len(keys) - 1))
                    if j % PAIRS == PAIRS - 1:
                        mm.then_inc(pj_ok, 1)

                pe.wait_ge(pj_out, h * NU + O0 + ONE)
                for j in range(NT + 3):
                    if j < NT:
                        scores(j)
                    if 0 <= j - 2 < NT:
                        p_transposes(j - 2)
                    if j >= 3:
                        weighted(j - 3)

        @block.scalar
        def _(act):
            begin(act, pj_out, exp_ok, wh_ok)

            def high_part(h, s):
                act.wait_ge(scaled, h * SLOTS + s + 1 + ONE)
                act.activation(wh[:, RING[s]], wr[:, RING[s]], ACT.Copy).then_inc(wh_ok, 1)

            for s in range(3):
                high_part(0, s)
            with act.Fori(0, HEADS) as h:
                n = 0
                for s in range(SLOTS):
                    if s == V_SLOT:
                        dst = hT[:, V_SLOT, :]
                    else:
                        r = s if s == 0 else s - 1
                        dst = raw[:, r % 2, :]
                        act.wait_ge(rope_ok, (h * (1 + GROUPS) + r - 1 if r >= 2 else h * (1 + GROUPS)) + ONE)
                    for c0, cn in CHUNKS:
                        act.wait_ge(proj_ok, h * SLOTS * NC + n + 1 + ONE)
                        act.activation(dst[:, c0:c0 + cn], bank(n)[:, 0:cn], ACT.Copy).then_inc(pj_out, 1)
                        n += 1
                    if s < 2:
                        high_part(h, s + 3)
                act.wait_ge(v_stored, h * 32 + ONE)
                for b, batch in enumerate(v_batches):
                    act.wait_ge(pj_ok, h * (NU - O0 + len(v_batches)) + b + 1 + ONE)
                    if batch is None:
                        act.activation(vs[:, :], bank(n)[:, 0:HD], ACT.Copy).then_inc(pj_out, 1)
                    else:
                        g, t = batch[0][:2]
                        act.activation(vb[:, g, t:t + PAIRS, :], bank(n)[:, :].rearrange("p (t c) -> p t c", c=HD),
                                       ACT.Copy).then_inc(pj_out, 1)
                    n += 1
                act.wait_ge(o_stored, h * 64 + ONE)
                for j in range(NT + 4):
                    if j in (4, 9, 14):
                        with act.If(h < HEADS - 1):
                            high_part(h + 1, (4, 9, 14).index(j))
                    if j < NT:
                        g, t, view, keys = TL[j]
                        w = len(keys) * P
                        act.wait_ge(masked, h * NT + j + 1 + ONE)
                        act.wait_ge(pt_ps, (h * NT + j - 2 if j >= 3 else h * NT) + ONE)
                        act.activation(pr[:, j % 3, 0:w], sc[:, j % 3, 0:w], ACT.Exp, bias=ob[:, g, t, HD:HD + 1],
                                       scale=-1.0, accum_out=ob[:, g, t, HD + 1:HD + 2]).then_inc(exp_ok, 1)
                    if j >= 4 and (j - 4) % PAIRS == PAIRS - 1:
                        b = (j - 4) // PAIRS
                        g, t = TL[b * PAIRS][:2]
                        act.wait_ge(pj_ok, h * (NU - O0 + len(v_batches)) + len(v_batches) + b + 1 + ONE)
                        act.activation(ob[:, g, t:t + PAIRS, 0:HD], bank(O0 + b)[:, :].rearrange("p (t c) -> p t c", c=HD),
                                       ACT.Copy).then_inc(pj_out, 1)

        @block.vector
        def _(dve):
            begin(dve, t1_ok, rope_ok, masked, pt_ok)
            dve.wait_ge(table_ready, 64 + ONE)
            HALF = HD // 2
            with dve.Fori(0, HEADS) as h:
                def rope(s, r):
                    dve.wait_ge(pj_out, h * NU + (s + 1) * NC + ONE)
                    if s == K_SLOT:
                        dve.wait_ge(k_stored, h * 16 + ONE)
                    src, dst = raw[:, r % 2, :], hT[:, s, :]
                    dve.tensor_tensor(dst, src, cos[:, :], ALU.mult)
                    dve.tensor_tensor(half[0:HALF, :], src[HALF:, :], sin[HALF:, :], ALU.mult)
                    dve.tensor_tensor(half[HALF:, :], src[0:HALF, :], sin[0:HALF, :], ALU.mult).then_inc(t1_ok, 1)
                    dve.wait_ge(t1_ok, h * (1 + GROUPS) + r + 1 + ONE)
                    dve.tensor_tensor(dst, dst, half[:, :], ALU.add).then_inc(rope_ok, 1)
                    dve.wait_ge(rope_ok, h * (1 + GROUPS) + r + 1 + ONE)
                    if s == K_SLOT:
                        dve.tensor_copy(H.ks[:, bass.ds(h, 1), :].rearrange("p a n -> p (a n)"), dst[:, SEQ:])
                    else:
                        dve.tensor_copy(H.qs[:, bass.ds(h, 1), s - Q_SLOT, :].rearrange("p a n -> p (a n)"), dst[:, SEQ:])

                for r, s in enumerate((K_SLOT, Q_SLOT, Q_SLOT + 1, Q_SLOT + 2)):
                    rope(s, r)
                for j in range(NT + 2):
                    if j < NT:
                        g, t, view, keys = TL[j]
                        w = len(keys) * P
                        mask = pair[:, :] if g == 2 else band[:, 2 * P - w:]
                        dve.wait_ge(sc_ok, h * NT + j + 1 + ONE)
                        dve.wait_ge(exp_ok, (h * NT + j - 2 if j >= 3 else h * NT) + ONE)
                        if j == 0:
                            dve.wait_ge(o_stored, h * 64 + ONE)
                        dve.sem_inc(passed, 1)
                        dve.tensor_tensor_reduce(out=sc[:, j % 3, 0:w], in0=psc[j % 2][:, 0:w], in1=mask, scale=-SCALE,
                                                 scalar=3.0e38, op0=ALU.add, op1=ALU.min,
                                                 accum_out=ob[:, g, t, HD:HD + 1]).then_inc(masked, 1)
                    if j >= 2:
                        b = j - 2
                        w = len(TL[b][3])
                        dve.wait_ge(pt_ps, h * NT + b + 1 + ONE)
                        dve.tensor_copy(pt[:, b % 3, 0:w, :], ppt[b % 2][:, 0:w, :]).then_inc(pt_ok, 1)
    c.close()


def stage_sample(nc, G, A, H):
    S = G.sem
    passed = S("sm_passed")
    (k_ready, v_ready, mask_ready, q_ok, kt_ps, kt_out, new_ok, st_ps, st_out, s_ps, masked, exp_ok, chain, norm_ok, pt_ps, pt_out,
     o_ps, o_out) = (S("sm_" + n) for n in (
         "k_ready", "v_ready", "mask_ready", "q", "kt_bank", "kt", "new_k", "st_bank", "st", "scores", "masked", "exp",
         "chain", "normed", "pt_bank", "pt", "o_bank", "o"))
    c = Ctx(nc, "sm_")
    NB = 2
    KC = PAST // P
    NK = PAST + DEC_S
    QN = GROUPS * DEC_S
    R = NB * HEADS * DEC_S
    assert R == P
    kc = c.sb("kc", [P, NB, KC, HEADS, HD])
    vc = c.sb("vc", [P, NB, KC, HEADS, HD])
    vn = c.sb("vn", [DEC_S, NB, HEADS, HD])
    mask = c.sb("mask", [P, GROUPS, NK])
    qb = c.sb("qb", [P, NB, HEADS, GROUPS, DEC_S])
    kT = c.sb("kT", [P, NB, HEADS, NK])
    sT = c.sb("sT", [P, KC + 1, GROUPS, NB, HEADS, DEC_S])
    sc = c.sb("sc", [P, GROUPS, NK])
    pr = c.sb("pr", [P, GROUPS, NK])
    stat = c.sb("stat", [P, 8])
    pT = c.sb("pT", [P, KC + 1, P])
    bk = [c.ps(f"bk{u}", [P, 4, P]) for u in range(2)]
    pst = [c.ps(f"pst{u}", [P, HEADS, GROUPS, DEC_S]) for u in range(2)]
    psc = c.ps("psc", [P, GROUPS, 512])
    px = c.ps("px", [P, 512])
    KB = NB * KC * HEADS // 4
    STEPS = DEC_B // NB
    LINKS = 4

    with nc.Block() as block:
        @block.sync
        def _(sp):
            begin(sp, mask_ready, k_ready, v_ready, H.wo_ready, H.h_ready)
            def keys(i):
                for b in range(NB):
                    sp.dma_start(kc[:, b], A["cache_k"][bass.ds(i * NB + b, 1)].rearrange("a (k p) h c -> p (a k) h c", p=P))\
                        .then_inc(k_ready, 16)

            def values(i):
                for b in range(NB):
                    sp.dma_start(vc[:, b], A["cache_v"][bass.ds(i * NB + b, 1)].rearrange("a (k p) h c -> p (a k) h c", p=P))\
                        .then_inc(v_ready, 16)
                    sp.dma_start(vn[:, b], A["o_v"][bass.ds(i * (NB * DEC_S) + SEQ + b * DEC_S, DEC_S)]).then_inc(v_ready, 16)

            keys(0)
            sp.dma_start(mask[:, :, :], A["c_smp"]).then_inc(mask_ready, 16)
            values(0)
            sp.wait_ge(kt_ps, KB + ONE)
            keys(1)
            sp.dma_start(G.h[:, :, :], A["s_h"].rearrange("(t p) d -> p t d", p=P)).then_inc(H.h_ready, 16)
            for k in range(HEADS):
                sp.dma_start(H.wo[:, k, :], A["attn_w_o"][0, k * P:(k + 1) * P, :]).then_inc(H.wo_ready, 16)
            with sp.Fori(0, STEPS - 2) as i:
                sp.wait_ge(kt_ps, i * KB + 2 * KB + ONE)
                keys(i + 2)
                sp.wait_ge(o_ps, i + 1 + ONE)
                values(i + 1)
            sp.wait_ge(o_ps, STEPS - 1 + ONE)
            values(STEPS - 1)

        @block.gpsimd
        def _(pool):
            begin(pool, q_ok)
            with pool.Fori(0, STEPS) as i:
                pool.wait_ge(st_ps, i * (NB * (KC + 1)) + ONE)
                for b in range(NB):
                    pool.wait_ge(q_ok, i * (2 * NB) + 2 * b + ONE)
                    t0 = i * (NB * DEC_S) + b * DEC_S
                    pool.tensor_copy(qb[:, b], H.qs[:, :, :, bass.ds(t0, DEC_S)]).then_inc(q_ok, 1)
                    pool.wait_ge(q_ok, i * (2 * NB) + 2 * b + 1 + ONE)
                    pool.tensor_copy(kT[:, b, :, PAST:], H.ks[:, :, bass.ds(t0, DEC_S)]).then_inc(q_ok, 1)

        @block.tensor
        def _(pe):
            begin(pe, kt_ps, st_ps, s_ps, pt_ps, o_ps)
            def scores(i):
                pe.wait_ge(k_ready, i * (16 * NB) + 16 * NB + ONE)
                n = 0
                for b in range(NB):
                    for h in range(0, HEADS, 2):
                        pe.wait_ge(kt_out, (i * KB + n - 1 if n >= 2 else i * KB) + ONE)
                        for q in range(4):
                            mm = pe.transpose(bk[n % 2][:, q, :], kc[:, b, q % 2, h + q // 2, :], G.ident[:, :])
                        mm.then_inc(kt_ps, 1)
                        n += 1
                pe.wait_ge(kt_out, i * KB + KB + ONE)
                pe.wait_ge(q_ok, i * (2 * NB) + 2 * NB + ONE)
                n = 0
                for k in range(KC + 1):
                    kw = P if k < KC else DEC_S
                    for b in range(NB):
                        pe.wait_ge(st_out, (i * (NB * (KC + 1)) + n - 1 if n >= 2 else i * (NB * (KC + 1))) + ONE)
                        for h in range(HEADS):
                            mm = pe.matmul(pst[n % 2][0:kw, h], kT[:, b, h, k * P:k * P + kw],
                                           qb[:, b, h], start=True, stop=True)
                        mm.then_inc(st_ps, 1)
                        n += 1
                pe.wait_ge(st_out, i * (NB * (KC + 1)) + n + ONE)
                pe.wait_ge(masked, i * GROUPS + ONE)
                for g in range(GROUPS):
                    for k in range(KC + 1):
                        kw = P if k < KC else DEC_S
                        mm = pe.transpose(psc[:, g, k * P:k * P + kw],
                                          sT[0:kw, k, g].rearrange("p b h n -> p (b h n)"), G.ident[0:kw, 0:kw])
                    mm.then_inc(s_ps, 1)

            def weighted(i):
                pe.wait_ge(norm_ok, i + 1 + ONE)
                pe.wait_ge(o_out, i + ONE)
                for k in range(KC + 1):
                    kw = P if k < KC else DEC_S
                    mm = pe.transpose(px[0:kw, k * P:(k + 1) * P], pr[:, 0, k * P:k * P + kw], G.ident[:, :])
                mm.then_inc(pt_ps, 1)
                pe.wait_ge(pt_out, i + 1 + ONE)
                pe.wait_ge(v_ready, i * (32 * NB) + 32 * NB + ONE)
                for b in range(NB):
                    for h in range(HEADS):
                        q0 = (b * HEADS + h) * DEC_S
                        for k in range(KC + 1):
                            kw = P if k < KC else DEC_S
                            v = vc[:, b, k, h, :] if k < KC else vn[:, b, h, :]
                            mm = pe.matmul(px[:, q0:q0 + DEC_S], v, pT[0:kw, k, q0:q0 + DEC_S],
                                           start=(k == 0), stop=(k == KC))
                mm.then_inc(o_ps, 1)

            scores(0)
            with pe.Fori(0, STEPS - 1) as i:
                scores(i + 1)
                weighted(i)
            weighted(STEPS - 1)

        @block.scalar
        def _(act):
            begin(act, kt_out, exp_ok)
            def keys(i):
                for n in range(KB):
                    b, h = n // (HEADS // 2), n % (HEADS // 2) * 2
                    act.wait_ge(kt_ps, i * KB + n + 1 + ONE)
                    if n == 0:
                        act.wait_ge(st_ps, i * (NB * (KC + 1)) + ONE)
                    act.activation(kT[:, b, h:h + 2, 0:PAST].rearrange("p h (k c) -> p h k c", c=P),
                                   bk[n % 2][:, :, :].rearrange("p (h k) c -> p h k c", k=KC), ACT.Copy).then_inc(kt_out, 1)

            def exp(i):
                act.wait_ge(chain, i * LINKS + 1 + ONE)
                act.wait_ge(norm_ok, i + ONE)
                act.activation(pr[:, :, :].rearrange("p g k -> p (g k)"), sc[:, :, :].rearrange("p g k -> p (g k)"),
                               ACT.Exp, bias=stat[:, 3:4], scale=-1.0, accum_out=stat[:, 4:5]).then_inc(exp_ok, 1)

            keys(0)
            with act.Fori(0, STEPS - 1) as i:
                exp(i)
                keys(i + 1)
            exp(STEPS - 1)

        @block.vector
        def _(dve):
            begin(dve, st_out, masked, norm_ok, pt_out, o_out, chain)
            dve.wait_ge(mask_ready, 16 + ONE)

            def scores(i):
                n = 0
                for k in range(KC + 1):
                    kw = P if k < KC else DEC_S
                    for b in range(NB):
                        dve.wait_ge(st_ps, i * (NB * (KC + 1)) + n + 1 + ONE)
                        if n == 0:
                            dve.wait_ge(s_ps, i * GROUPS + ONE)
                        dve.tensor_copy(sT[0:kw, k, :, b], pst[n % 2][0:kw].rearrange("p h g n -> p g h n"))\
                            .then_inc(st_out, 1)
                        n += 1
                for g in range(GROUPS):
                    dve.wait_ge(s_ps, i * GROUPS + g + 1 + ONE)
                    if g == 0:
                        dve.wait_ge(exp_ok, i + ONE)
                    dve.sem_inc(passed, 1)
                    dve.tensor_tensor_reduce(out=sc[:, g, :], in0=psc[:, g, 0:NK], in1=mask[:, g, :], scale=-SCALE,
                                             scalar=3.0e38, op0=ALU.add, op1=ALU.min,
                                             accum_out=stat[:, g:g + 1]).then_inc(masked, 1)

            def softmax(i):
                link = Chain(dve, chain, i * LINKS)
                dve.wait_ge(masked, i * GROUPS + GROUPS + ONE)
                link(dve.tensor_reduce(stat[:, 3:4], stat[:, 0:3], AX.X, ALU.min))
                dve.wait_ge(exp_ok, i + 1 + ONE)
                link(dve.reciprocal(stat[:, 5:6], stat[:, 4:5]))
                link(dve.tensor_tensor(pr[:, 0, :], pr[:, 0, :], pr[:, 1, :], ALU.add))
                link(dve.tensor_tensor(pr[:, 0, :], pr[:, 0, :], pr[:, 2, :], ALU.add))
                assert link.n == LINKS
                dve.wait_ge(pt_ps, i + ONE)
                dve.tensor_scalar(pr[:, 0, :], pr[:, 0, :], stat[:, 5:6], None, ALU.mult).then_inc(norm_ok, 1)

            def weighted(i):
                dve.wait_ge(pt_ps, i + 1 + ONE)
                dve.wait_ge(o_ps, i + ONE)
                dve.tensor_copy(pT[:, 0:KC, :], px[:, 0:KC * P].rearrange("p (k c) -> p k c", c=P))
                dve.tensor_copy(pT[0:DEC_S, KC, :], px[0:DEC_S, KC * P:(KC + 1) * P]).then_inc(pt_out, 1)
                dve.wait_ge(o_ps, i + 1 + ONE)
                for b in range(NB):
                    last = dve.tensor_copy(H.oT[:, :, bass.ds(i * (NB * DEC_S) + b * DEC_S, DEC_S)],
                                           px[:, b * HEADS * DEC_S:(b + 1) * HEADS * DEC_S].rearrange("p (h n) -> p h n", n=DEC_S))
                last.then_inc(o_out, 1)

            scores(0)
            with dve.Fori(0, STEPS - 1) as i:
                softmax(i)
                scores(i + 1)
                weighted(i)
            softmax(STEPS - 1)
            weighted(STEPS - 1)
    c.close()


def stage_merge(nc, G, A, H):
    S = G.sem
    og_ready = [S(f"mg_og_ready{u}") for u in range(2)]
    wh_ok, wl_ok, diff_ok, exp_ok, chain, rows_ok, tr_ok, oh_ok, ol_ok, prod, added, sq = (S("mg_" + n) for n in (
        "w_high", "w_low", "diff", "exp", "chain", "rows", "transposed", "o_high", "o_low", "product", "added", "squares"))
    c = Ctx(nc, "mg_")
    wh = c.sb("wh", [P, HEADS, D], F32R)
    wl = c.sb("wl", [P, HEADS, D], F32R)
    og = c.sb("og", [P, 2, GROUPS, HEADS, HD + 2])
    df = c.sb("df", [P, 2, GROUPS, HEADS])
    ex = c.sb("ex", [P, 2, GROUPS, HEADS])
    den = c.sb("den", [P, 2, 3, HEADS])
    orow = c.sb("orow", [P, 2, HEADS, HD])
    term = c.sb("term", [P, HEADS, HD])
    oh = c.sb("oh", [P, 2, HEADS, P], F32R)
    ol = c.sb("ol", [P, 2, HEADS, P], F32R)
    tp = [c.ps(f"tp{u}", [P, HEADS, P]) for u in range(2)]
    py = [c.ps(f"py{u}", [P, 2, 512]) for u in range(2)]
    junk = H.wo[:, 0, :]
    LINKS = 11

    with nc.Block() as block:
        @block.sync
        def _(sp):
            begin(sp, og_ready)
            def load(t, u):
                for g in range(GROUPS):
                    sp.dma_start(og[:, u, g], A["s_og"][g, bass.ds(t * P, P)]).then_inc(og_ready[u], 16)

            for u in range(2):
                load(u, u)
            with sp.Fori(0, QT // 2 - 1) as i:
                for u in range(2):
                    sp.wait_ge(rows_ok, i * 2 + u + 1 + ONE)
                    load(i * 2 + u + 2, u)

        @block.gpsimd
        def _(pool):
            begin(pool, wl_ok)
            for k in range(HEADS):
                pool.wait_ge(wh_ok, k + 1 + ONE)
                pool.wait_ge(wl_ok, k + ONE)
                pool.tensor_tensor(wl[:, k, :], H.wo[:, k, :], wh[:, k, :].bitcast(F32), ALU.subtract).then_inc(wl_ok, 1)

        @block.vector
        def _(dve):
            begin(dve, added, diff_ok, rows_ok, ol_ok, chain)

            def merge(t, u, turn):
                link = Chain(dve, chain, t * LINKS)
                nmax = og[:, u, :, :, HD]
                low, dn, rc = (den[:, u, n] for n in range(3))
                dve.wait_ge(og_ready[u], turn * 48 + 48 + ONE)
                link(dve.tensor_tensor(low, nmax[:, 0], nmax[:, 1], ALU.min))
                link(dve.tensor_tensor(low, low, nmax[:, 2], ALU.min))
                dve.tensor_tensor(df[:, u], low.unsqueeze(1).to_broadcast([P, GROUPS, HEADS]), nmax,
                                  ALU.subtract).then_inc(diff_ok, 1)
                dve.wait_ge(exp_ok, t + 1 + ONE)
                link(dve.tensor_tensor(df[:, u], ex[:, u], og[:, u, :, :, HD + 1], ALU.mult))
                link(dve.tensor_tensor(dn, df[:, u, 0], df[:, u, 1], ALU.add))
                link(dve.tensor_tensor(dn, dn, df[:, u, 2], ALU.add))
                link(dve.reciprocal(rc, dn))
                link(dve.tensor_tensor(ex[:, u], ex[:, u], rc.unsqueeze(1).to_broadcast([P, GROUPS, HEADS]), ALU.mult))
                dve.wait_ge(tr_ok, turn * 2 + u + ONE)
                for g in range(GROUPS):
                    w = ex[:, u, g].unsqueeze(2).to_broadcast([P, HEADS, HD])
                    if g == 0:
                        link(dve.tensor_tensor(orow[:, u], og[:, u, g, :, 0:HD], w, ALU.mult))
                    else:
                        link(dve.tensor_tensor(term[:, :, :], og[:, u, g, :, 0:HD], w, ALU.mult))
                        if g == 1:
                            link(dve.tensor_tensor(orow[:, u], orow[:, u], term[:, :, :], ALU.add))
                        else:
                            dve.tensor_tensor(orow[:, u], orow[:, u], term[:, :, :], ALU.add).then_inc(rows_ok, 1)
                assert link.n == LINKS

            def low_part(t, u):
                dve.wait_ge(oh_ok, t + 1 + ONE)
                dve.tensor_tensor(ol[:, u], tp[u][:, :, :], oh[:, u].bitcast(F32), ALU.subtract).then_inc(ol_ok, 1)

            def finish(t, u, n):
                dve.wait_ge(prod, t + 1 + ONE)
                row = G.h[0:n, bass.ds(t, 1), :].rearrange("p a d -> p (a d)")
                dve.tensor_tensor(row, py[u][0:n].rearrange("p a n -> p (a n)"), row, ALU.add).then_inc(added, 1)

            for u in range(2):
                merge(u, u, 0)
            dve.wait_ge(H.h_ready, 16 + ONE)
            for u in range(2):
                low_part(u, u)
            with dve.Fori(0, QT // 2 - 1) as i:
                for u in range(2):
                    merge(i * 2 + u + 2, u, i + 1)
                    finish(i * 2 + u, u, P)
                    low_part(i * 2 + u + 2, u)
            finish(QT - 2, 0, P)
            dve.wait_ge(oh_ok, QT + 1 + ONE)
            dve.tensor_tensor(ol[:, 0, :, 0:NSMP], H.oT[:, :, :], oh[:, 0, :, 0:NSMP].bitcast(F32), ALU.subtract).then_inc(ol_ok, 1)
            finish(QT - 1, 1, P)
            finish(QT, 0, NSMP)

        @block.tensor
        def _(pe):
            begin(pe, prod, tr_ok)

            def transposes(t, u):
                pe.wait_ge(rows_ok, t + 1 + ONE)
                for k in range(HEADS):
                    mm = pe.transpose(tp[u][:, k, :], orow[:, u, k, :], G.ident[:, :])
                mm.then_inc(tr_ok, 1)

            def project(t, u, n):
                pe.wait_ge(ol_ok, t + 1 + ONE)
                for half in range(2):
                    cols = slice(half * 512, (half + 1) * 512)
                    terms = [(k, a, b) for k in range(HEADS) for a, b in ((oh, wh), (ol, wh), (oh, wl))]
                    for m, (k, a, b) in enumerate(terms):
                        mm = pe.matmul(py[u][0:n, half, :], a[:, u, k, 0:n], b[:, k, cols],
                                       start=(m == 0), stop=(m == len(terms) - 1))
                mm.then_inc(prod, 1)

            for u in range(2):
                transposes(u, u)
            pe.wait_ge(wl_ok, HEADS + ONE)
            with pe.Fori(0, QT // 2 - 1) as i:
                for u in range(2):
                    pe.wait_ge(added, i * 2 + ONE)
                    project(i * 2 + u, u, P)
                    transposes(i * 2 + u + 2, u)
            pe.wait_ge(added, QT - 2 + ONE)
            project(QT - 2, 0, P)
            project(QT - 1, 1, P)
            pe.wait_ge(added, QT - 1 + ONE)
            project(QT, 0, NSMP)

        @block.scalar
        def _(act):
            begin(act, wh_ok, oh_ok, sq, exp_ok)

            def exp(t, u):
                act.wait_ge(diff_ok, t + 1 + ONE)
                act.activation(ex[:, u], df[:, u], ACT.Exp).then_inc(exp_ok, 1)

            def high_part(t, u):
                act.wait_ge(tr_ok, t + 1 + ONE)
                act.wait_ge(prod, t - 1 + ONE)
                act.activation(oh[:, u], tp[u][:, :, :], ACT.Copy).then_inc(oh_ok, 1)

            def square(t):
                act.wait_ge(added, t + 1 + ONE)
                act.wait_ge(sq, t + ONE)
                act.activation(junk, G.h[:, bass.ds(t, 1), :], ACT.Square,
                               accum_out=G.ssq[:, bass.ds(t, 1)]).then_inc(sq, 1)

            exp(0, 0)
            act.wait_ge(H.wo_ready, 16 * HEADS + ONE)
            for k in range(HEADS // 2):
                act.activation(wh[:, k, :], H.wo[:, k, :], ACT.Copy).then_inc(wh_ok, 1)
            exp(1, 1)
            for k in range(HEADS // 2, HEADS):
                act.activation(wh[:, k, :], H.wo[:, k, :], ACT.Copy).then_inc(wh_ok, 1)
            act.wait_ge(wl_ok, 1 + ONE)
            for u in range(2):
                act.wait_ge(tr_ok, u + 1 + ONE)
                act.activation(oh[:, u], tp[u][:, :, :], ACT.Copy).then_inc(oh_ok, 1)
            with act.Fori(0, QT // 2 - 1) as i:
                for u in range(2):
                    exp(i * 2 + u + 2, u)
                    high_part(i * 2 + u + 2, u)
                    square(i * 2 + u)
            act.wait_ge(prod, QT - 1 + ONE)
            act.activation(oh[:, 0, :, 0:NSMP], H.oT[:, :, :], ACT.Copy).then_inc(oh_ok, 1)
            for t in (QT - 2, QT - 1, QT):
                square(t)
    c.close()


def stage_out(nc, G, A):
    S = G.sem
    var_ok, root_ok, rstd_ok, rows_ok, out_ok, g_ready = (S("fn_" + n) for n in ("var", "root", "rstd", "rows", "out", "gain"))
    stored = [S(f"fn_stored{u}") for u in range(3)]
    c = Ctx(nc, "fn_")
    st = c.sb("stats", [P, 3, TILES])
    g = c.sb("gain", [P, D])
    rows = c.sb("rows", [P, 3, D])
    with nc.Block() as block:
        @block.sync
        def _(sp):
            begin(sp, g_ready, stored)
            sp.dma_start(g[:, :], A["norm_final"].partition_broadcast(P)).then_inc(g_ready, 16)
            with sp.Fori(0, QT // 2) as i:
                for u in range(2):
                    sp.wait_ge(out_ok, i * 2 + u + 1 + ONE)
                    sp.dma_start(A["o_y"][bass.ds((i * 2 + u) * P, P), :], rows[:, u, :]).then_inc(stored[u], 16)
            sp.wait_ge(out_ok, TILES + ONE)
            sp.dma_start(A["o_y"][SEQ:, :], rows[0:NSMP, 2, :]).then_inc(stored[2], 16)
            sp.wait_ge(stored[0], 16 * (QT // 2) + ONE)
            sp.wait_ge(stored[1], 16 * (QT // 2) + ONE)
            sp.wait_ge(stored[2], 16 + ONE)

        @block.scalar
        def _(act):
            begin(act, root_ok)
            act.wait_ge(var_ok, 1 + ONE)
            act.activation(st[:, 1, :], st[:, 0, :], ACT.Sqrt).then_inc(root_ok, 1)

        @block.vector
        def _(dve):
            begin(dve, var_ok, rstd_ok, rows_ok, out_ok)
            dve.tensor_scalar(st[:, 0, :], G.ssq[:, :], 1.0 / D, EPS, ALU.mult, ALU.add).then_inc(var_ok, 1)
            dve.wait_ge(root_ok, 1 + ONE)
            dve.reciprocal(st[:, 2, :], st[:, 1, :]).then_inc(rstd_ok, 1)
            dve.wait_ge(rstd_ok, 1 + ONE)
            dve.wait_ge(g_ready, 16 + ONE)

            def row(t, u):
                dve.tensor_scalar(rows[:, u, :], G.h[:, bass.ds(t, 1), :].rearrange("p a d -> p (a d)"),
                                  st[:, 2, bass.ds(t, 1)], None, ALU.mult).then_inc(rows_ok, 1)
                dve.wait_ge(rows_ok, t + 1 + ONE)
                dve.tensor_tensor(rows[:, u, :], rows[:, u, :], g[:, :], ALU.mult).then_inc(out_ok, 1)

            with dve.Fori(0, QT // 2) as i:
                for u in range(2):
                    dve.wait_ge(stored[u], i * 16 + ONE)
                    row(i * 2 + u, u)
            row(QT, 2)
    c.close()


def layer_attention(nc, G, A):
    H = Ctx(nc, "la_")
    H.qs = H.sb("qs", [P, HEADS, GROUPS, NSMP])
    H.ks = H.sb("ks", [P, HEADS, NSMP])
    H.oT = H.sb("oT", [P, HEADS, NSMP])
    cx = Ctx(nc, "lb_")
    xh = cx.sb("xh", [P, DK, NPAD], F32R)
    xl = cx.sb("xl", [P, DK, NPAD], F32R)
    stage_norm(nc, G, "n1", xh, xl, A["s_h"])
    stage_heads(nc, G, A, xh, xl, H)
    cx.close()
    H.wo = H.sb("wo", [P, HEADS, D])
    H.wo_ready = G.sem("wo_ready")
    H.h_ready = G.sem("h_ready")
    stage_sample(nc, G, A, H)
    stage_merge(nc, G, A, H)
    H.close()
def build(nc, A):
    G = Ctx(nc)
    sems = []

    def new_sem(name):
        sems.append(nc.alloc_semaphore(name))
        return sems[-1]

    def clear_sems():
        nc.clear_and_free_semaphores(sems)
        nc.all_engine_barrier()
        sems.clear()

    G.sem = new_sem
    G.h = G.sb("h", [P, TILES, D])
    G.ssq = G.sb("ssq", [P, TILES])
    G.ident = G.sb("ident", [P, P])
    G.gcol = G.sb("gcol", [P, N_GAINS, DK])
    layer_conv(nc, G, A)
    layer_moe(nc, G, A, 0)
    clear_sems()
    layer_attention(nc, G, A)
    layer_moe(nc, G, A, 1)
    stage_out(nc, G, A)
    clear_sems()
    G.close()


def layer_conv(nc, G, A):
    c = Ctx(nc, "lc_")
    zT = c.sb("zT", [P, DK, NPAD])
    cx = Ctx(nc, "lx_")
    W = cx
    W.wh = cx.sb("wh", [P, 2, DK, 3, P], F32R)
    W.wl = cx.sb("wl", [P, 2, DK, 3, P], F32R)
    W.first = zT[:, DK - 3:, :].rearrange("p k n -> p (k n)")[:, 0:DK * 3 * P].rearrange("p (k c n) -> p k c n", k=DK, c=3)
    stage_load(nc, G, A, W)
    xh = cx.sb("xh", [P, DK, NPAD], F32R)
    xl = cx.sb("xl", [P, DK, NPAD], F32R)
    w_out = Ctx(nc)
    w_out.raw = G.h[:, 0:DK, :]
    w_out.dram = A["conv_w_out"].rearrange("a (k p) n -> p (a k) n", p=P)
    w_out.early = 2 * DK * 3 * P // D
    w_out.ready = G.sem("w_out_ready")
    stage_norm(nc, G, "n0", xh, xl, W=W)
    stage_conv(nc, G, A, xh, xl, W, zT, w_out)
    cx.close()
    stage_project(nc, G, A, "po", zT, w_out)
    c.close()


IOTA_COLS = P + 2 * TILES + EG
N_GAINS = 3
GAIN_MIX0, GAIN_MIX1, GAIN_KV = range(N_GAINS)


def _col(a, np):
    b = a.reshape(a.shape[:-1] + (DK, P))
    return np.ascontiguousarray(np.moveaxis(b, -1, 0))


def _constants(np):
    f = np.float32
    half = HD // 2
    inv = np.power(f(10000.0), -np.arange(half, dtype=f) / f(half)).astype(f)
    pos = np.concatenate([np.arange(SEQ), PAST + np.tile(np.arange(DEC_S), DEC_B)]).astype(f)
    ang = (inv[:, None] * pos[None, :]).astype(f)
    q, k = np.arange(P)[:, None], np.arange(2 * P)[None, :]
    rel = q + P - k
    band = np.where((rel >= 0) & (rel <= WINDOW_KEYS), 0.0, NEG)
    n = np.arange(P)
    back = n[:, None] - n[None, :]
    pair = np.where((back >= 0) & (back % 2 == 0), 0.0, NEG)
    qn = np.arange(P) % DEC_S
    j = np.arange(PAST + DEC_S)
    smp = []
    for dil in (1, 4, 16):
        dist = PAST + qn[:, None] - j[None, :]
        smp.append(np.where((dist >= 0) & (dist % dil == 0) & (dist // dil <= WINDOW_KEYS), 0.0, NEG))
    tok = np.arange(TILES)[None, :] * P + np.arange(P)[:, None]
    return {
        "c_ident": np.eye(P, dtype=f),
        "c_upper": (np.arange(P)[:, None] < np.arange(P)[None, :]).astype(f),
        "c_iota": np.concatenate([np.tile(np.arange(P), (P, 1)), tok, np.tile(np.arange(EG, 0, -1), (P, 1)),
                                  np.tile(np.arange(TILES) * P, (P, 1))], axis=1).astype(f),
        "c_cos": np.concatenate([np.cos(ang)] * 2).astype(f),
        "c_sin": np.concatenate([np.sin(ang), -np.sin(ang)]).astype(f),
        "c_band": band.astype(f),
        "c_pair": pair.astype(f),
        "c_smp": np.stack(smp, axis=1).astype(f),
    }


_OUTS = {
    "o_y": (NTOK, D), "o_kT": (HEADS, HD, NTOK), "o_v": (NTOK, HEADS, HD), "o_conv": (P, DK, (CONV - 1) * (1 + DEC_B)),
}
_PLAIN = ["x_prompt", "x_sample", "conv_w_out", "attn_w_o", "expert_w1", "expert_w3", "expert_w2", "cache_k", "cache_v",
          "norm_final", "norm_ffn", "router_group_b", "router_expert_b"]


def kernel(**inputs):
    import numpy as _np
    import concourse.bacc as _bacc
    from concourse import mybir as _mybir
    from concourse.bass_utils import run_bass_kernel_spmd as _run

    x = {k: _np.asarray(v) for k, v in inputs.items()}
    arrays = {k: _np.ascontiguousarray(x[k]) for k in _PLAIN}
    arrays.update(_constants(_np))
    gains = _np.stack([x["norm_mix"][0], x["norm_mix"][1], x["norm_kv"]])
    arrays["gains_col"] = _col(gains, _np)
    arrays["conv_kernel_col"] = _np.ascontiguousarray(_col(x["conv_kernel"][0], _np).transpose(0, 2, 1))
    arrays["state_col"] = _np.ascontiguousarray(_col(x["state_conv"][0], _np).transpose(0, 3, 1, 2))
    w = x["conv_w_in"][0].reshape(DK, P, 3, DK, P)
    arrays["conv_w_in_t"] = _np.ascontiguousarray(w.transpose(3, 1, 0, 2, 4))
    kv = x["attn_w_kv"].reshape(DK, P, 2, HEADS, HD)
    q = x["attn_w_q"][0].reshape(DK, P, GROUPS, HEADS, HD)
    arrays["w_heads"] = _np.ascontiguousarray(_np.concatenate([kv, q], axis=2).transpose(3, 2, 1, 0, 4))
    wr = _np.concatenate([x["router_group_w"], x["router_expert_w"]], axis=2).reshape(2, DK, P, ROUTE)
    arrays["router_w"] = _np.ascontiguousarray(wr.transpose(2, 0, 1, 3))

    nc = _bacc.Bacc("TRN2", target_bir_lowering=False, num_devices=1)
    A = {}
    for name, a in arrays.items():
        A[name] = nc.dram_tensor("in_" + name, a.shape, _mybir.dt.from_np(a.dtype), kind="ExternalInput").ap()
    for name, shape in _OUTS.items():
        A[name] = nc.dram_tensor("out_" + name, shape, _mybir.dt.float32, kind="ExternalOutput").ap()
    A["s_rows"] = nc.dram_tensor("s_rows", (NPAD, D), _mybir.dt.float32).ap()
    A["s_h"] = nc.dram_tensor("s_h", (NPAD, D), _mybir.dt.float32).ap()
    A["s_ys"] = nc.dram_tensor("s_ys", (MBLK * P, D), _mybir.dt.float32).ap()
    A["s_og"] = nc.dram_tensor("s_og", (GROUPS, SEQ, HEADS, HD + 2), _mybir.dt.float32).ap()
    build(nc, A)
    r = _run(nc, [{"in_" + k: v for k, v in arrays.items()}], core_ids=[0]).results[0]
    y, kT, v, cv = (r["out_" + n] for n in ("o_y", "o_kT", "o_v", "o_conv"))
    k = kT.transpose(2, 0, 1)
    cv = _np.ascontiguousarray(cv.transpose(2, 1, 0)).reshape(1, 1 + DEC_B, CONV - 1, D)
    return (
        y[:SEQ].reshape(1, SEQ, D), y[SEQ:].reshape(DEC_B, DEC_S, D),
        _np.ascontiguousarray(k[:SEQ]).reshape(1, SEQ, HEADS, HD), v[:SEQ].reshape(1, SEQ, HEADS, HD),
        cv[:, :1], _np.ascontiguousarray(k[SEQ:]).reshape(DEC_B, DEC_S, HEADS, HD),
        v[SEQ:].reshape(DEC_B, DEC_S, HEADS, HD), cv[:, 1:],
    )
```

```python
import math
from contextlib import ExitStack

import numpy as np
import concourse.bass as bass
from concourse import mybir

F32 = mybir.dt.float32
F32R = mybir.dt.float32r
I32 = mybir.dt.int32
ALU = mybir.AluOpType
ACT = mybir.ActivationFunctionType
AX = mybir.AxisListType

D = 1024
SEQ = 1024
DEC_B, DEC_S = 8, 8
NSMP = DEC_B * DEC_S
NTOK = SEQ + NSMP
P = 128
TILES = (NTOK + P - 1) // P
NPAD = TILES * P
DK = D // P
PAST = 256
WINDOW_KEYS = 128
GROUPS = 3
HEADS = 8
HD = 128
NE = 16
EG = 4
DE = 512
EPS = 1e-6
NEG = -1e30
SCALE = HD ** -0.5
CONV = 3
MBLK = (2 * NTOK + NE * (P - 1)) // P
CHUNKS = [(0, 384), (384, 384), (768, NTOK - 768)]
C2P = SEQ - 768
UW = SEQ + CONV - 1
US = DEC_S + CONV - 1
ROUTE = EG + NE
ONE = 1


def begin(eng, *sems):
    for s in sems:
        for one in s if isinstance(s, list) else [s]:
            eng.sem_inc(one, ONE)


class Chain:

    def __init__(self, eng, sem, base=0):
        self.eng, self.sem, self.base, self.n = eng, sem, base, 0

    def __call__(self, ins):
        self.n += 1
        ins.then_inc(self.sem, 1)
        self.eng.wait_ge(self.sem, self.base + self.n + ONE)


class Ctx:

    def __init__(self, nc, tag=""):
        self.nc, self.stack, self.tag = nc, ExitStack(), tag

    def sb(self, name, shape, dt=F32):
        return self.stack.enter_context(self.nc.sbuf_tensor(self.tag + name, shape, dt))

    def ps(self, name, shape, dt=F32):
        return self.stack.enter_context(self.nc.psum_tensor(self.tag + name, shape, dt))

    def close(self):
        self.stack.close()


def stage_load(nc, G, A, W):
    S = G.sem
    W.x_ready = [S(f"ld_x{u}") for u in range(TILES // 3)]
    W.w_ready, c_ready, zeroed = S("ld_w"), S("ld_const"), S("ld_zeroed")
    with nc.Block() as block:
        @block.sync
        def _(sp):
            begin(sp, W.x_ready, W.w_ready)
            x = A["x_prompt"].rearrange("b (t p) d -> p (b t) d", p=P)
            for u in range(TILES // 3):
                full = min(u * 3 + 3, QT)
                sp.dma_start(G.h[:, u * 3:full, :], x[:, u * 3:full, :]).then_inc(W.x_ready[u], 16)
            sp.dma_start(G.h[0:NSMP, QT, :], A["x_sample"].rearrange("b s d -> (b s) d")).then_inc(W.x_ready[-1], 16)
            sp.dma_start(W.first, A["conv_w_in_t"][0]).then_inc(W.w_ready, 16)

        @block.gpsimd
        def _(pool):
            begin(pool, zeroed)
            pool.memset(G.h[NSMP:P, QT, :], 0.0).then_inc(zeroed, 1)
            pool.wait_ge(zeroed, 1 + ONE)

        @block.scalar
        def _(act):
            begin(act, c_ready)
            act.dma_start(G.ident[:, :], A["c_ident"]).then_inc(c_ready, 16)
            act.dma_start(G.gcol[:, :, :], A["gains_col"]).then_inc(c_ready, 16)
            act.wait_ge(c_ready, 16 * 2 + ONE)


def stage_norm(nc, G, tag, xh, xl, keep=None, W=None, early=None):
    S = G.sem
    squares, var_ok, root_ok, rstd_ok, rows_ok, tr_ok, high_ok, low_ok, kept, w_scaled, w_high = (
        S(f"{tag}_{n}") for n in ("squares", "var", "root", "rstd", "rows", "transposed", "high", "low", "kept",
                                  "w_scaled", "w_high"))
    c = Ctx(nc, tag + "_")
    st = c.sb("stats", [P, 3, TILES])
    rows = c.sb("rows", [P, 3, D])
    SETS = TILES // 3
    junk = c.ps("junk", [P, 2, 512])
    tp = [c.ps(f"tp{u}", [P, DK, P]) for u in range(3)]
    parts = [slice(i * 3, i * 3 + 3) for i in range(SETS)] if W is not None else [slice(0, TILES)]
    with nc.Block() as block:
        if keep is not None:
            @block.sync
            def _(sp):
                to, source, sem = early
                begin(sp, kept, sem)
                sp.dma_start(to, source).then_inc(sem, 16)
                sp.dma_start(keep.rearrange("(t p) d -> p t d", p=P), G.h[:, :, :]).then_inc(kept, 16)
                sp.wait_ge(kept, 16 + ONE)

        if W is not None:
            @block.gpsimd
            def _(pool):
                begin(pool, w_scaled)
                pool.wait_ge(W.w_ready, 16 + ONE)
                g = G.gcol[:, GAIN_MIX0, :].unsqueeze(2).to_broadcast([P, DK, 3 * P])
                flat = W.first.rearrange("p k c n -> p k (c n)")
                pool.tensor_tensor(flat, flat, g, ALU.mult).then_inc(w_scaled, 1)
                pool.wait_ge(w_high, 1 + ONE)
                pool.tensor_tensor(W.wl[:, 0], W.first, W.wh[:, 0].bitcast(F32), ALU.subtract)

        @block.scalar
        def _(act):
            begin(act, squares, root_ok, high_ok, w_high)

            def high_parts(i):
                for u in range(3):
                    t = i * 3 + u
                    act.wait_ge(tr_ok, t + 1 + ONE)
                    act.activation(xh[:, :, t * P:(t + 1) * P], tp[u][:, :, :], ACT.Copy).then_inc(high_ok, 1)

            def root(i):
                act.wait_ge(var_ok, i + 1 + ONE)
                act.activation(st[:, 1, parts[i]], st[:, 0, parts[i]], ACT.Sqrt).then_inc(root_ok, 1)

            if W is None:
                root(0)
            else:
                for i in range(SETS):
                    act.wait_ge(W.x_ready[i], (16 if i < SETS - 1 else 32) + ONE)
                    for t in range(i * 3, i * 3 + 3):
                        if t >= 1:
                            act.wait_ge(squares, t + ONE)
                        act.activation(junk[:, :, :].rearrange("p a n -> p (a n)"), G.h[:, t, :], ACT.Square,
                                       accum_out=G.ssq[:, t:t + 1]).then_inc(squares, 1)
                    root(i)
                    if i == 1:
                        high_parts(0)
                act.wait_ge(w_scaled, 1 + ONE)
            for i in range(1 if W is not None else 0, SETS):
                if W is not None and i == 1:
                    act.activation(W.wh[:, 0], W.first, ACT.Copy).then_inc(w_high, 1)
                high_parts(i)

        @block.vector
        def _(dve):
            begin(dve, var_ok, rstd_ok, rows_ok, low_ok)

            def statistics(i):
                if W is not None:
                    dve.wait_ge(squares, parts[i].stop + ONE)
                dve.tensor_scalar(st[:, 0, parts[i]], G.ssq[:, parts[i]], 1.0 / D, EPS, ALU.mult, ALU.add).then_inc(var_ok, 1)
                dve.wait_ge(root_ok, i + 1 + ONE)
                dve.reciprocal(st[:, 2, parts[i]], st[:, 1, parts[i]]).then_inc(rstd_ok, 1)
                dve.wait_ge(rstd_ok, i + 1 + ONE)

            def low_part(t):
                dve.wait_ge(high_ok, t + 1 + ONE)
                dve.tensor_tensor(xl[:, :, t * P:(t + 1) * P], tp[t % 3][:, :, :], xh[:, :, t * P:(t + 1) * P].bitcast(F32),
                                  ALU.subtract).then_inc(low_ok, 1)

            for i in range(SETS):
                if i < len(parts):
                    statistics(i)
                for u in range(3):
                    t = i * 3 + u
                    if i >= 1:
                        dve.wait_ge(tr_ok, t - 2 + ONE)
                    dve.tensor_scalar(rows[:, u, :], G.h[:, t, :], st[:, 2, t:t + 1], None, ALU.mult).then_inc(rows_ok, 1)
                    if i >= 1:
                        low_part(t - 3)
            for t in range(TILES - 3, TILES):
                low_part(t)

        @block.tensor
        def _(pe):
            begin(pe, tr_ok)

            def transposes(t, u):
                pe.wait_ge(rows_ok, t + 1 + ONE)
                for k in range(DK):
                    mm = pe.transpose(tp[u][:, k, :], rows[:, u, k * P:(k + 1) * P], G.ident[:, :])
                mm.then_inc(tr_ok, 1)

            for u in range(3):
                transposes(u, u)
            with pe.Fori(0, TILES // 3 - 1) as i:
                for u in range(3):
                    pe.wait_ge(low_ok, i * 3 + u + 1 + ONE)
                    transposes(i * 3 + u + 3, u)
    c.close()


def stage_conv(nc, G, A, xh, xl, W, zT, w_out):
    S = G.sem
    w_ready = [S(f"cv_w_ready{u}") for u in range(2)]
    cb_ok, u_ok = ([S(f"cv_{n}{v}") for v in range(2)] for n in ("copied", "gated"))
    small_ready, scaled, high_ok, low_ok, prod_ok, chain, last_ok, stored, zero_ok, z_ok = (S("cv_" + n) for n in (
        "small_ready", "w_scaled", "w_high", "w_low", "product", "chain", "last", "stored", "zeroed", "z"))
    c = Ctx(nc, "cv_")
    flat_h = G.h[:, :, :].rearrange("p t d -> p (t d)")
    SLICE = DK * 3 * P
    UB = UW + DEC_B * US
    assert 2 * (SLICE + UB) <= TILES * D
    raw = [flat_h[:, u * SLICE:(u + 1) * SLICE].rearrange("p (k c n) -> p k c n", k=DK, c=3) for u in range(2)]
    ub = flat_h[:, 2 * SLICE:2 * (SLICE + UB)].rearrange("p (u n) -> p u n", u=2)
    wh, wl = W.wh, W.wl
    kc = c.sb("kc", [P, DK, CONV])
    hist = c.sb("hist", [P, DK, DEC_B, CONV - 1])
    csb = c.sb("csb", [P, 2, 384])
    acc = c.sb("acc", [P, NTOK])
    last = c.sb("last", [P, DK, (CONV - 1) * (1 + DEC_B)])
    pp = [[c.ps(f"pp{part}{v}", [P, 512]) for v in range(2)] for part in range(3)]
    NC = len(CHUNKS)

    def hist_view(u):
        return ub[:, u, UW:].rearrange("p (b s) -> p b s", s=US)

    with nc.Block() as block:
        @block.sync
        def _(sp):
            begin(sp, small_ready, w_ready, stored, w_out.ready)

            def load(f, u):
                sp.dma_start(raw[u], A["conv_w_in_t"][bass.ds(f, 1)].rearrange("a p k c n -> p (a k) c n"))\
                    .then_inc(w_ready[u], 16)

            load(1, 1)
            sp.dma_start(kc[:, :, :], A["conv_kernel_col"]).then_inc(small_ready, 16)
            sp.dma_start(hist[:, :, :, :], A["state_col"]).then_inc(small_ready, 16)
            load(2, 0)
            with sp.Fori(0, DK // 2 - 2) as i:
                for u in (1, 0):
                    f = i * 2 + (1 if u else 2)
                    sp.wait_ge(low_ok, f + ONE)
                    load(f + 2, u)
            sp.wait_ge(low_ok, DK - 3 + ONE)
            load(DK - 1, 1)
            sp.wait_ge(low_ok, DK - 2 + ONE)
            n = w_out.early // 2
            for u in range(2):
                if u:
                    sp.wait_ge(low_ok, DK - 1 + ONE)
                sp.dma_start(w_out.raw[:, u * n:(u + 1) * n, :], w_out.dram[:, u * n:(u + 1) * n, :]).then_inc(w_out.ready, 16)
            sp.wait_ge(last_ok, DK + ONE)
            sp.dma_start(A["o_conv"], last[:, :, :]).then_inc(stored, 16)
            sp.wait_ge(stored, 16 + ONE)

        @block.gpsimd
        def _(pool):
            begin(pool, zero_ok, scaled, low_ok)
            pool.memset(ub[:, :, 0:CONV - 1], 0.0).then_inc(zero_ok, 1)
            pool.wait_ge(zero_ok, 1 + ONE)
            pool.memset(zT[:, :, NTOK:], 0.0).then_inc(zero_ok, 1)
            g = G.gcol[:, GAIN_MIX0, :].unsqueeze(2).to_broadcast([P, DK, 3 * P])

            def prepare(f, u, turn):
                flat = raw[u].rearrange("p k c n -> p k (c n)")
                pool.wait_ge(w_ready[u], turn * 16 + 16 + ONE)
                pool.wait_ge(low_ok, f - 1 + ONE)
                pool.tensor_tensor(flat, flat, g, ALU.mult).then_inc(scaled, 1)
                pool.wait_ge(high_ok, f + ONE)
                pool.tensor_tensor(wl[:, u], raw[u], wh[:, u].bitcast(F32), ALU.subtract).then_inc(low_ok, 1)

            pool.wait_ge(zero_ok, 2 + ONE)
            with pool.Fori(0, DK // 2 - 1) as i:
                prepare(i * 2 + 1, 1, i)
                prepare(i * 2 + 2, 0, i)
            prepare(DK - 1, 1, DK // 2 - 1)

        @block.tensor
        def _(pe):
            begin(pe, prod_ok)
            with pe.Fori(0, DK // 2) as i:
                for u in range(2):
                    pe.wait_ge(low_ok, i * 2 + u + ONE)
                    for n, (c0, cn) in enumerate(CHUNKS):
                        m = u * NC + n
                        pe.wait_ge(cb_ok[m % 2], i * NC + m // 2 + ONE)
                        pe.wait_ge(u_ok[m % 2], i * NC + m // 2 + ONE)
                        for part in range(3):
                            for k in range(DK):
                                for q, (w, x) in enumerate(((wh, xh), (wh, xl), (wl, xh))):
                                    mm = pe.matmul(pp[part][m % 2][:, 0:cn], w[:, u, k, part, :], x[:, k, c0:c0 + cn],
                                                   start=(k == 0 and q == 0), stop=(k == DK - 1 and q == 2))
                        mm.then_inc(prod_ok, 1)

        @block.scalar
        def _(act):
            begin(act, cb_ok, high_ok)

            def high_part(f, u):
                act.wait_ge(scaled, f + ONE)
                act.activation(wh[:, u], raw[u], ACT.Copy).then_inc(high_ok, 1)

            def copies(i, u, n, c0, cn):
                m = u * NC + n
                act.wait_ge(prod_ok, i * (2 * NC) + m + 1 + ONE)
                act.wait_ge(u_ok[m % 2], i * NC + m // 2 + ONE)
                act.activation(zT[:, bass.ds(i * 2 + u, 1), c0:c0 + cn].rearrange("p a n -> p (a n)"), pp[1][m % 2][:, 0:cn],
                               ACT.Copy)
                act.activation(csb[:, m % 2, 0:cn], pp[0][m % 2][:, 0:cn], ACT.Copy).then_inc(cb_ok[m % 2], 1)

            def tile(i, u):
                for n, (c0, cn) in enumerate(CHUNKS):
                    copies(i, u, n, c0, cn)

            high_part(1, 1)
            with act.Fori(0, DK // 2 - 1) as i:
                tile(i, 0)
                high_part(i * 2 + 2, 0)
                tile(i, 1)
                high_part(i * 2 + 3, 1)
            tile(DK // 2 - 1, 0)
            tile(DK // 2 - 1, 1)

        @block.vector
        def _(dve):
            begin(dve, u_ok, last_ok, z_ok, chain)
            dve.wait_ge(small_ready, 32 + ONE)
            dve.wait_ge(zero_ok, 2 + ONE)
            LINKS = 2 * CONV
            with dve.Fori(0, DK // 2) as i:
                for u in range(2):
                    f = i * 2 + u
                    link = Chain(dve, chain, f * LINKS)
                    dve.tensor_copy(hist_view(u)[:, :, 0:CONV - 1],
                                    hist[:, bass.ds(f, 1), :, :].rearrange("p a b s -> p (a b) s"))
                    for n, (c0, cn) in enumerate(CHUNKS):
                        m = u * NC + n
                        dve.wait_ge(cb_ok[m % 2], i * NC + m // 2 + 1 + ONE)
                        q, cs = pp[2][m % 2], csb[:, m % 2, :]
                        w = cn if n < NC - 1 else C2P
                        up = dve.tensor_tensor(ub[:, u, CONV - 1 + c0:CONV - 1 + c0 + w], q[:, 0:w], cs[:, 0:w], ALU.mult)
                        if n == NC - 1:
                            up = dve.tensor_tensor(hist_view(u)[:, :, CONV - 1:],
                                                   q[:, w:cn].rearrange("p (b s) -> p b s", s=DEC_S),
                                                   cs[:, w:cn].rearrange("p (b s) -> p b s", s=DEC_S), ALU.mult)
                        up.then_inc(u_ok[m % 2], 1)
                    dve.wait_ge(u_ok[m % 2], i * NC + m // 2 + 1 + ONE)
                    dve.tensor_copy(last[:, bass.ds(f, 1), 0:CONV - 1], ub[:, u, SEQ:UW])
                    dve.tensor_copy(last[:, bass.ds(f, 1), CONV - 1:].rearrange("p a (b s) -> p (a b) s", s=CONV - 1),
                                    hist_view(u)[:, :, DEC_S:]).then_inc(last_ok, 1)
                    for j in range(CONV):
                        k = kc[:, bass.ds(f, 1), j]
                        for src, dst in (
                            (ub[:, u, j:j + SEQ], acc[:, 0:SEQ]),
                            (hist_view(u)[:, :, j:j + DEC_S], acc[:, SEQ:].rearrange("p (b s) -> p b s", s=DEC_S)),
                        ):
                            if j == 0:
                                op = dve.tensor_scalar(dst, src, k, None, ALU.mult)
                            else:
                                op = dve.scalar_tensor_tensor(out=dst, in0=src, scalar=k, in1=dst,
                                                              op0=ALU.mult, op1=ALU.add)
                            link(op)
                    assert link.n == LINKS
                    z = zT[:, bass.ds(f, 1), 0:NTOK].rearrange("p a n -> p (a n)")
                    dve.tensor_tensor(z, acc[:, :], z, ALU.mult).then_inc(z_ok, 1)
    c.close()


def stage_project(nc, G, A, tag, zT, w):
    S = G.sem
    wl_ok = [S(f"{tag}_w_low_{who}") for who in ("vector", "pool")]
    rest, wh_ok, zh_ok, zl_ok, prod, added, sq, zeroed = (S(f"{tag}_{n}") for n in (
        "rest", "w_high", "z_high", "z_low", "product", "added", "squares", "zeroed"))
    x_ready = S(f"{tag}_x_ready")
    c = Ctx(nc, tag + "_")
    wh = c.sb("wh", [P, DK, D], F32R)
    wl = c.sb("wl", [P, DK, D], F32R)
    zh = c.sb("zh", [P, 3, DK, P], F32R)
    zl = c.sb("zl", [P, 3, DK, P], F32R)
    junk = c.sb("junk", [P, D])
    py = [c.ps(f"py{u}", [P, 2, 512]) for u in range(3)]
    with nc.Block() as block:
        @block.sync
        def _(sp):
            begin(sp, rest, x_ready)
            sp.dma_start(w.raw[:, w.early:, :], w.dram[:, w.early:, :]).then_inc(rest, 16)
            for who in range(2):
                sp.wait_ge(wl_ok[who], DK // 2 + ONE)
            sp.dma_start(G.h[:, 0:QT, :], A["x_prompt"].rearrange("b (t p) d -> p (b t) d", p=P)).then_inc(x_ready, 16)
            sp.dma_start(G.h[0:NSMP, QT, :], A["x_sample"].rearrange("b s d -> (b s) d")).then_inc(x_ready, 16)

        @block.gpsimd
        def _(pool):
            begin(pool, wl_ok[1], zeroed)
            for k in range(1, DK, 2):
                pool.wait_ge(wh_ok, k + 1 + ONE)
                pool.tensor_tensor(wl[:, k, :], w.raw[:, k, :], wh[:, k, :].bitcast(F32), ALU.subtract).then_inc(wl_ok[1], 1)
                pool.wait_ge(wl_ok[1], k // 2 + 1 + ONE)
            pool.memset(G.h[NSMP:P, QT, :], 0.0).then_inc(zeroed, 1)

        @block.tensor
        def _(pe):
            begin(pe, prod)

            def project(t, u):
                pe.wait_ge(zl_ok, t + 1 + ONE)
                for half in range(2):
                    cols = slice(half * 512, (half + 1) * 512)
                    for k in range(DK):
                        if half == 0:
                            pe.wait_ge(wl_ok[k % 2], k // 2 + 1 + ONE)
                        for q, (a, b) in enumerate(((zh, wh), (zl, wh), (zh, wl))):
                            mm = pe.matmul(py[u][:, half, :], a[:, u, k, :], b[:, k, cols],
                                           start=(k == 0 and q == 0), stop=(k == DK - 1 and q == 2))
                mm.then_inc(prod, 1)

            for u in range(3):
                project(u, u)
            with pe.Fori(0, TILES // 3 - 1) as i:
                for u in range(3):
                    pe.wait_ge(added, i * 3 + u + 1 + ONE)
                    project(i * 3 + u + 3, u)

        @block.vector
        def _(dve):
            begin(dve, added, zl_ok, wl_ok[0])

            def low_part(t, u):
                dve.wait_ge(zh_ok, t + 1 + ONE)
                dve.tensor_tensor(zl[:, u], zT[:, :, bass.ds(t * P, P)], zh[:, u].bitcast(F32), ALU.subtract).then_inc(zl_ok, 1)

            def finish(t, u):
                dve.wait_ge(prod, t + 1 + ONE)
                row = G.h[:, bass.ds(t, 1), :].rearrange("p a d -> p (a d)")
                dve.tensor_tensor(row, py[u][:, :, :].rearrange("p a n -> p (a n)"), row, ALU.add).then_inc(added, 1)

            low_part(0, 0)
            for k in range(0, DK, 2):
                dve.wait_ge(wh_ok, k + 1 + ONE)
                dve.tensor_tensor(wl[:, k, :], w.raw[:, k, :], wh[:, k, :].bitcast(F32), ALU.subtract).then_inc(wl_ok[0], 1)
            for u in range(1, 3):
                low_part(u, u)
            dve.wait_ge(x_ready, 32 + ONE)
            dve.wait_ge(zeroed, 1 + ONE)
            with dve.Fori(0, TILES // 3 - 1) as i:
                for u in range(3):
                    finish(i * 3 + u, u)
                    low_part(i * 3 + u + 3, u)
            for t in range(TILES - 3, TILES):
                finish(t, t % 3)

        @block.scalar
        def _(act):
            begin(act, wh_ok, zh_ok, sq)

            def high_part(t, u):
                act.activation(zh[:, u], zT[:, :, bass.ds(t * P, P)], ACT.Copy).then_inc(zh_ok, 1)

            def square(t):
                act.wait_ge(added, t + 1 + ONE)
                act.wait_ge(sq, t + ONE)
                act.activation(junk[:, :], G.h[:, bass.ds(t, 1), :], ACT.Square,
                               accum_out=G.ssq[:, bass.ds(t, 1)]).then_inc(sq, 1)

            high_part(0, 0)
            act.wait_ge(w.ready, 32 + ONE)
            for k in range(DK):
                if k == w.early:
                    act.wait_ge(rest, 16 + ONE)
                act.activation(wh[:, k, :], w.raw[:, k, :], ACT.Copy).then_inc(wh_ok, 1)
            for u in range(1, 3):
                high_part(u, u)
            with act.Fori(0, TILES // 3 - 1) as i:
                for u in range(3):
                    act.wait_ge(prod, i * 3 + u + 1 + ONE)
                    high_part(i * 3 + u + 3, u)
                    square(i * 3 + u)
            for t in range(TILES - 3, TILES):
                square(t)
    c.close()


def expert_weights(A, layer, m):
    return A[("expert_w1", "expert_w3", "expert_w2")[m]][layer].rearrange("e (k p) n -> e p k n", p=P)


def halves(m, half):
    n = (DK, DK, DE // P)[m] // 2
    return slice(half * n, (half + 1) * n)


def stage_route(nc, G, A, tag, layer, R):
    S = G.sem
    scaled, gain_ready = S(f"{tag}_scaled"), S(f"{tag}_gain_ready")
    (var_ok, root_ok, rstd_ok, rows_ok, tr_ok, xt_ok, small_ready, logit_ok, bias_ok, chain, exp_in, exp_ok, both_ok,
     count_ok, hot_ok, tok_ok) = (S(f"{tag}_{n}") for n in (
         "var", "root", "rstd", "rows", "transposed", "xt", "small_ready", "logits", "biased", "chain", "exp_in",
         "exp", "both", "counted", "one_hot", "slot_tok"))
    stored = [S(f"{tag}_stored{u}") for u in range(3)]
    piece = S(f"{tag}_w_low_half")
    c = Ctx(nc, tag + "_")
    st = c.sb("stats", [P, 3, TILES])
    rows = c.sb("rows", [P, 3, D])
    xt = c.sb("xt", [P, 3, DK, P])
    wr = c.sb("wr", [P, DK, ROUTE])
    bias = c.sb("bias", [P, ROUTE])
    gain = c.sb("gain", [P, D])
    lg = c.sb("logits", [P, TILES, ROUTE])
    tp = [c.ps(f"tp{u}", [P, DK, P]) for u in range(3)]
    pl = [c.ps(f"pl{u}", [P, 512]) for u in range(2)]

    T = TILES
    e4 = c.sb("e4", [P, 6, T, EG])
    group, pick1, pick2, l4, l4b, tmp4 = (e4[:, n] for n in range(6))
    col = c.sb("col", [P, 8, T])
    m, s, m1, m2, ge, gp, r, e2 = (col[:, n] for n in range(8))
    big = c.sb("big", [P, 5, T, NE])
    sel, hot1, hot2, both, slots = (big[:, n] for n in range(5))
    pre = c.sb("pre", [P, T + 1, NE])
    tot = c.sb("tot", [P, T, NE])
    exp_t = c.sb("exp_t", [P, 2, T, EG])
    ex = c.sb("ex", [P, 4, NE])
    nb, ends, base, one16 = (ex[:, n] for n in range(4))
    cmp9 = c.sb("cmp9", [P, NE, T])
    cmpb = c.sb("cmpb", [P, MBLK + 1, NE])
    bef = c.sb("bef", [P, MBLK + 1])
    slotf = c.sb("slotf", [P, 2, T])
    part_i = c.sb("part_i", [P, 2, 2, T], I32)
    part_f = c.sb("part_f", [P, 2, 2, T])
    assert NPAD < 2 ** 12
    hr = c.sb("hr", [P, 2, P], F32R)
    hb = c.sb("hb", [P, 2, MBLK], F32R)
    upper = c.sb("upper", [P, P])
    ones = c.sb("ones", [P, P])
    iota = c.sb("iota", [P, IOTA_COLS])
    desc = iota[:, P + T:P + T + EG].unsqueeze(1).to_broadcast([P, T, EG])
    steps = iota[:, P + T + EG:P + 2 * T + EG].unsqueeze(1).to_broadcast([P, NE, T])

    def b4(x):
        return x.unsqueeze(2).to_broadcast([P, T, EG])

    with nc.Block() as block:
        @block.sync
        def _(sp):
            begin(sp, gain_ready, small_ready, stored, R.raw_ready)
            sp.dma_start(gain[:, :], A["norm_ffn"][layer, :].partition_broadcast(P)).then_inc(gain_ready, 16)
            sp.dma_start(wr[:, :, :], A["router_w"][:, layer]).then_inc(small_ready, 16)
            sp.dma_start(bias[:, 0:EG], A["router_group_b"][layer, :].partition_broadcast(P)).then_inc(small_ready, 16)
            sp.dma_start(bias[:, EG:], A["router_expert_b"][layer, :].partition_broadcast(P)).then_inc(small_ready, 16)
            sp.dma_start(upper[:, :], A["c_upper"]).then_inc(small_ready, 16)
            sp.dma_start(iota[:, :], A["c_iota"]).then_inc(small_ready, 16)
            with sp.Fori(0, T // 3) as i:
                for u in range(3):
                    sp.wait_ge(rows_ok, i * 3 + u + 1 + ONE)
                    sp.dma_start(A["s_rows"][bass.ds((i * 3 + u) * P, P), :], rows[:, u, :]).then_inc(stored[u], 16)
            for m in range(3):
                sp.dma_start(R.raw[m][:, :, :], expert_weights(A, layer, m)[0]).then_inc(R.raw_ready[m], 16)
            for m in range(2):
                sp.wait_ge(R.lo_ok[m], 1 + ONE)
                sp.dma_start(R.raw[m][:, :, :], expert_weights(A, layer, m)[1]).then_inc(R.raw_ready[m], 16)
            for u in range(3):
                sp.wait_ge(stored[u], 16 * (T // 3) + ONE)

        @block.scalar
        def _(act):
            begin(act, root_ok, exp_ok, xt_ok, R.hi_ok)
            act.wait_ge(var_ok, 1 + ONE)
            act.activation(st[:, 1, :], st[:, 0, :], ACT.Sqrt).then_inc(root_ok, 1)

            def copy_out(t, u):
                act.wait_ge(tr_ok, t + 1 + ONE)
                act.activation(xt[:, u], tp[u][:, :, :], ACT.Copy).then_inc(xt_ok, 1)

            for u in range(3):
                copy_out(u, u)
            with act.Fori(0, T // 3 - 1) as i:
                for u in range(3):
                    act.wait_ge(logit_ok, i * 3 + u + 1 + ONE)
                    copy_out(i * 3 + u + 3, u)
            def high(m):
                act.wait_ge(R.raw_ready[m], 16 + ONE)
                for half in range(2):
                    k = halves(m, half)
                    act.activation(R.wh[m][:, k, :], R.raw[m][:, k, :], ACT.Copy).then_inc(R.hi_ok[m], 1)

            high(0)
            act.wait_ge(exp_in, 1 + ONE)
            act.activation(exp_t[:, 1], exp_t[:, 0], ACT.Exp).then_inc(exp_ok, 1)
            act.wait_ge(exp_in, 2 + ONE)
            act.activation(e2, ge, ACT.Exp).then_inc(exp_ok, 1)
            high(1)

        @block.gpsimd
        def _(pool):
            begin(pool, R.lo_ok, piece)
            for m in range(2):
                for half in range(2):
                    k = halves(m, half)
                    pool.wait_ge(R.hi_ok[m], half + 1 + ONE)
                    op = pool.tensor_tensor(R.wl[m][:, k, :], R.raw[m][:, k, :], R.wh[m][:, k, :].bitcast(F32), ALU.subtract)
                    if half == 0:
                        op.then_inc(piece, 1)
                        pool.wait_ge(piece, m + 1 + ONE)
                    else:
                        op.then_inc(R.lo_ok[m], 1)
                        if m == 0:
                            pool.wait_ge(R.lo_ok[m], 1 + ONE)

        @block.tensor
        def _(pe):
            begin(pe, tr_ok, logit_ok, count_ok, tok_ok)
            pe.wait_ge(small_ready, 16 * 5 + ONE)

            def transposes(t, u):
                pe.wait_ge(rows_ok, t + 1 + ONE)
                for k in range(DK):
                    mm = pe.transpose(tp[u][:, k, :], rows[:, u, k * P:(k + 1) * P], G.ident[:, :])
                mm.then_inc(tr_ok, 1)

            def logits(t, u):
                pe.wait_ge(xt_ok, t + 1 + ONE)
                pe.wait_ge(bias_ok, t + ONE)
                for k in range(DK):
                    mm = pe.matmul(pl[0][:, 0:ROUTE], xt[:, u, k, :], wr[:, k, :], start=(k == 0), stop=(k == DK - 1))
                mm.then_inc(logit_ok, 1)

            transposes(0, 0)
            with pe.Fori(0, T // 3 - 1) as i:
                for u in range(3):
                    transposes(i * 3 + u + 1, (u + 1) % 3)
                    logits(i * 3 + u, u)
            for t in range(T - 3, T):
                if t + 1 < T:
                    transposes(t + 1, (t + 1) % 3)
                logits(t, t % 3)
            pe.wait_ge(both_ok, 1 + ONE)
            pe.matmul(pl[0][:, 0:T * NE], upper[:, :], both.rearrange("p t e -> p (t e)"), start=True, stop=True)
            pe.matmul(pl[1][:, 0:T * NE], ones[:, :], both.rearrange("p t e -> p (t e)"), start=True, stop=True)\
                .then_inc(count_ok, 1)
            n = 0
            for t in range(T):
                rows_in = P if t < T - 1 else NTOK - P * (T - 1)
                for k in range(2):
                    pe.wait_ge(hot_ok, n + 1 + ONE)
                    mm = pe.matmul(pl[1][:, 256:256 + MBLK], hr[0:rows_in, n % 2, :], hb[0:rows_in, n % 2, :],
                                   start=(n == 0), stop=(n == 2 * T - 1))
                    mm.then_inc(tok_ok, 1)
                    n += 1

        @block.vector
        def _(dve):
            dve.memset(ones[:, :], 1.0)
            begin(dve, var_ok, rstd_ok, rows_ok, scaled, bias_ok, exp_in, both_ok, hot_ok, chain)
            dve.tensor_scalar(st[:, 0, :], G.ssq[:, :], 1.0 / D, EPS, ALU.mult, ALU.add).then_inc(var_ok, 1)
            dve.wait_ge(root_ok, 1 + ONE)
            dve.reciprocal(st[:, 2, :], st[:, 1, :]).then_inc(rstd_ok, 1)
            dve.wait_ge(rstd_ok, 1 + ONE)
            def scale_rows(t, u):
                dve.tensor_scalar(rows[:, u, :], G.h[:, bass.ds(t, 1), :].rearrange("p a d -> p (a d)"),
                                  st[:, 2, bass.ds(t, 1)], None, ALU.mult).then_inc(scaled, 1)
                dve.wait_ge(scaled, t + 1 + ONE)
                dve.tensor_tensor(rows[:, u, :], rows[:, u, :], gain[:, :], ALU.mult).then_inc(rows_ok, 1)

            def add_bias(t):
                dve.wait_ge(logit_ok, t + 1 + ONE)
                dve.tensor_tensor(lg[:, bass.ds(t, 1), :].rearrange("p a n -> p (a n)"), pl[0][:, 0:ROUTE],
                                  bias[:, :], ALU.add).then_inc(bias_ok, 1)

            dve.wait_ge(gain_ready, 16 + ONE)
            for u in range(3):
                scale_rows(u, u)
            dve.wait_ge(small_ready, 16 * 5 + ONE)
            with dve.Fori(0, T // 3 - 1) as i:
                for u in range(3):
                    dve.wait_ge(tr_ok, i * 3 + u + 1 + ONE)
                    dve.wait_ge(stored[u], i * 16 + 16 + ONE)
                    scale_rows(i * 3 + u + 3, u)
                    add_bias(i * 3 + u)
            for t in range(T - 3, T):
                add_bias(t)
            dve.wait_ge(bias_ok, T + ONE)
            link = Chain(dve, chain)

            def tt(out, a, b, op):
                link(dve.tensor_tensor(out, a, b, op))

            def first_max(logits, top, hot):
                link(dve.tensor_reduce(top, logits, AX.X, ALU.max))
                tt(hot, logits, b4(top), ALU.is_equal)
                tt(hot, hot, desc, ALU.mult)
                link(dve.tensor_reduce(s, hot, AX.X, ALU.max))
                tt(hot, hot, b4(s), ALU.is_equal)

            grp = lg[:, :, 0:EG]
            first_max(grp, m, group)
            dve.tensor_tensor(exp_t[:, 0], grp, b4(m), ALU.subtract).then_inc(exp_in, 1)
            lexp = lg[:, :, EG:].rearrange("p t (g j) -> p t g j", j=EG)
            hot_g = group.unsqueeze(3).to_broadcast([P, T, EG, EG])
            sel4 = sel.rearrange("p t (g j) -> p t g j", j=EG)
            tt(sel4, lexp, hot_g, ALU.mult)
            link(dve.tensor_reduce(l4, sel4.rearrange("p t g j -> p t j g"), AX.X, ALU.add))
            first_max(l4, m1, pick1)
            link(dve.scalar_tensor_tensor(out=l4b, in0=pick1, scalar=NEG, in1=l4, op0=ALU.mult, op1=ALU.add))
            first_max(l4b, m2, pick2)
            dve.tensor_tensor(ge, m2, m1, ALU.subtract).then_inc(exp_in, 1)
            for hot, pick in ((hot1, pick1), (hot2, pick2)):
                tt(hot.rearrange("p t (g j) -> p t g j", j=EG), hot_g,
                   pick.unsqueeze(2).to_broadcast([P, T, EG, EG]), ALU.mult)
            tt(both, hot1, hot2, ALU.add)
            dve.memset(both[NTOK - P * (T - 1):, T - 1:T, :], 0.0).then_inc(both_ok, 1)
            dve.wait_ge(exp_ok, 2 + ONE)
            link(dve.tensor_reduce(s, exp_t[:, 1], AX.X, ALU.add))
            link(dve.reciprocal(gp, s))
            link(dve.tensor_scalar(r, e2, 1.0, None, ALU.add))
            link(dve.reciprocal(r, r))
            tt(R.gates[:, 0], gp, r, ALU.mult)
            tt(R.gates[:, 1], R.gates[:, 0], e2, ALU.mult)
            dve.wait_ge(count_ok, 1 + ONE)
            link(dve.tensor_copy(tot.rearrange("p t e -> p (t e)"), pl[1][:, 0:T * NE]))
            link(dve.memset(pre[:, 0], 0.0))
            for t in range(T):
                tt(pre[:, t + 1], pre[:, t], tot[:, t], ALU.add)
            tt(cmp9[:, :, :], pre[:, T].unsqueeze(2).to_broadcast([P, NE, T]), steps, ALU.is_gt)
            link(dve.tensor_reduce(nb, cmp9[:, :, :], AX.X, ALU.add))
            link(dve.tensor_scalar(nb, nb, 1.0, None, ALU.max))
            link(dve.memset(one16, 1.0))
            link(dve.tensor_tensor_scan(ends, one16, nb, 0.0, ALU.mult, ALU.add))
            tt(base, ends, nb, ALU.subtract)
            link(dve.tensor_scalar(base, base, float(P), None, ALU.mult))
            tt(slots, pl[0][:, 0:T * NE].rearrange("p (t e) -> p t e", e=NE), pre[:, 0:T], ALU.add)
            tt(slots, slots, base.unsqueeze(1).to_broadcast([P, T, NE]), ALU.add)
            for k, hot in enumerate((hot1, hot2)):
                tt(sel, slots, hot, ALU.mult)
                link(dve.tensor_reduce(slotf[:, k], sel, AX.X, ALU.add))
            link(dve.tensor_copy(R.slot[:, :, :], slotf[:, :, :]))
            link(dve.tensor_scalar(part_i[:, 0], R.slot[:, :, :], 7, None, ALU.logical_shift_right))
            link(dve.tensor_scalar(part_i[:, 1], R.slot[:, :, :], P - 1, None, ALU.bitwise_and))
            link(dve.tensor_copy(part_f.rearrange("p a k t -> p (a k t)"), part_i.rearrange("p a k t -> p (a k t)")))
            tt(cmpb[:, :, :], ends.unsqueeze(1).to_broadcast([P, MBLK + 1, NE]),
               iota[:, 0:MBLK + 1].unsqueeze(2).to_broadcast([P, MBLK + 1, NE]), ALU.is_le)
            link(dve.tensor_reduce(bef[:, :], cmpb[:, :, :], AX.X, ALU.add))
            link(dve.tensor_scalar(R.block_expert[:, :], bef[:, :], float(NE - 1), None, ALU.min))
            link(dve.tensor_scalar(R.last[:, :], ends[:, NE - 1:NE], -1.0, None, ALU.add))
            link(dve.memset(R.slot_tok[:, MBLK:], 0))
            n = 0
            for t in range(T):
                for k in range(2):
                    if n >= 2:
                        dve.wait_ge(tok_ok, n - 1 + ONE)
                    dve.tensor_scalar(hr[:, n % 2, :], iota[:, 0:P], part_f[:, 1, k, t:t + 1], None, ALU.is_equal)
                    dve.tensor_scalar(hb[:, n % 2, :], iota[:, 0:MBLK], part_f[:, 0, k, t:t + 1],
                                      iota[:, P + t:P + t + 1], ALU.is_equal, ALU.mult).then_inc(hot_ok, 1)
                    n += 1
            dve.wait_ge(tok_ok, 2 * T + ONE)
            link(dve.tensor_copy(R.slot_tok[:, 0:MBLK], pl[1][:, 256:256 + MBLK]))
    c.close()


def stage_experts(nc, G, A, tag, layer, R):
    S = G.sem
    hi_ok = R.hi_ok + [S(f"{tag}_w2_high")]
    lo_ok = R.lo_ok + [S(f"{tag}_w2_low")]
    xg_ok = S(f"{tag}_x_rows")
    (blank, zero_ok, passed, index_ok, gathered, xt_ps, xh_ok, xl_ok, a_ok, b_ok, silu_ok, hid_ok, hid_ps, hh_ok, hl_ok,
     y_ok, ys_ok, stored) = (S(f"{tag}_{n}") for n in (
         "blank", "zero", "passed", "index", "gathered", "x_transposed", "x_high", "x_low", "w1_product", "w3_product",
         "silu", "hidden", "hidden_transposed", "hidden_high", "hidden_low", "w2_product", "rows", "stored"))
    passed_end = S(f"{tag}_passed_end")
    c = Ctx(nc, tag + "_")
    HK = DE // P
    raw, raw_ready = R.raw, R.raw_ready
    wh = R.wh + [c.sb("wh_w2", [P, HK, D], F32R)]
    wl = R.wl + [c.sb("wl_w2", [P, HK, D], F32R)]
    zero = c.sb("zero", [P, 64])
    idx = c.sb("idx", [P, 1], I32)
    xn = c.sb("xn", [P, D])
    xg = c.sb("xg", [P, D])
    xh = c.sb("xh", [P, DK, P], F32R)
    xl = c.sb("xl", [P, DK, P], F32R)
    hid = c.sb("hid", [P, DE])
    hh = c.sb("hh", [P, HK, P], F32R)
    hl = c.sb("hl", [P, HK, P], F32R)
    ys = c.sb("ys", [P, D])
    tp = c.ps("tp", [P, DK, P])
    pa = c.ps("pa", [P, DE])
    pb = c.ps("pb", [P, DE])
    ph = c.ps("ph", [P, HK, P])
    py = c.ps("py", [P, 2, 512])

    def last_block(eng):
        return eng.value_load(R.last[0:1, 0:1], min_val=NE - 1, max_val=MBLK - 1)

    def expert_of(eng, b):
        return eng.value_load(R.block_expert[0:1, bass.ds(b, 1)], min_val=0, max_val=NE - 1)

    with nc.Block() as block:
        @block.sync
        def _(sp):
            begin(sp, blank)
            def load(m, e):
                sp.wait_ge(lo_ok[m], e + ONE)
                sp.dma_start(raw[m][:, :, :], expert_weights(A, layer, m)[bass.ds(e, 1)]
                             .rearrange("a p k n -> p (a k) n")).then_inc(raw_ready[m], 16)

            with sp.Fori(2, NE) as e:
                load(0, e)
                load(1, e)
                load(2, e - 1)
            load(2, NE - 1)
            sp.wait_ge(zero_ok, 1 + ONE)
            last = last_block(sp)
            with sp.Fori(NE, MBLK) as b:
                sp.dma_start(A["s_ys"][bass.ds(b * P, P), :].rearrange("p (a d) -> p a d", d=64),
                             zero[:, :].unsqueeze(1).to_broadcast([P, D // 64, 64]), cond=(b > last)).then_inc(blank, 16)
            sp.wait_ge(blank, 16 * (MBLK - NE) + ONE)

        @block.gpsimd
        def _(pool):
            begin(pool, index_ok, xg_ok)
            bound = pool.to_reg(NPAD - 1)

            def gather(b, to):
                pool.tensor_copy(idx[:, :], R.slot_tok[:, bass.ds(b, 1)]).then_inc(index_ok, 1)
                pool.wait_ge(index_ok, b + 1 + ONE)
                pool.sem_inc(passed, 1)
                pool.indirect_dma_start(out=to[:, :], out_offset=None, in_=A["s_rows"][:, :],
                                        in_offset=bass.IndirectOffsetOnAxis(ap=idx[:, 0:1], axis=0),
                                        bounds_check=bound).then_inc(gathered, 16)

            gather(0, xg)
            last = last_block(pool)
            pool.wait_ge(gathered, 16)
            pool.sem_inc(xg_ok, 1)
            gather(1, xn)
            with pool.Fori(1, MBLK + 1) as b:
                with pool.If(b <= last + 1):
                    pool.wait_ge(gathered, b * 16 + 16)
                    pool.wait_ge(xt_ps, b + ONE)
                    pool.sem_inc(passed, 1)
                    pool.tensor_copy(xg[:, :], xn[:, :]).then_inc(xg_ok, 1)
                    pool.wait_ge(xg_ok, b + 1 + ONE)
                    gather(b + 1, xn)
            pool.wait_ge(gathered, last * 16 + 48)
            pool.sem_inc(passed, 1)

        @block.tensor
        def _(pe):
            begin(pe, xt_ps, a_ok, b_ok, hid_ps, y_ok)

            def product(out, lh, ll, m, k0, k1, cols):
                terms = [(k, a, b) for k in range(k0, k1) for a, b in ((lh, wh), (lh, wl), (ll, wh))]
                for n, (k, a, b) in enumerate(terms):
                    mm = pe.matmul(out, a[:, k, :], b[m][:, k, cols], start=(n == 0), stop=(n == len(terms) - 1))
                return mm

            def x_transposes(b):
                pe.wait_ge(xg_ok, b + 1 + ONE)
                pe.wait_ge(xl_ok, b + ONE)
                for k in range(DK):
                    mm = pe.transpose(tp[:, k, :], xg[:, k * P:(k + 1) * P], G.ident[:, :])
                mm.then_inc(xt_ps, 1)

            def up(b, e):
                pe.wait_ge(lo_ok[0], e + 1 + ONE)
                pe.wait_ge(xl_ok, b + 1 + ONE)
                pe.wait_ge(silu_ok, b + ONE)
                product(pa[:, :], xh, xl, 0, 0, DK, slice(0, DE)).then_inc(a_ok, 1)

            def gate(b, e):
                pe.wait_ge(lo_ok[1], e + 1 + ONE)
                pe.wait_ge(hid_ok, b + ONE)
                product(pb[:, :], xh, xl, 1, 0, DK, slice(0, DE)).then_inc(b_ok, 1)

            def hidden_transposes(b):
                pe.wait_ge(hid_ok, b + 1 + ONE)
                pe.wait_ge(hl_ok, b + ONE)
                for k in range(HK):
                    mm = pe.transpose(ph[:, k, :], hid[:, k * P:(k + 1) * P], G.ident[:, :])
                mm.then_inc(hid_ps, 1)

            def down(b, e):
                pe.wait_ge(lo_ok[2], e + 1 + ONE)
                pe.wait_ge(hl_ok, b + 1 + ONE)
                pe.wait_ge(ys_ok, b + ONE)
                for half in range(2):
                    mm = product(py[:, half, :], hh, hl, 2, 0, HK, slice(half * 512, (half + 1) * 512))
                mm.then_inc(y_ok, 1)

            x_transposes(0)
            up(0, 0)
            gate(0, 0)
            x_transposes(1)
            last = last_block(pe)
            with pe.Fori(1, MBLK) as b:
                with pe.If(b <= last):
                    e = expert_of(pe, b)
                    up(b, e)
                    hidden_transposes(b - 1)
                    gate(b, e)
                    x_transposes(b + 1)
                    down(b - 1, expert_of(pe, b - 1))
            hidden_transposes(last)
            down(last, NE - 1)

        @block.scalar
        def _(act):
            begin(act, hi_ok[2], silu_ok, hh_ok, xh_ok, ys_ok, stored)

            def high(m, e, used, count):
                act.wait_ge(raw_ready[m], e * 16 + 16 + ONE)
                act.wait_ge(used, count + ONE)
                for half in range(2):
                    k = halves(m, half)
                    act.activation(wh[m][:, k, :], raw[m][:, k, :], ACT.Copy).then_inc(hi_ok[m], 1)

            def silu(b):
                act.wait_ge(a_ok, b + 1 + ONE)
                act.wait_ge(hid_ps, b + ONE)
                act.activation(hid[:, :], pa[:, :], ACT.Silu).then_inc(silu_ok, 1)

            def x_high(b):
                act.wait_ge(xt_ps, b + 1 + ONE)
                act.wait_ge(b_ok, b + ONE)
                act.activation(xh[:, :, :], tp[:, :, :], ACT.Copy).then_inc(xh_ok, 1)

            def hidden_high(b):
                act.wait_ge(hid_ps, b + 1 + ONE)
                act.wait_ge(y_ok, b + ONE)
                act.activation(hh[:, :, :], ph[:, :, :], ACT.Copy).then_inc(hh_ok, 1)

            def rows(b):
                act.wait_ge(y_ok, b + 1 + ONE)
                act.wait_ge(stored, b * 16 + ONE)
                act.activation(ys[:, :], py[:, :, :].rearrange("p a n -> p (a n)"), ACT.Copy).then_inc(ys_ok, 1)
                act.wait_ge(ys_ok, b + 1 + ONE)
                act.dma_start(A["s_ys"][bass.ds(b * P, P), :], ys[:, :]).then_inc(stored, 16)

            x_high(0)
            high(2, 0, raw_ready[2], 16)
            last = last_block(act)
            silu(0)
            x_high(1)
            e_next = expert_of(act, 1)
            with act.If(e_next > 0):
                high(0, e_next, a_ok, 1)
                high(1, e_next, b_ok, 1)
            with act.Fori(1, MBLK) as b:
                with act.If(b <= last):
                    before, e, after = (expert_of(act, b + n) for n in (-1, 0, 1))
                    silu(b)
                    hidden_high(b - 1)
                    with act.If(after > e):
                        high(0, after, a_ok, b + 1)
                    x_high(b + 1)
                    with act.If(after > e):
                        high(1, after, b_ok, b + 1)
                    rows(b - 1)
                    with act.If(e > before):
                        high(2, e, y_ok, b)
            hidden_high(last)
            rows(last)
            act.wait_ge(stored, last * 16 + 16 + ONE)
            act.sem_inc(passed_end, 1)

        @block.vector
        def _(dve):
            begin(dve, lo_ok[2], xl_ok, hid_ok, hl_ok, zero_ok)
            dve.memset(zero[:, :], 0.0).then_inc(zero_ok, 1)

            def low(m, e):
                for half in range(2):
                    k = halves(m, half)
                    dve.wait_ge(hi_ok[m], e * 2 + half + 1 + ONE)
                    op = dve.tensor_tensor(wl[m][:, k, :], raw[m][:, k, :], wh[m][:, k, :].bitcast(F32), ALU.subtract)
                op.then_inc(lo_ok[m], 1)

            def hidden(b):
                dve.wait_ge(b_ok, b + 1 + ONE)
                dve.wait_ge(silu_ok, b + 1 + ONE)
                dve.tensor_tensor(hid[:, :], pb[:, :], hid[:, :], ALU.mult).then_inc(hid_ok, 1)

            def x_low(b):
                dve.wait_ge(xh_ok, b + 1 + ONE)
                dve.tensor_tensor(xl[:, :, :], tp[:, :, :], xh[:, :, :].bitcast(F32), ALU.subtract).then_inc(xl_ok, 1)

            def hidden_low(b):
                dve.wait_ge(hh_ok, b + 1 + ONE)
                dve.tensor_tensor(hl[:, :, :], ph[:, :, :], hh[:, :, :].bitcast(F32), ALU.subtract).then_inc(hl_ok, 1)

            x_low(0)
            low(2, 0)
            last = last_block(dve)
            hidden(0)
            x_low(1)
            e_next = expert_of(dve, 1)
            with dve.If(e_next > 0):
                low(0, e_next)
                low(1, e_next)
            with dve.Fori(1, MBLK) as b:
                with dve.If(b <= last):
                    before, e, after = (expert_of(dve, b + n) for n in (-1, 0, 1))
                    hidden_low(b - 1)
                    with dve.If(after > e):
                        low(0, after)
                    hidden(b)
                    x_low(b + 1)
                    with dve.If(after > e):
                        low(1, after)
                    with dve.If(e > before):
                        low(2, e)
            hidden_low(last)
    c.close()


def stage_combine(nc, G, A, tag, R):
    S = G.sem
    got = [S(f"{tag}_gathered{u}") for u in range(3)]
    first, done, sq = (S(f"{tag}_{n}") for n in ("first", "added", "squares"))
    c = Ctx(nc, tag + "_")
    y = [[c.sb(f"y{u}{k}", [P, D]) for k in range(2)] for u in range(3)]
    junk = c.sb("junk", [P, D])

    def rows_of(t):
        return P if t < TILES - 1 else NTOK - P * (TILES - 1)

    with nc.Block() as block:
        @block.gpsimd
        def _(pool):
            for t in range(TILES):
                if t >= 3:
                    pool.wait_ge(done, t - 2 + ONE)
                for k in range(2):
                    pool.indirect_dma_start(out=y[t % 3][k][0:rows_of(t), :], out_offset=None, in_=A["s_ys"][:, :],
                                            in_offset=bass.IndirectOffsetOnAxis(ap=R.slot[0:rows_of(t), k, t:t + 1], axis=0),
                                            bounds_check=MBLK * P - 1).then_inc(got[t % 3], 16)

        @block.vector
        def _(dve):
            begin(dve, first, done)
            for t in range(TILES):
                n = rows_of(t)
                dve.wait_ge(got[t % 3], 32 * (t // 3 + 1))
                for k, s in ((0, first), (1, done)):
                    dve.scalar_tensor_tensor(out=G.h[0:n, t, :], in0=y[t % 3][k][0:n, :], scalar=R.gates[0:n, k, t:t + 1],
                                             in1=G.h[0:n, t, :], op0=ALU.mult, op1=ALU.add).then_inc(s, 1)
                    dve.wait_ge(s, t + 1 + ONE)

        @block.scalar
        def _(act):
            begin(act, sq)
            with act.Fori(0, TILES) as t:
                act.wait_ge(done, t + 1 + ONE)
                act.wait_ge(sq, t + ONE)
                act.activation(junk[:, :], G.h[:, bass.ds(t, 1), :], ACT.Square,
                               accum_out=G.ssq[:, bass.ds(t, 1)]).then_inc(sq, 1)
    c.close()


def stage_combine_out(nc, G, A, tag, R):
    S = G.sem
    got = [S(f"{tag}_gathered{u}") for u in range(3)]
    stored = [S(f"{tag}_stored{u}") for u in range(3)]
    first, done, sq, var_ok, root_ok, rstd_ok, out_ok, g_ready = (S(f"{tag}_{n}") for n in (
        "first", "added", "squares", "var", "root", "rstd", "out", "gain"))
    c = Ctx(nc, tag + "_")
    y = [[c.sb(f"y{u}{k}", [P, D]) for k in range(2)] for u in range(3)]
    junk = c.sb("junk", [P, 2, D])
    st = c.sb("stats", [P, 3, TILES])
    g = c.sb("gain", [P, D])
    rows = c.sb("rows", [P, 3, D])
    SETS = TILES // 3

    def rows_of(t):
        return P if t < TILES - 1 else NTOK - P * (TILES - 1)

    with nc.Block() as block:
        @block.gpsimd
        def _(pool):
            for t in range(TILES):
                if t >= 3:
                    pool.wait_ge(done, t - 2 + ONE)
                for k in range(2):
                    pool.indirect_dma_start(out=y[t % 3][k][0:rows_of(t), :], out_offset=None, in_=A["s_ys"][:, :],
                                            in_offset=bass.IndirectOffsetOnAxis(ap=R.slot[0:rows_of(t), k, t:t + 1], axis=0),
                                            bounds_check=MBLK * P - 1).then_inc(got[t % 3], 16)

        @block.sync
        def _(sp):
            begin(sp, g_ready, stored)
            sp.dma_start(g[:, :], A["norm_final"].partition_broadcast(P)).then_inc(g_ready, 16)
            for t in range(TILES):
                n = rows_of(t)
                sp.wait_ge(out_ok, t + 1 + ONE)
                sp.dma_start(A["o_y"][t * P:t * P + n, :], rows[0:n, t % 3, :]).then_inc(stored[t % 3], 16)
            for u in range(3):
                sp.wait_ge(stored[u], 16 * SETS + ONE)

        @block.scalar
        def _(act):
            begin(act, sq, root_ok)
            for t in range(TILES):
                act.wait_ge(done, t + 1 + ONE)
                if t >= 2:
                    act.wait_ge(sq, t - 1 + ONE)
                act.activation(junk[:, t % 2, :], G.h[:, t, :], ACT.Square, accum_out=G.ssq[:, t:t + 1]).then_inc(sq, 1)
                if t % 3 == 2:
                    i = t // 3
                    act.wait_ge(var_ok, i + 1 + ONE)
                    act.activation(st[:, 1, t - 2:t + 1], st[:, 0, t - 2:t + 1], ACT.Sqrt).then_inc(root_ok, 1)

        @block.vector
        def _(dve):
            begin(dve, first, done, var_ok, rstd_ok, out_ok)

            def norm(i):
                dve.wait_ge(root_ok, i + 1 + ONE)
                dve.reciprocal(st[:, 2, i * 3:i * 3 + 3], st[:, 1, i * 3:i * 3 + 3]).then_inc(rstd_ok, 1)
                dve.wait_ge(rstd_ok, i + 1 + ONE)
                for u in range(3):
                    t = i * 3 + u
                    if i >= 1:
                        dve.wait_ge(stored[u], i * 16 + ONE)
                    dve.scalar_tensor_tensor(out=rows[:, u, :], in0=G.h[:, t, :], scalar=st[:, 2, t:t + 1], in1=g[:, :],
                                             op0=ALU.mult, op1=ALU.mult).then_inc(out_ok, 1)

            for i in range(SETS):
                for u in range(3):
                    t = i * 3 + u
                    n = rows_of(t)
                    dve.wait_ge(got[u], 32 * (i + 1))
                    for k, s in ((0, first), (1, done)):
                        dve.scalar_tensor_tensor(out=G.h[0:n, t, :], in0=y[u][k][0:n, :], scalar=R.gates[0:n, k, t:t + 1],
                                                 in1=G.h[0:n, t, :], op0=ALU.mult, op1=ALU.add).then_inc(s, 1)
                        dve.wait_ge(s, t + 1 + ONE)
                if i == 0:
                    dve.wait_ge(g_ready, 16 + ONE)
                else:
                    norm(i - 1)
                dve.wait_ge(sq, i * 3 + 3 + ONE)
                dve.tensor_scalar(st[:, 0, i * 3:i * 3 + 3], G.ssq[:, i * 3:i * 3 + 3], 1.0 / D, EPS,
                                  ALU.mult, ALU.add).then_inc(var_ok, 1)
            norm(SETS - 1)
    c.close()


def layer_moe(nc, G, A, layer):
    R = Ctx(nc, f"moe{layer}_")
    R.gates = R.sb("gates", [P, 2, TILES])
    R.slot = R.sb("slot", [P, 2, TILES], I32)
    R.slot_tok = R.sb("slot_tok", [P, MBLK + 2], I32)
    R.block_expert = R.sb("block_expert", [P, MBLK + 1], I32)
    R.last = R.sb("last", [P, 1], I32)
    X = Ctx(nc, f"raw{layer}_")
    R.raw = [X.sb("w1", [P, DK, DE]), X.sb("w3", [P, DK, DE]), X.sb("w2", [P, DE // P, D])]
    R.wh, R.wl = ([X.sb(f"{part}_{m}", [P, DK, DE], F32R) for m in ("w1", "w3")] for part in ("high", "low"))
    R.hi_ok, R.lo_ok = ([G.sem(f"moe{layer}_{m}_{part}") for m in ("w1", "w3")] for part in ("high", "low"))
    R.raw_ready = [G.sem(f"raw{layer}_ready{m}") for m in range(3)]
    stage_route(nc, G, A, f"r{layer}", layer, R)
    stage_experts(nc, G, A, f"e{layer}", layer, R)
    X.close()
    if layer == 0:
        stage_combine(nc, G, A, f"c{layer}", R)
    else:
        stage_combine_out(nc, G, A, f"c{layer}", R)
    R.close()
SLOTS = 2 + GROUPS
K_SLOT, Q_SLOT, V_SLOT = 0, 1, 1 + GROUPS
QT = SEQ // P
PAIRS = 4


def group_tiles():
    def plain(t):
        return lambda x: x[:, t * P:(t + 1) * P]

    def by4(nb, r):
        return lambda x: x[:, 4 * P * nb + r:4 * P * (nb + 1) - 3 + r:4]

    def by8(j):
        return lambda x: x[:, j:SEQ - 7 + j:8]

    out = []
    for t in range(QT):
        out.append((0, t, plain(t), [t] if t == 0 else [t - 1, t]))
    for nb in range(2):
        for r in range(4):
            out.append((1, 4 * nb + r, by4(nb, r), [4 * k + r for k in range(nb + 1)]))
    for j in range(8):
        out.append((2, j, by8(j), [j]))
    return out


def stage_heads(nc, G, A, xh, xl, H, wr, w_first):
    S = G.sem
    RING = (0, 1, 2, 0, 1)
    BEFORE = (2, 2, 5, 3, 3)
    w_ready = [w_first] + [S(f"hd_w_ready{s}") for s in (1, 2)]
    wh_ok, wl_ok = S("hd_w_high"), S("hd_w_low")
    scaled, proj_ok, pj_ok, pj_out, t1_ok, rope_ok, table_ready, k_stored, v_stored, o_stored = (
        S("hd_" + n) for n in ("w_scaled", "product", "bank_full", "bank_read", "rope_part", "rope",
                               "tables", "k_stored", "v_stored", "o_stored"))
    passed, sc_ok, masked, exp_ok, pt_ps, pt_ok = (S("hd_" + n) for n in (
        "passed", "scores", "masked", "exp", "p_transposed", "pt"))
    c = Ctx(nc, "hd_")
    wh = c.sb("wh", [P, 3, DK, P], F32R)
    wl = c.sb("wl", [P, 3, DK, P], F32R)
    cos = c.sb("cos", [P, NTOK])
    sin = c.sb("sin", [P, NTOK])
    band = c.sb("band", [P, 2 * P])
    pair = c.sb("pair", [P, P])
    raw = c.sb("raw", [P, 2, NTOK])
    half = c.sb("half", [P, NTOK])
    flat_h = G.h[:, :, :].rearrange("p t d -> p (t d)")
    OB = GROUPS * QT * (HD + 2)
    assert SLOTS * NTOK + OB <= TILES * D
    hT = flat_h[:, 0:SLOTS * NTOK].rearrange("p (s n) -> p s n", s=SLOTS)
    ob = flat_h[:, SLOTS * NTOK:SLOTS * NTOK + OB].rearrange("p (g t c) -> p g t c", g=GROUPS, t=QT)
    vb = c.sb("vb", [P, GROUPS, QT, HD])
    vs = c.sb("vs", [P, HD])
    sc = c.sb("sc", [P, 3, 2 * P])
    pr = c.sb("pr", [P, 3, 2 * P])
    pt = c.sb("pt", [P, 3, 2, P])
    pj = [c.ps(f"pj{u}", [P, 512]) for u in range(3)]
    psc = [c.ps(f"psc{u}", [P, 512]) for u in range(2)]
    ppt = [c.ps(f"ppt{u}", [P, 2, P]) for u in range(2)]
    NC = len(CHUNKS)
    TL = group_tiles()
    NT = len(TL)

    uses = [("proj", s, n) for s in range(SLOTS) for n in range(NC)]
    v_batches = [TL[n:n + PAIRS] for n in range(0, NT, PAIRS)] + [None]
    uses += [("v", b) for b in range(len(v_batches))] + [("o", b) for b in range(NT // PAIRS)]
    NU = len(uses)
    O0 = SLOTS * NC + len(v_batches)

    def bank(n):
        return pj[n % 3]

    with nc.Block() as block:
        @block.sync
        def _(sp):
            begin(sp, table_ready, k_stored, v_stored, o_stored, w_ready[1:])
            def stores(h):
                sp.wait_ge(rope_ok, h * (1 + GROUPS) + 1 + ONE)
                sp.dma_start(A["o_kT"][bass.ds(h, 1)].rearrange("a c t -> c (a t)"), hT[:, K_SLOT, :]).then_inc(k_stored, 16)
                sp.wait_ge(pj_out, h * NU + O0 + ONE)
                v_out = A["o_v"][:, bass.ds(h, 1), :].rearrange("t a c -> t (a c)")
                sp.dma_start(v_out[0:SEQ, :].rearrange("(t p) c -> p t c", p=P), vb[:, 0]).then_inc(v_stored, 16)
                sp.dma_start(v_out[SEQ:, :], vs[P - NSMP:, :]).then_inc(v_stored, 16)
                sp.wait_ge(pj_out, h * NU + NU + ONE)
                og = A["s_og"][:, :, bass.ds(h, 1), :].rearrange("g t a c -> g t (a c)")
                sp.dma_start(og[0].rearrange("(t p) c -> p t c", p=P), ob[:, 0]).then_inc(o_stored, 16)
                by4 = og[1].rearrange("(n p r) c -> n p r c", n=2, r=4)
                for n in range(2):
                    sp.dma_start(by4[n], ob[:, 1, 4 * n:4 * n + 4]).then_inc(o_stored, 16)
                sp.dma_start(og[2].rearrange("(n j) c -> n j c", j=8), ob[:, 2]).then_inc(o_stored, 16)

            def load(h, s):
                sp.dma_start(wr[:, RING[s]], A["w_heads"][bass.ds(h, 1), s].rearrange("a p k n -> p (a k) n"))\
                    .then_inc(w_ready[RING[s]], 16)

            def late_loads(h):
                for s in (3, 4):
                    sp.wait_ge(wl_ok, h * SLOTS + s - BEFORE[s] + 1 + ONE)
                    load(h, s)

            load(0, 1)
            load(0, 2)
            sp.dma_start(cos[:, :], A["c_cos"]).then_inc(table_ready, 16)
            sp.dma_start(sin[:, :], A["c_sin"]).then_inc(table_ready, 16)
            sp.dma_start(band[:, :], A["c_band"]).then_inc(table_ready, 16)
            sp.dma_start(pair[:, :], A["c_pair"]).then_inc(table_ready, 16)
            with sp.Fori(0, HEADS - 1) as h:
                late_loads(h)
                for s in range(3):
                    sp.wait_ge(wl_ok, (h + 1) * SLOTS + s - BEFORE[s] + 1 + ONE)
                    load(h + 1, s)
                stores(h)
            late_loads(HEADS - 1)
            stores(HEADS - 1)
            sp.wait_ge(k_stored, 16 * HEADS + ONE)
            sp.wait_ge(v_stored, 32 * HEADS + ONE)
            sp.wait_ge(o_stored, 64 * HEADS + ONE)

        @block.gpsimd
        def _(pool):
            begin(pool, scaled, wl_ok)

            def scale(h, s):
                g = G.gcol[:, GAIN_KV if s in (K_SLOT, V_SLOT) else GAIN_MIX1, :].unsqueeze(2).to_broadcast([P, DK, P])
                per_head, turn = (RING.count(RING[s]), RING[:s].count(RING[s]))
                pool.wait_ge(w_ready[RING[s]], h * (16 * per_head) + (16 * turn + 16) + ONE)
                pool.tensor_tensor(wr[:, RING[s]], wr[:, RING[s]], g, ALU.mult).then_inc(scaled, 1)

            def low_part(h, s):
                pool.wait_ge(wh_ok, h * SLOTS + s + 1 + ONE)
                pool.tensor_tensor(wl[:, RING[s]], wr[:, RING[s]], wh[:, RING[s]].bitcast(F32), ALU.subtract)\
                    .then_inc(wl_ok, 1)

            scale(0, 0)
            with pool.Fori(0, HEADS) as h:
                for s in range(SLOTS - 1):
                    pool.wait_ge(scaled, h * SLOTS + s + 1 + ONE)
                    pool.wait_ge(wl_ok, h * SLOTS + s + ONE)
                    scale(h, s + 1)
                    pool.wait_ge(scaled, h * SLOTS + s + 2 + ONE)
                    low_part(h, s)
                pool.wait_ge(wl_ok, h * SLOTS + SLOTS - 1 + ONE)
                low_part(h, SLOTS - 1)
                with pool.If(h < HEADS - 1):
                    pool.wait_ge(wl_ok, h * SLOTS + SLOTS + ONE)
                    scale(h + 1, 0)

        @block.tensor
        def _(pe):
            begin(pe, proj_ok, pj_ok, sc_ok, pt_ps)
            with pe.Fori(0, HEADS) as h:
                def claim(n):
                    pe.wait_ge(pj_out, (h * NU + n - 2 if n >= 2 else h * NU) + ONE)

                n = 0
                for s in range(SLOTS):
                    pe.wait_ge(wl_ok, h * SLOTS + s + 1 + ONE)
                    for c0, cn in CHUNKS:
                        claim(n)
                        for k in range(DK):
                            for q, (w, x) in enumerate(((wh, xh), (wh, xl), (wl, xh))):
                                mm = pe.matmul(bank(n)[:, 0:cn], w[:, RING[s], k, :], x[:, k, c0:c0 + cn],
                                               start=(k == 0 and q == 0), stop=(k == DK - 1 and q == 2))
                        mm.then_inc(proj_ok, 1)
                        n += 1

                def value_rows(n):
                    pe.wait_ge(pj_out, h * NU + (V_SLOT + 1) * NC + ONE)
                    for batch in v_batches:
                        claim(n)
                        if batch is None:
                            pe.transpose(bank(n)[:, 0:HD], hT[:, V_SLOT, NTOK - P:], G.ident[:, :]).then_inc(pj_ok, 1)
                        else:
                            for q, (g, t, view, keys) in enumerate(batch):
                                mm = pe.transpose(bank(n)[:, q * P:(q + 1) * P], view(hT[:, V_SLOT, :]), G.ident[:, :])
                            mm.then_inc(pj_ok, 1)
                        n += 1

                def scores(j):
                    g, t, view, keys = TL[j]
                    pe.wait_ge(rope_ok, h * (1 + GROUPS) + 2 + g + ONE)
                    pe.wait_ge(masked, (h * NT + j - 1 if j >= 2 else h * NT) + ONE)
                    kT = hT[:, K_SLOT, :]
                    for b, key in enumerate(keys):
                        kv = [x for x in TL if x[0] == g and x[1] == key][0][2]
                        mm = pe.matmul(psc[j % 2][:, b * P:(b + 1) * P], view(hT[:, Q_SLOT + g, :]), kv(kT),
                                       start=True, stop=True)
                    mm.then_inc(sc_ok, 1)

                def p_transposes(j):
                    pe.wait_ge(exp_ok, h * NT + j + 1 + ONE)
                    pe.wait_ge(pt_ok, (h * NT + j - 1 if j >= 2 else h * NT) + ONE)
                    for b in range(len(TL[j][3])):
                        mm = pe.transpose(ppt[j % 2][:, b, :], pr[:, j % 3, b * P:(b + 1) * P], G.ident[:, :])
                    mm.then_inc(pt_ps, 1)

                def weighted(j):
                    g, t, view, keys = TL[j]
                    if j % PAIRS == 0:
                        claim(O0 + j // PAIRS)
                    pe.wait_ge(pt_ok, h * NT + j + 1 + ONE)
                    for b, key in enumerate(keys):
                        mm = pe.matmul(bank(O0 + j // PAIRS)[:, (j % PAIRS) * P:(j % PAIRS + 1) * P], pt[:, j % 3, b, :],
                                       vb[:, g, key, :], start=(b == 0), stop=(b == len(keys) - 1))
                    if j % PAIRS == PAIRS - 1:
                        mm.then_inc(pj_ok, 1)

                for j in range(2):
                    scores(j)
                value_rows(n)
                pe.wait_ge(pj_out, h * NU + O0 + ONE)
                for j in range(NT + 3):
                    if 2 <= j < NT:
                        scores(j)
                    if 0 <= j - 2 < NT:
                        p_transposes(j - 2)
                    if j >= 3:
                        weighted(j - 3)

        @block.scalar
        def _(act):
            begin(act, pj_out, exp_ok, wh_ok)

            def high_part(h, s):
                act.wait_ge(scaled, h * SLOTS + s + 1 + ONE)
                act.activation(wh[:, RING[s]], wr[:, RING[s]], ACT.Copy).then_inc(wh_ok, 1)

            for s in range(3):
                high_part(0, s)
            with act.Fori(0, HEADS) as h:
                n = 0
                for s in range(SLOTS):
                    if s == V_SLOT:
                        dst = hT[:, V_SLOT, :]
                    else:
                        r = s
                        dst = raw[:, r % 2, :]
                        act.wait_ge(rope_ok, (h * (1 + GROUPS) + r - 1 if r >= 2 else h * (1 + GROUPS)) + ONE)
                    for c0, cn in CHUNKS:
                        act.wait_ge(proj_ok, h * SLOTS * NC + n + 1 + ONE)
                        act.activation(dst[:, c0:c0 + cn], bank(n)[:, 0:cn], ACT.Copy).then_inc(pj_out, 1)
                        n += 1
                    if s < 2:
                        high_part(h, s + 3)
                act.wait_ge(v_stored, h * 32 + ONE)
                for b, batch in enumerate(v_batches):
                    act.wait_ge(pj_ok, h * (NU - O0 + len(v_batches)) + b + 1 + ONE)
                    if batch is None:
                        act.activation(vs[:, :], bank(n)[:, 0:HD], ACT.Copy).then_inc(pj_out, 1)
                    else:
                        g, t = batch[0][:2]
                        act.activation(vb[:, g, t:t + PAIRS, :], bank(n)[:, :].rearrange("p (t c) -> p t c", c=HD),
                                       ACT.Copy).then_inc(pj_out, 1)
                    n += 1
                act.wait_ge(o_stored, h * 64 + ONE)
                for j in range(NT + 4):
                    if j in (4, 9, 14):
                        with act.If(h < HEADS - 1):
                            high_part(h + 1, (4, 9, 14).index(j))
                    if j < NT:
                        g, t, view, keys = TL[j]
                        w = len(keys) * P
                        act.wait_ge(masked, h * NT + j + 1 + ONE)
                        act.wait_ge(pt_ps, (h * NT + j - 2 if j >= 3 else h * NT) + ONE)
                        act.activation(pr[:, j % 3, 0:w], sc[:, j % 3, 0:w], ACT.Exp, bias=ob[:, g, t, HD:HD + 1],
                                       scale=-1.0, accum_out=ob[:, g, t, HD + 1:HD + 2]).then_inc(exp_ok, 1)
                    if j >= 4 and (j - 4) % PAIRS == PAIRS - 1:
                        b = (j - 4) // PAIRS
                        g, t = TL[b * PAIRS][:2]
                        act.wait_ge(pj_ok, h * (NU - O0 + len(v_batches)) + len(v_batches) + b + 1 + ONE)
                        act.activation(ob[:, g, t:t + PAIRS, 0:HD], bank(O0 + b)[:, :].rearrange("p (t c) -> p t c", c=HD),
                                       ACT.Copy).then_inc(pj_out, 1)

        @block.vector
        def _(dve):
            begin(dve, t1_ok, rope_ok, masked, pt_ok)
            dve.wait_ge(table_ready, 64 + ONE)
            HALF = HD // 2
            with dve.Fori(0, HEADS) as h:
                def rope(s, r):
                    dve.wait_ge(pj_out, h * NU + (s + 1) * NC + ONE)
                    if s == K_SLOT:
                        dve.wait_ge(k_stored, h * 16 + ONE)
                    src, dst = raw[:, r % 2, :], hT[:, s, :]
                    dve.tensor_tensor(dst, src, cos[:, :], ALU.mult)
                    dve.tensor_tensor(half[0:HALF, :], src[HALF:, :], sin[HALF:, :], ALU.mult)
                    dve.tensor_tensor(half[HALF:, :], src[0:HALF, :], sin[0:HALF, :], ALU.mult).then_inc(t1_ok, 1)
                    dve.wait_ge(t1_ok, h * (1 + GROUPS) + r + 1 + ONE)
                    dve.tensor_tensor(dst, dst, half[:, :], ALU.add).then_inc(rope_ok, 1)
                    dve.wait_ge(rope_ok, h * (1 + GROUPS) + r + 1 + ONE)
                    if s == K_SLOT:
                        dve.tensor_copy(H.ks[:, bass.ds(h, 1), :].rearrange("p a n -> p (a n)"), dst[:, SEQ:])
                    else:
                        dve.tensor_copy(H.qs[:, bass.ds(h, 1), s - Q_SLOT, :].rearrange("p a n -> p (a n)"), dst[:, SEQ:])

                for r, s in enumerate((K_SLOT, Q_SLOT, Q_SLOT + 1, Q_SLOT + 2)):
                    rope(s, r)
                for j in range(NT + 2):
                    if j < NT:
                        g, t, view, keys = TL[j]
                        w = len(keys) * P
                        mask = pair[:, :] if g == 2 else band[:, 2 * P - w:]
                        dve.wait_ge(sc_ok, h * NT + j + 1 + ONE)
                        dve.wait_ge(exp_ok, (h * NT + j - 2 if j >= 3 else h * NT) + ONE)
                        if j == 0:
                            dve.wait_ge(o_stored, h * 64 + ONE)
                        dve.sem_inc(passed, 1)
                        dve.tensor_tensor_reduce(out=sc[:, j % 3, 0:w], in0=psc[j % 2][:, 0:w], in1=mask, scale=-SCALE,
                                                 scalar=3.0e38, op0=ALU.add, op1=ALU.min,
                                                 accum_out=ob[:, g, t, HD:HD + 1]).then_inc(masked, 1)
                    if j >= 2:
                        b = j - 2
                        w = len(TL[b][3])
                        dve.wait_ge(pt_ps, h * NT + b + 1 + ONE)
                        dve.tensor_copy(pt[:, b % 3, 0:w, :], ppt[b % 2][:, 0:w, :]).then_inc(pt_ok, 1)
    c.close()


def load_outputs(eng, A, H, t, u):
    for g in range(GROUPS):
        eng.dma_start(H.og[:, u, g], A["s_og"][g, bass.ds(t * P, P)]).then_inc(H.og_ready[u], 16)


def stage_sample(nc, G, A, H):
    S = G.sem
    passed, wo_ready, wh_ok, wl_ok = (S("sm_" + n) for n in ("passed", "wo_ready", "wo_high", "wo_low"))
    (k_ready, v_ready, mask_ready, q_ok, kt_ps, kt_out, new_ok, st_ps, st_out, s_ps, masked, exp_ok, chain, norm_ok, pt_ps, pt_out,
     o_ps, o_out) = (S("sm_" + n) for n in (
         "k_ready", "v_ready", "mask_ready", "q", "kt_bank", "kt", "new_k", "st_bank", "st", "scores", "masked", "exp",
         "chain", "normed", "pt_bank", "pt", "o_bank", "o"))
    c = Ctx(nc, "sm_")
    NB = 2
    KC = PAST // P
    NEW = NB * DEC_S
    NK = PAST + NEW
    R = NB * HEADS * DEC_S
    assert R == P
    kc = c.sb("kc", [P, NB, KC, HEADS, HD])
    vc = c.sb("vc", [P, NB, KC, HEADS, HD])
    vn = c.sb("vn", [NEW, HEADS, HD])
    mask = c.sb("mask", [P, GROUPS, NK])
    qb = c.sb("qb", [P, NB, HEADS, GROUPS, DEC_S])
    kT = c.sb("kT", [P, NB, HEADS, PAST])
    kn = c.sb("kn", [P, HEADS, NB, DEC_S])
    sT = c.sb("sT", [P, KC + 1, GROUPS, NB, HEADS, DEC_S])
    sc = c.sb("sc", [P, GROUPS, NK])
    pr = c.sb("pr", [P, GROUPS, NK])
    stat = c.sb("stat", [P, 8])
    pT = c.sb("pT", [P, KC + 1, P])
    bk = [c.ps(f"bk{u}", [P, 4, P]) for u in range(2)]
    pst = [c.ps(f"pst{u}", [P, 512]) for u in range(2)]
    psc = c.ps("psc", [P, GROUPS, 512])
    px = c.ps("px", [P, 512])
    SB = NB * KC + 1
    QW = HEADS * GROUPS * DEC_S
    KB = NB * KC * HEADS // 4
    STEPS = DEC_B // NB
    LINKS = 4

    with nc.Block() as block:
        @block.sync
        def _(sp):
            begin(sp, mask_ready, k_ready, v_ready, wo_ready, H.h_ready, H.og_ready)
            def keys(i):
                for b in range(NB):
                    sp.dma_start(kc[:, b], A["cache_k"][bass.ds(i * NB + b, 1)].rearrange("a (k p) h c -> p (a k) h c", p=P))\
                        .then_inc(k_ready, 16)

            def values(i):
                for b in range(NB):
                    sp.dma_start(vc[:, b], A["cache_v"][bass.ds(i * NB + b, 1)].rearrange("a (k p) h c -> p (a k) h c", p=P))\
                        .then_inc(v_ready, 16)
                sp.dma_start(vn[:, :, :], A["o_v"][bass.ds(i * NEW + SEQ, NEW)]).then_inc(v_ready, 16)

            keys(0)
            sp.dma_start(mask[:, :, :], A["c_smp"]).then_inc(mask_ready, 16)
            values(0)
            sp.wait_ge(kt_ps, KB + ONE)
            keys(1)
            sp.dma_start(H.wo, A["attn_w_o"][0].rearrange("(k p) n -> p k n", p=P)).then_inc(wo_ready, 16)
            with sp.Fori(0, STEPS - 2) as i:
                sp.wait_ge(kt_ps, i * KB + 2 * KB + ONE)
                keys(i + 2)
                sp.wait_ge(o_ps, i + 1 + ONE)
                values(i + 1)
            sp.wait_ge(o_ps, STEPS - 1 + ONE)
            values(STEPS - 1)
            sp.wait_ge(wl_ok, HEADS + ONE)
            sp.dma_start(G.h[:, :, :], A["s_h"].rearrange("(t p) d -> p t d", p=P)).then_inc(H.h_ready, 16)
            load_outputs(sp, A, H, 0, 0)
            load_outputs(sp, A, H, 1, 1)

        @block.gpsimd
        def _(pool):
            begin(pool, q_ok, wh_ok, wl_ok)

            def queries(i):
                pool.wait_ge(st_ps, i * SB + ONE)
                for b in range(NB):
                    pool.wait_ge(q_ok, i * (2 * NB) + 2 * b + ONE)
                    t0 = i * (NB * DEC_S) + b * DEC_S
                    pool.tensor_copy(qb[:, b], H.qs[:, :, :, bass.ds(t0, DEC_S)]).then_inc(q_ok, 1)
                    pool.wait_ge(q_ok, i * (2 * NB) + 2 * b + 1 + ONE)
                    pool.tensor_copy(kn[:, :, b, :], H.ks[:, :, bass.ds(t0, DEC_S)]).then_inc(q_ok, 1)

            with pool.Fori(0, 2) as i:
                queries(i)
            pool.wait_ge(wo_ready, 16 + ONE)
            pool.wait_ge(q_ok, 4 * NB + ONE)
            for k in range(HEADS):
                pool.tensor_copy(H.wh[:, k, :], H.wo[:, k, :]).then_inc(wh_ok, 1)
                pool.wait_ge(wh_ok, k + 1 + ONE)
                pool.tensor_tensor(H.wl[:, k, :], H.wo[:, k, :], H.wh[:, k, :].bitcast(F32), ALU.subtract).then_inc(wl_ok, 1)
                pool.wait_ge(wl_ok, k + 1 + ONE)
            with pool.Fori(2, STEPS) as i:
                queries(i)

        @block.tensor
        def _(pe):
            begin(pe, kt_ps, st_ps, s_ps, pt_ps, o_ps)
            def scores(i):
                pe.wait_ge(k_ready, i * (16 * NB) + 16 * NB + ONE)
                n = 0
                for b in range(NB):
                    for h in range(0, HEADS, 2):
                        pe.wait_ge(kt_out, (i * KB + n - 1 if n >= 2 else i * KB) + ONE)
                        for q in range(4):
                            mm = pe.transpose(bk[n % 2][:, q, :], kc[:, b, q % 2, h + q // 2, :], G.ident[:, :])
                        mm.then_inc(kt_ps, 1)
                        n += 1
                pe.wait_ge(kt_out, i * KB + KB + ONE)
                pe.wait_ge(q_ok, i * (2 * NB) + 2 * NB + ONE)
                n = 0

                def free_bank(n):
                    pe.wait_ge(st_out, (i * SB + n - 1 if n >= 2 else i * SB) + ONE)

                for k in range(KC):
                    for b in range(NB):
                        free_bank(n)
                        for h in range(HEADS):
                            mm = pe.matmul(pst[n % 2][:, 0:QW].rearrange("p (h q) -> p h q", h=HEADS)[:, h],
                                           kT[:, b, h, k * P:(k + 1) * P], qb[:, b, h], start=True, stop=True)
                        mm.then_inc(st_ps, 1)
                        n += 1
                free_bank(n)
                for h in range(HEADS):
                    mm = pe.matmul(pst[n % 2][0:NEW, 0:NB * QW].rearrange("p (h b q) -> p h b q", h=HEADS, b=NB)[:, h],
                                   kn[:, h].rearrange("p b n -> p (b n)"),
                                   qb[:, :, h].rearrange("p b g n -> p b (g n)"), start=True, stop=True)
                mm.then_inc(st_ps, 1)
                n += 1
                pe.wait_ge(st_out, i * SB + SB + ONE)
                pe.wait_ge(masked, i * GROUPS + ONE)
                for g in range(GROUPS):
                    for k in range(KC + 1):
                        kw = P if k < KC else NEW
                        mm = pe.transpose(psc[:, g, k * P:k * P + kw],
                                          sT[0:kw, k, g].rearrange("p b h n -> p (b h n)"), G.ident[0:kw, 0:kw])
                    mm.then_inc(s_ps, 1)

            def weighted(i):
                pe.wait_ge(norm_ok, i + 1 + ONE)
                pe.wait_ge(o_out, i + ONE)
                for k in range(KC + 1):
                    kw = P if k < KC else NEW
                    mm = pe.transpose(px[0:kw, k * P:(k + 1) * P], pr[:, 0, k * P:k * P + kw], G.ident[:, :])
                mm.then_inc(pt_ps, 1)
                pe.wait_ge(pt_out, i + 1 + ONE)
                pe.wait_ge(v_ready, i * (16 * NB + 16) + (16 * NB + 16) + ONE)
                def columns(x):
                    return x.rearrange("p (b h n) -> p b h n", b=NB, h=HEADS)[:, :, h, :]

                for h in range(HEADS):
                    for b in range(NB):
                        q0 = (b * HEADS + h) * DEC_S
                        for k in range(KC):
                            pe.matmul(px[:, q0:q0 + DEC_S], vc[:, b, k, h, :], pT[:, k, q0:q0 + DEC_S],
                                      start=(h == 0 and b == 0 and k == 0), stop=False)
                    mm = pe.matmul(columns(px[:, 0:P]), vn[:, h, :], columns(pT[0:NEW, KC, :]), start=False,
                                   stop=(h == HEADS - 1))
                mm.then_inc(o_ps, 1)

            scores(0)
            with pe.Fori(0, STEPS - 1) as i:
                scores(i + 1)
                weighted(i)
            weighted(STEPS - 1)

        @block.scalar
        def _(act):
            begin(act, kt_out, exp_ok)
            def keys(i):
                for n in range(KB):
                    b, h = n // (HEADS // 2), n % (HEADS // 2) * 2
                    act.wait_ge(kt_ps, i * KB + n + 1 + ONE)
                    if n == 0:
                        act.wait_ge(st_ps, i * SB + ONE)
                    act.activation(kT[:, b, h:h + 2, 0:PAST].rearrange("p h (k c) -> p h k c", c=P),
                                   bk[n % 2][:, :, :].rearrange("p (h k) c -> p h k c", k=KC), ACT.Copy).then_inc(kt_out, 1)

            def exp(i):
                act.wait_ge(chain, i * LINKS + 1 + ONE)
                act.wait_ge(norm_ok, i + ONE)
                act.activation(pr[:, :, :].rearrange("p g k -> p (g k)"), sc[:, :, :].rearrange("p g k -> p (g k)"),
                               ACT.Exp, bias=stat[:, 3:4], scale=-1.0, accum_out=stat[:, 4:5]).then_inc(exp_ok, 1)

            keys(0)
            with act.Fori(0, STEPS - 1) as i:
                exp(i)
                keys(i + 1)
            exp(STEPS - 1)

        @block.vector
        def _(dve):
            begin(dve, st_out, masked, norm_ok, pt_out, o_out, chain)
            dve.wait_ge(mask_ready, 16 + ONE)

            def scores(i):
                dve.wait_ge(s_ps, i * GROUPS + ONE)
                n = 0
                for k in range(KC):
                    for b in range(NB):
                        dve.wait_ge(st_ps, i * SB + n + 1 + ONE)
                        dve.tensor_copy(sT[:, k, :, b], pst[n % 2][:, 0:QW].rearrange("p (h g n) -> p g h n", h=HEADS, g=GROUPS))\
                            .then_inc(st_out, 1)
                        n += 1
                dve.wait_ge(st_ps, i * SB + n + 1 + ONE)
                for b in range(NB):
                    last = dve.tensor_copy(sT[0:NEW, KC, :, b], pst[n % 2][0:NEW, 0:NB * QW].rearrange(
                        "p (h b g n) -> p b g h n", h=HEADS, b=NB, g=GROUPS)[:, b])
                last.then_inc(st_out, 1)
                for g in range(GROUPS):
                    dve.wait_ge(s_ps, i * GROUPS + g + 1 + ONE)
                    if g == 0:
                        dve.wait_ge(exp_ok, i + ONE)
                    dve.sem_inc(passed, 1)
                    dve.tensor_tensor_reduce(out=sc[:, g, :], in0=psc[:, g, 0:NK], in1=mask[:, g, :], scale=-SCALE,
                                             scalar=3.0e38, op0=ALU.add, op1=ALU.min,
                                             accum_out=stat[:, g:g + 1]).then_inc(masked, 1)

            def softmax(i):
                link = Chain(dve, chain, i * LINKS)
                dve.wait_ge(masked, i * GROUPS + GROUPS + ONE)
                link(dve.tensor_reduce(stat[:, 3:4], stat[:, 0:3], AX.X, ALU.min))
                dve.wait_ge(exp_ok, i + 1 + ONE)
                link(dve.reciprocal(stat[:, 5:6], stat[:, 4:5]))
                link(dve.tensor_tensor(pr[:, 0, :], pr[:, 0, :], pr[:, 1, :], ALU.add))
                link(dve.tensor_tensor(pr[:, 0, :], pr[:, 0, :], pr[:, 2, :], ALU.add))
                assert link.n == LINKS
                dve.wait_ge(pt_ps, i + ONE)
                dve.tensor_scalar(pr[:, 0, :], pr[:, 0, :], stat[:, 5:6], None, ALU.mult).then_inc(norm_ok, 1)

            def weighted(i):
                dve.wait_ge(pt_ps, i + 1 + ONE)
                dve.wait_ge(o_ps, i + ONE)
                dve.tensor_copy(pT[:, 0:KC, :], px[:, 0:KC * P].rearrange("p (k c) -> p k c", c=P))
                dve.tensor_copy(pT[0:NEW, KC, :], px[0:NEW, KC * P:(KC + 1) * P]).then_inc(pt_out, 1)
                dve.wait_ge(o_ps, i + 1 + ONE)
                for b in range(NB):
                    last = dve.tensor_copy(H.oT[:, :, bass.ds(i * (NB * DEC_S) + b * DEC_S, DEC_S)],
                                           px[:, b * HEADS * DEC_S:(b + 1) * HEADS * DEC_S].rearrange("p (h n) -> p h n", n=DEC_S))
                last.then_inc(o_out, 1)

            scores(0)
            with dve.Fori(0, STEPS - 1) as i:
                softmax(i)
                scores(i + 1)
                weighted(i)
            softmax(STEPS - 1)
            weighted(STEPS - 1)
    c.close()


def stage_merge(nc, G, A, H):
    S = G.sem
    og_ready = H.og_ready
    diff_ok, exp_ok, chain, rows_ok, tr_ok, oh_ok, ol_ok, prod, added, sq = (S("mg_" + n) for n in (
        "diff", "exp", "chain", "rows", "transposed", "o_high", "o_low", "product", "added", "squares"))
    c = Ctx(nc, "mg_")
    wh, wl, og = H.wh, H.wl, H.og
    df = c.sb("df", [P, 2, GROUPS, HEADS])
    ex = c.sb("ex", [P, 2, GROUPS, HEADS])
    den = c.sb("den", [P, 2, 3, HEADS])
    orow = c.sb("orow", [P, 2, HEADS, HD])
    term = c.sb("term", [P, HEADS, HD])
    oh = c.sb("oh", [P, 2, HEADS, P], F32R)
    ol = c.sb("ol", [P, 2, HEADS, P], F32R)
    tp = [c.ps(f"tp{u}", [P, HEADS, P]) for u in range(2)]
    py = [c.ps(f"py{u}", [P, 2, 512]) for u in range(2)]
    junk = c.sb("junk", [P, D])
    LINKS = 11

    with nc.Block() as block:
        @block.sync
        def _(sp):
            with sp.Fori(0, QT // 2 - 1) as i:
                for u in range(2):
                    sp.wait_ge(rows_ok, i * 2 + u + 1 + ONE)
                    load_outputs(sp, A, H, i * 2 + u + 2, u)

        @block.vector
        def _(dve):
            begin(dve, added, diff_ok, rows_ok, ol_ok, chain)

            def merge(t, u, turn):
                link = Chain(dve, chain, t * LINKS)
                nmax = og[:, u, :, :, HD]
                low, dn, rc = (den[:, u, n] for n in range(3))
                dve.wait_ge(og_ready[u], turn * 48 + 48 + ONE)
                link(dve.tensor_tensor(low, nmax[:, 0], nmax[:, 1], ALU.min))
                link(dve.tensor_tensor(low, low, nmax[:, 2], ALU.min))
                dve.tensor_tensor(df[:, u], low.unsqueeze(1).to_broadcast([P, GROUPS, HEADS]), nmax,
                                  ALU.subtract).then_inc(diff_ok, 1)
                dve.wait_ge(exp_ok, t + 1 + ONE)
                link(dve.tensor_tensor(df[:, u], ex[:, u], og[:, u, :, :, HD + 1], ALU.mult))
                link(dve.tensor_tensor(dn, df[:, u, 0], df[:, u, 1], ALU.add))
                link(dve.tensor_tensor(dn, dn, df[:, u, 2], ALU.add))
                link(dve.reciprocal(rc, dn))
                link(dve.tensor_tensor(ex[:, u], ex[:, u], rc.unsqueeze(1).to_broadcast([P, GROUPS, HEADS]), ALU.mult))
                dve.wait_ge(tr_ok, turn * 2 + u + ONE)
                for g in range(GROUPS):
                    w = ex[:, u, g].unsqueeze(2).to_broadcast([P, HEADS, HD])
                    if g == 0:
                        link(dve.tensor_tensor(orow[:, u], og[:, u, g, :, 0:HD], w, ALU.mult))
                    else:
                        link(dve.tensor_tensor(term[:, :, :], og[:, u, g, :, 0:HD], w, ALU.mult))
                        if g == 1:
                            link(dve.tensor_tensor(orow[:, u], orow[:, u], term[:, :, :], ALU.add))
                        else:
                            dve.tensor_tensor(orow[:, u], orow[:, u], term[:, :, :], ALU.add).then_inc(rows_ok, 1)
                assert link.n == LINKS

            def low_part(t, u):
                dve.wait_ge(oh_ok, t + 2 + ONE)
                dve.tensor_tensor(ol[:, 1 - u], tp[u][:, :, :], oh[:, 1 - u].bitcast(F32), ALU.subtract).then_inc(ol_ok, 1)

            def finish(t, u):
                dve.wait_ge(prod, t + 2 + ONE)
                row = G.h[:, bass.ds(t, 1), :].rearrange("p a d -> p (a d)")
                dve.tensor_tensor(row, py[1 - u][:, :, :].rearrange("p a n -> p (a n)"), row, ALU.add).then_inc(added, 1)

            dve.wait_ge(oh_ok, 1 + ONE)
            dve.tensor_tensor(ol[:, 0, :, 0:NSMP], H.oT[:, :, :], oh[:, 0, :, 0:NSMP].bitcast(F32), ALU.subtract).then_inc(ol_ok, 1)
            for u in range(2):
                merge(u, u, 0)
            for u in range(2):
                low_part(u, u)
            dve.wait_ge(H.h_ready, 16 + ONE)
            dve.wait_ge(prod, 1 + ONE)
            row = G.h[0:NSMP, QT, :]
            dve.tensor_tensor(row, py[0][0:NSMP].rearrange("p a n -> p (a n)"), row, ALU.add).then_inc(added, 1)
            with dve.Fori(0, QT // 2 - 1) as i:
                for u in range(2):
                    merge(i * 2 + u + 2, u, i + 1)
                    finish(i * 2 + u, u)
                    low_part(i * 2 + u + 2, u)
            for t in (QT - 2, QT - 1):
                finish(t, t % 2)

        @block.tensor
        def _(pe):
            begin(pe, prod, tr_ok)

            def transposes(t, u):
                pe.wait_ge(rows_ok, t + 1 + ONE)
                for k in range(HEADS):
                    mm = pe.transpose(tp[u][:, k, :], orow[:, u, k, :], G.ident[:, :])
                mm.then_inc(tr_ok, 1)

            def project(turn, v, n):
                pe.wait_ge(ol_ok, turn + 1 + ONE)
                for half in range(2):
                    cols = slice(half * 512, (half + 1) * 512)
                    terms = [(k, a, b) for k in range(HEADS) for a, b in ((oh, wh), (ol, wh), (oh, wl))]
                    for m, (k, a, b) in enumerate(terms):
                        mm = pe.matmul(py[v][0:n, half, :], a[:, v, k, 0:n], b[:, k, cols],
                                       start=(m == 0), stop=(m == len(terms) - 1))
                mm.then_inc(prod, 1)

            project(0, 0, NSMP)
            for u in range(2):
                transposes(u, u)
            with pe.Fori(0, QT // 2 - 1) as i:
                for u in range(2):
                    pe.wait_ge(added, i * 2 + u + ONE)
                    project(i * 2 + u + 1, 1 - u, P)
                    transposes(i * 2 + u + 2, u)
            for t in (QT - 2, QT - 1):
                pe.wait_ge(added, t + ONE)
                project(t + 1, 1 - t % 2, P)

        @block.scalar
        def _(act):
            begin(act, oh_ok, sq, exp_ok)

            def exp(t, u):
                act.wait_ge(diff_ok, t + 1 + ONE)
                act.activation(ex[:, u], df[:, u], ACT.Exp).then_inc(exp_ok, 1)

            def high_part(t, u):
                act.wait_ge(tr_ok, t + 1 + ONE)
                act.activation(oh[:, 1 - u], tp[u][:, :, :], ACT.Copy).then_inc(oh_ok, 1)

            def square(t, turn, count):
                act.wait_ge(added, turn + 1 + ONE)
                act.wait_ge(sq, count + ONE)
                act.activation(junk[:, :], G.h[:, bass.ds(t, 1), :], ACT.Square,
                               accum_out=G.ssq[:, bass.ds(t, 1)]).then_inc(sq, 1)

            act.activation(oh[:, 0, :, 0:NSMP], H.oT[:, :, :], ACT.Copy).then_inc(oh_ok, 1)
            for u in range(2):
                exp(u, u)
            high_part(0, 0)
            act.wait_ge(prod, 1 + ONE)
            high_part(1, 1)
            with act.Fori(0, QT // 2 - 1) as i:
                for u in range(2):
                    exp(i * 2 + u + 2, u)
                    act.wait_ge(prod, i * 2 + u + 2 + ONE)
                    high_part(i * 2 + u + 2, u)
                    square(i * 2 + u, i * 2 + u + 1, i * 2 + u)
            square(QT, 0, QT - 2)
            square(QT - 2, QT - 1, QT - 1)
            square(QT - 1, QT, QT)
    c.close()


def layer_attention(nc, G, A):
    H = Ctx(nc, "la_")
    H.qs = H.sb("qs", [P, HEADS, GROUPS, NSMP])
    H.ks = H.sb("ks", [P, HEADS, NSMP])
    H.oT = H.sb("oT", [P, HEADS, NSMP])
    cx = Ctx(nc, "lb_")
    xh = cx.sb("xh", [P, DK, NPAD], F32R)
    xl = cx.sb("xl", [P, DK, NPAD], F32R)
    wr = cx.sb("wr", [P, 3, DK, P])
    w_first = G.sem("hd_w_ready0")
    stage_norm(nc, G, "n1", xh, xl, A["s_h"], early=(wr[:, 0], A["w_heads"][0, 0], w_first))
    stage_heads(nc, G, A, xh, xl, H, wr, w_first)
    cx.close()
    H.wo = G.h[:, 0:HEADS, :]
    H.wh = H.sb("wh", [P, HEADS, D], F32R)
    H.wl = H.sb("wl", [P, HEADS, D], F32R)
    H.og = H.sb("og", [P, 2, GROUPS, HEADS, HD + 2])
    H.h_ready = G.sem("h_ready")
    H.og_ready = [G.sem(f"og_ready{u}") for u in range(2)]
    stage_sample(nc, G, A, H)
    stage_merge(nc, G, A, H)
    H.close()
def build(nc, A):
    G = Ctx(nc)
    sems = []

    def new_sem(name):
        sems.append(nc.alloc_semaphore(name))
        return sems[-1]

    def clear_sems():
        nc.clear_and_free_semaphores(sems)
        nc.all_engine_barrier()
        sems.clear()

    G.sem = new_sem
    G.h = G.sb("h", [P, TILES, D])
    G.ssq = G.sb("ssq", [P, TILES])
    G.ident = G.sb("ident", [P, P])
    G.gcol = G.sb("gcol", [P, N_GAINS, DK])
    layer_conv(nc, G, A)
    layer_moe(nc, G, A, 0)
    clear_sems()
    layer_attention(nc, G, A)
    layer_moe(nc, G, A, 1)
    clear_sems()
    G.close()


def layer_conv(nc, G, A):
    c = Ctx(nc, "lc_")
    zT = c.sb("zT", [P, DK, NPAD])
    cx = Ctx(nc, "lx_")
    W = cx
    W.wh = cx.sb("wh", [P, 2, DK, 3, P], F32R)
    W.wl = cx.sb("wl", [P, 2, DK, 3, P], F32R)
    W.first = zT[:, DK - 3:, :].rearrange("p k n -> p (k n)")[:, 0:DK * 3 * P].rearrange("p (k c n) -> p k c n", k=DK, c=3)
    stage_load(nc, G, A, W)
    xh = cx.sb("xh", [P, DK, NPAD], F32R)
    xl = cx.sb("xl", [P, DK, NPAD], F32R)
    w_out = Ctx(nc)
    w_out.raw = G.h[:, 0:DK, :]
    w_out.dram = A["conv_w_out"].rearrange("a (k p) n -> p (a k) n", p=P)
    w_out.early = 2 * DK * 3 * P // D
    w_out.ready = G.sem("w_out_ready")
    stage_norm(nc, G, "n0", xh, xl, W=W)
    stage_conv(nc, G, A, xh, xl, W, zT, w_out)
    cx.close()
    stage_project(nc, G, A, "po", zT, w_out)
    c.close()


IOTA_COLS = P + 2 * TILES + EG
N_GAINS = 3
GAIN_MIX0, GAIN_MIX1, GAIN_KV = range(N_GAINS)


def _col(a, np):
    b = a.reshape(a.shape[:-1] + (DK, P))
    return np.ascontiguousarray(np.moveaxis(b, -1, 0))


def _constants(np):
    f = np.float32
    half = HD // 2
    inv = np.power(f(10000.0), -np.arange(half, dtype=f) / f(half)).astype(f)
    pos = np.concatenate([np.arange(SEQ), PAST + np.tile(np.arange(DEC_S), DEC_B)]).astype(f)
    ang = (inv[:, None] * pos[None, :]).astype(f)
    q, k = np.arange(P)[:, None], np.arange(2 * P)[None, :]
    rel = q + P - k
    band = np.where((rel >= 0) & (rel <= WINDOW_KEYS), 0.0, NEG)
    n = np.arange(P)
    back = n[:, None] - n[None, :]
    pair = np.where((back >= 0) & (back % 2 == 0), 0.0, NEG)
    qn = np.arange(P) % DEC_S
    j = np.concatenate([np.arange(PAST), np.tile(PAST + np.arange(DEC_S), P // (HEADS * DEC_S))])
    row_seq, key_seq = np.arange(P) // (HEADS * DEC_S), (np.arange(len(j)) - PAST) // DEC_S
    own = (key_seq[None, :] < 0) | (key_seq[None, :] == row_seq[:, None])
    smp = []
    for dil in (1, 4, 16):
        dist = PAST + qn[:, None] - j[None, :]
        smp.append(np.where((dist >= 0) & (dist % dil == 0) & (dist // dil <= WINDOW_KEYS) & own, 0.0, NEG))
    tok = np.arange(TILES)[None, :] * P + np.arange(P)[:, None]
    return {
        "c_ident": np.eye(P, dtype=f),
        "c_upper": (np.arange(P)[:, None] < np.arange(P)[None, :]).astype(f),
        "c_iota": np.concatenate([np.tile(np.arange(P), (P, 1)), tok, np.tile(np.arange(EG, 0, -1), (P, 1)),
                                  np.tile(np.arange(TILES) * P, (P, 1))], axis=1).astype(f),
        "c_cos": np.concatenate([np.cos(ang)] * 2).astype(f),
        "c_sin": np.concatenate([np.sin(ang), -np.sin(ang)]).astype(f),
        "c_band": band.astype(f),
        "c_pair": pair.astype(f),
        "c_smp": np.stack(smp, axis=1).astype(f),
    }


_OUTS = {
    "o_y": (NTOK, D), "o_kT": (HEADS, HD, NTOK), "o_v": (NTOK, HEADS, HD), "o_conv": (P, DK, (CONV - 1) * (1 + DEC_B)),
}
_PLAIN = ["x_prompt", "x_sample", "conv_w_out", "attn_w_o", "expert_w1", "expert_w3", "expert_w2", "cache_k", "cache_v",
          "norm_final", "norm_ffn", "router_group_b", "router_expert_b"]


def kernel(**inputs):
    import numpy as _np
    import concourse.bacc as _bacc
    from concourse import mybir as _mybir
    from concourse.bass_utils import run_bass_kernel_spmd as _run

    x = {k: _np.asarray(v) for k, v in inputs.items()}
    arrays = {k: _np.ascontiguousarray(x[k]) for k in _PLAIN}
    arrays.update(_constants(_np))
    gains = _np.stack([x["norm_mix"][0], x["norm_mix"][1], x["norm_kv"]])
    arrays["gains_col"] = _col(gains, _np)
    arrays["conv_kernel_col"] = _np.ascontiguousarray(_col(x["conv_kernel"][0], _np).transpose(0, 2, 1))
    arrays["state_col"] = _np.ascontiguousarray(_col(x["state_conv"][0], _np).transpose(0, 3, 1, 2))
    w = x["conv_w_in"][0].reshape(DK, P, 3, DK, P)
    arrays["conv_w_in_t"] = _np.ascontiguousarray(w.transpose(3, 1, 0, 2, 4))
    kv = x["attn_w_kv"].reshape(DK, P, 2, HEADS, HD)
    q = x["attn_w_q"][0].reshape(DK, P, GROUPS, HEADS, HD)
    arrays["w_heads"] = _np.ascontiguousarray(_np.concatenate([kv[:, :, :1], q, kv[:, :, 1:]], axis=2).transpose(3, 2, 1, 0, 4))
    wr = _np.concatenate([x["router_group_w"], x["router_expert_w"]], axis=2).reshape(2, DK, P, ROUTE)
    arrays["router_w"] = _np.ascontiguousarray(wr.transpose(2, 0, 1, 3))

    nc = _bacc.Bacc("TRN2", target_bir_lowering=False, num_devices=1)
    A = {}
    for name, a in arrays.items():
        A[name] = nc.dram_tensor("in_" + name, a.shape, _mybir.dt.from_np(a.dtype), kind="ExternalInput").ap()
    for name, shape in _OUTS.items():
        A[name] = nc.dram_tensor("out_" + name, shape, _mybir.dt.float32, kind="ExternalOutput").ap()
    A["s_rows"] = nc.dram_tensor("s_rows", (NPAD, D), _mybir.dt.float32).ap()
    A["s_h"] = nc.dram_tensor("s_h", (NPAD, D), _mybir.dt.float32).ap()
    A["s_ys"] = nc.dram_tensor("s_ys", (MBLK * P, D), _mybir.dt.float32).ap()
    A["s_og"] = nc.dram_tensor("s_og", (GROUPS, SEQ, HEADS, HD + 2), _mybir.dt.float32).ap()
    build(nc, A)
    r = _run(nc, [{"in_" + k: v for k, v in arrays.items()}], core_ids=[0]).results[0]
    y, kT, v, cv = (r["out_" + n] for n in ("o_y", "o_kT", "o_v", "o_conv"))
    k = kT.transpose(2, 0, 1)
    cv = _np.ascontiguousarray(cv.transpose(2, 1, 0)).reshape(1, 1 + DEC_B, CONV - 1, D)
    return (
        y[:SEQ].reshape(1, SEQ, D), y[SEQ:].reshape(DEC_B, DEC_S, D),
        _np.ascontiguousarray(k[:SEQ]).reshape(1, SEQ, HEADS, HD), v[:SEQ].reshape(1, SEQ, HEADS, HD),
        cv[:, :1], _np.ascontiguousarray(k[SEQ:]).reshape(DEC_B, DEC_S, HEADS, HD),
        v[SEQ:].reshape(DEC_B, DEC_S, HEADS, HD), cv[:, 1:],
    )
```
